# Optimizing a Trainium2 kernel written in Bass

```python
import jax, jax.numpy as jnp
from jax import lax
import numpy as np

D_MODEL = 2048
BATCH = 1
SEQ = 1024
DEPTH = 1
DEC_BATCH = 8
DEC_SEQ = 16
PAST_LEN = 1024

CHUNK = 64
WINDOW = 128
WIN_CHUNKS = WINDOW // CHUNK
ATT_WIDTH = D_MODEL // 2
GLA_WIDTH = D_MODEL - ATT_WIDTH
HEAD_DIM = 64
N_HEADS = ATT_WIDTH // HEAD_DIM
N_KV = 4
GQA_REP = N_HEADS // N_KV
N_GLA = 4
GLA_DV = GLA_WIDTH // N_GLA
GLA_DK = GLA_DV // 2
GLA_KW = N_GLA * GLA_DK
GATE_RANK = 16
GATE_TAU = 16.0
EPS = 1e-6
ATT_SCALE = HEAD_DIM ** -0.5
ATT_CACHE = min(WINDOW, PAST_LEN)
IN_SIZES = (ATT_WIDTH, N_KV * HEAD_DIM, N_KV * HEAD_DIM, ATT_WIDTH,
            GLA_KW, GLA_KW, GLA_WIDTH, GLA_WIDTH, GATE_RANK)
IN_TOTAL = sum(IN_SIZES)
SPLITS = tuple(int(s) for s in np.cumsum(IN_SIZES)[:-1])

kernel_name = "hymba_swa_sink_gla_streaming_step"

def rmsnorm(x, g):
    xf = x.astype(jnp.float32)
    y = xf * lax.rsqrt(jnp.mean(xf * xf, axis=-1, keepdims=True) + EPS)
    return (y * g.astype(jnp.float32)).astype(x.dtype)

def sink_softmax(s, sink):
    m = jnp.maximum(jnp.max(s, axis=-1, keepdims=True), sink)
    e = jnp.exp(s - m)
    return e / (jnp.sum(e, axis=-1, keepdims=True) + jnp.exp(sink - m))

def branch_inputs(x, norm_g, w_in, w_gate_up, b_gate, q_norm_g, k_norm_g):
    B, T, _ = x.shape
    xn = rmsnorm(x, norm_g)
    h = xn @ w_in
    qa, ka, va, ga, qg, kg, vg, gg, lr = jnp.split(h, SPLITS, axis=-1)
    qa = rmsnorm(qa.reshape(B, T, N_HEADS, HEAD_DIM), q_norm_g)
    ka = rmsnorm(ka.reshape(B, T, N_KV, HEAD_DIM), k_norm_g)
    va = va.reshape(B, T, N_KV, HEAD_DIM)
    qg = qg.reshape(B, T, N_GLA, GLA_DK) * (GLA_DK ** -0.5)
    kg = kg.reshape(B, T, N_GLA, GLA_DK)
    vg = vg.reshape(B, T, N_GLA, GLA_DV)
    log_a = jax.nn.log_sigmoid((lr @ w_gate_up + b_gate).astype(jnp.float32)) / GATE_TAU
    log_a = log_a.reshape(B, T, N_GLA, GLA_DK)
    return qa, ka, va, ga, qg, kg, vg, gg, log_a

def swa_prompt(q, k, v, sinks):
    B, S = q.shape[:2]
    n = S // CHUNK
    L = (WIN_CHUNKS + 1) * CHUNK
    qb = q.reshape(B, n, CHUNK, N_KV, GQA_REP, HEAD_DIM).astype(jnp.float32)
    pad = ((0, 0), (WINDOW, 0), (0, 0), (0, 0))
    kp = jnp.pad(k, pad).reshape(B, n + WIN_CHUNKS, CHUNK, N_KV, HEAD_DIM)
    vp = jnp.pad(v, pad).reshape(B, n + WIN_CHUNKS, CHUNK, N_KV, HEAD_DIM)
    kband = jnp.concatenate([kp[:, i:i + n] for i in range(WIN_CHUNKS + 1)], axis=2)
    vband = jnp.concatenate([vp[:, i:i + n] for i in range(WIN_CHUNKS + 1)], axis=2)
    key_pos = jnp.arange(n)[:, None] * CHUNK - WINDOW + jnp.arange(L)[None, :]
    valid = key_pos >= 0
    s = jnp.einsum('bnqgrd,bnkgd->bngrqk', qb, kband.astype(jnp.float32)) * ATT_SCALE
    s = jnp.where(valid[None, :, None, None, None, :], s, -jnp.inf)
    sink = sinks.astype(jnp.float32).reshape(N_KV, GQA_REP)[None, None, :, :, None, None]
    p = sink_softmax(s, sink)
    o = jnp.einsum('bngrqk,bnkgd->bnqgrd', p.astype(v.dtype), vband)
    return o.reshape(B, S, ATT_WIDTH)

def swa_sample(q, k_new, v_new, cache_k, cache_v, sinks):
    B, T = q.shape[:2]
    keys = jnp.concatenate([cache_k.astype(k_new.dtype), k_new], axis=1)
    vals = jnp.concatenate([cache_v.astype(v_new.dtype), v_new], axis=1)
    qg = q.reshape(B, T, N_KV, GQA_REP, HEAD_DIM).astype(jnp.float32)
    s = jnp.einsum('btgrd,bsgd->bgrts', qg, keys.astype(jnp.float32)) * ATT_SCALE
    sink = sinks.astype(jnp.float32).reshape(N_KV, GQA_REP)[None, :, :, None, None]
    p = sink_softmax(s, sink)
    o = jnp.einsum('bgrts,bsgd->btgrd', p.astype(vals.dtype), vals).reshape(B, T, ATT_WIDTH)
    return o, keys[:, -ATT_CACHE:], vals[:, -ATT_CACHE:]

def gla_scan(q, k, v, log_a, s0):
    B, T, H, _ = q.shape
    blk = min(CHUNK, T)
    n = T // blk

    def blocks(a):
        return jnp.moveaxis(a.astype(jnp.float32).reshape(B, n, blk, H, a.shape[-1]), 1, 0)

    causal = jnp.tril(jnp.ones((blk, blk), dtype=bool))

    def step(S, inp):
        qc, kc, vc, ac = inp
        bcum = jnp.cumsum(ac, axis=1)
        diff = bcum[:, :, None] - bcum[:, None, :]
        decay = jnp.exp(jnp.where(causal[None, :, :, None, None], diff, -jnp.inf))
        att = jnp.einsum('bijhd,bjhd->bhij', qc[:, :, None] * decay, kc)
        o = (jnp.einsum('bhij,bjhe->bihe', att, vc)
             + jnp.einsum('bihd,bhde->bihe', qc * jnp.exp(bcum), S))
        blast = bcum[:, -1]
        S = (jnp.exp(blast)[..., None] * S
             + jnp.einsum('bjhd,bjhe->bhde', kc * jnp.exp(blast[:, None] - bcum), vc))
        return S, o

    S, o = lax.scan(step, s0.astype(jnp.float32), (blocks(q), blocks(k), blocks(v), blocks(log_a)))
    o = jnp.moveaxis(o, 0, 1).reshape(B, T, H, v.shape[-1])
    return o, S

def merge(x, o_attn, ga, o_gla, gg, gla_norm_g, w_out):
    B, T, _ = x.shape
    o_gla = rmsnorm(o_gla.astype(x.dtype), gla_norm_g).reshape(B, T, GLA_WIDTH)
    mix = jnp.concatenate([o_attn * jax.nn.silu(ga), o_gla * jax.nn.silu(gg)], axis=-1)
    return x + mix @ w_out

def setup_inputs(seed: int = 0) -> dict:
    key = jax.random.key(seed)
    ks = jax.random.split(key, 16)
    f32 = jnp.float32
    nrm = jax.random.normal
    return {
        "x_prompt": nrm(ks[0], (BATCH, SEQ, D_MODEL), f32),
        "x_sample": nrm(ks[1], (DEC_BATCH, DEC_SEQ, D_MODEL), f32),
        "cache_k": nrm(ks[2], (DEPTH, DEC_BATCH, ATT_CACHE, N_KV, HEAD_DIM), f32),
        "cache_v": nrm(ks[3], (DEPTH, DEC_BATCH, ATT_CACHE, N_KV, HEAD_DIM), f32),
        "state_gla": nrm(ks[4], (DEPTH, DEC_BATCH, N_GLA, GLA_DK, GLA_DV), f32) * 0.5,
        "norm_g": 1.0 + 0.02 * nrm(ks[5], (DEPTH, D_MODEL), f32),
        "w_in": nrm(ks[6], (DEPTH, D_MODEL, IN_TOTAL), f32) * D_MODEL ** -0.5,
        "w_gate_up": nrm(ks[7], (DEPTH, GATE_RANK, GLA_KW), f32) * GATE_RANK ** -0.5,
        "b_gate": 0.1 * nrm(ks[8], (DEPTH, GLA_KW), f32),
        "q_norm_g": 1.0 + 0.02 * nrm(ks[9], (DEPTH, HEAD_DIM), f32),
        "k_norm_g": 1.0 + 0.02 * nrm(ks[10], (DEPTH, HEAD_DIM), f32),
        "sinks": 0.5 * nrm(ks[11], (DEPTH, N_HEADS), f32),
        "gla_norm_g": 1.0 + 0.02 * nrm(ks[12], (DEPTH, GLA_DV), f32),
        "w_out": nrm(ks[13], (DEPTH, ATT_WIDTH + GLA_WIDTH, D_MODEL), f32) * (ATT_WIDTH + GLA_WIDTH) ** -0.5,
    }

def reference(x_prompt, x_sample, cache_k, cache_v, state_gla, norm_g, w_in, w_gate_up, b_gate,
              q_norm_g, k_norm_g, sinks, gla_norm_g, w_out):
    h_p, h_s = x_prompt, x_sample
    pk, pv, ps, sk, sv, ss = [], [], [], [], [], []
    for l in range(DEPTH):
        qa, ka, va, ga, qg, kg, vg, gg, la = branch_inputs(
            h_p, norm_g[l], w_in[l], w_gate_up[l], b_gate[l], q_norm_g[l], k_norm_g[l])
        oa = swa_prompt(qa, ka, va, sinks[l])
        s0 = jnp.zeros((h_p.shape[0], N_GLA, GLA_DK, GLA_DV), jnp.float32)
        og, sg = gla_scan(qg, kg, vg, la, s0)
        h_p = merge(h_p, oa, ga, og, gg, gla_norm_g[l], w_out[l])
        pk.append(ka[:, -ATT_CACHE:])
        pv.append(va[:, -ATT_CACHE:])
        ps.append(sg.astype(state_gla.dtype))
        qa, ka, va, ga, qg, kg, vg, gg, la = branch_inputs(
            h_s, norm_g[l], w_in[l], w_gate_up[l], b_gate[l], q_norm_g[l], k_norm_g[l])
        oa, nk, nv = swa_sample(qa, ka, va, cache_k[l], cache_v[l], sinks[l])
        og, sg = gla_scan(qg, kg, vg, la, state_gla[l])
        h_s = merge(h_s, oa, ga, og, gg, gla_norm_g[l], w_out[l])
        sk.append(nk)
        sv.append(nv)
        ss.append(sg.astype(state_gla.dtype))
    return (h_p, h_s, jnp.stack(pk), jnp.stack(pv), jnp.stack(ps), jnp.stack(sk), jnp.stack(sv), jnp.stack(ss))


_drawn_inputs = setup_inputs


def setup_inputs(seed=0):
    import zlib

    import numpy as np

    out = dict(_drawn_inputs(seed))
    spreads = {}
    factors = {'q_norm_g': 64.0, 'sinks': 64.0, 'gla_norm_g': 23.926}
    for name, (base, spread) in spreads.items():
        noise = np.random.default_rng([zlib.crc32(name.encode()), seed]).standard_normal(out[name].shape)
        drawn = base * np.exp(spread * noise) if base else spread * noise
        out[name] = __import__('jax').numpy.asarray(drawn.astype(out[name].dtype))
    for name, factor in factors.items():
        out[name] = (out[name] * factor).astype(out[name].dtype)
    return out
```

```python
from contextlib import ExitStack

import concourse.bass as bass
from concourse import mybir

P = 128
D_MODEL = 2048
SEQ = 1024
DEC_BATCH = 8
DEC_SEQ = 16
CACHE = 128
HEAD_DIM = 64
N_HEADS = 16
N_KV = 4
GQA = N_HEADS // N_KV
N_GLA = 4
DK = 128
DV = 256
RANK = 16
TAU = 16.0
EPS = 1e-6
CHUNK = 64

TOK = SEQ + DEC_BATCH * DEC_SEQ
NT = TOK // P
NTP = SEQ // P
KT = D_MODEL // P
TN = 384
NG = TOK // TN
PAD = P

Q0, K0, V0, GA0, GQ0, GK0, GV0, GG0, LR0 = 0, 1024, 1280, 1536, 2560, 3072, 3584, 4608, 5632
IN_TOTAL = LR0 + RANK

N_QK = (V0 - Q0) // P
N_PLAIN = (GA0 - Q0 + GG0 - GQ0) // P
N_ITEMS = (IN_TOTAL - RANK) // P
J_GLA = 1 + N_PLAIN + NTP
WCH = 256
NCH = D_MODEL // WCH
LEVELS = (64, 32, 16, 8, 4, 2, 1)
DEC_LEVELS = (8, 4, 2, 1)

F32 = mybir.dt.float32
F32R = mybir.dt.float32r
U8 = mybir.dt.uint8
ALU = mybir.AluOpType
ACT = mybir.ActivationFunctionType
AX = mybir.AxisListType
ds = bass.ds


C_IDENT, C_PAIR, C_SEQ, C_MASK0 = 0, P, 2 * P, 2 * P + DEC_BATCH
C_MASK = C_MASK0 + 2 * P
C_ALL = C_MASK + 2 * P
M_DIAG = len(LEVELS) * 256
M_SCAN = M_DIAG + 4 * P
M_SCAN_DEC = M_SCAN + 4 * P
M_ALL = M_SCAN_DEC + 4 * P
MASKED = -1.0e30


def project_in(nc, sem, dram):
    (x_p, x_s, cache_k, cache_v, state, norm_g, w_in, w_up, b_gate, qg, kg, sinks, gla_g, consts, tables,
     win_kp, win_vp, gla_p, win_ks, win_vs, gla_s, h_t, o_t) = dram
    with ExitStack() as ctx:
        def sb(name, shape, dt=F32):
            return ctx.enter_context(nc.sbuf_tensor(name, shape, dt))

        x_hi = sb("x_hi", [P, KT, TOK], F32R)
        x_lo = sb("x_lo", [P, KT, TOK], F32R)
        raw = sb("raw", [P, D_MODEL])
        w_hi = sb("w_hi", [P, KT, P], F32R)
        w_lo = sb("w_lo", [P, KT, P], F32R)
        xn = sb("xn", [P, D_MODEL])
        work = sb("work", [P, 9216])
        consts_sb = sb("consts_sb", [P, C_MASK0])
        tables_sb = sb("tables_sb", [P, M_ALL], U8)
        w_up_sb = sb("w_up_sb", [RANK + 1, N_GLA * DK])
        lr = sb("lr", [RANK + 1, P])
        sink_row = sb("sink_row", [P, N_HEADS])
        sink_dec = sb("sink_dec", [P, 2])
        gq_col = sb("gq_col", [P, 2])
        gn_col = sb("gn_col", [P, 2])
        small = sb("small", [P, 96])
        mhalf = sb("mhalf", [P, 4])
        ident = consts_sb[:, C_IDENT:C_IDENT + P]
        ones_pair = consts_sb[:, C_PAIR:C_PAIR + P]
        seq_col = consts_sb[:, C_SEQ:C_SEQ + DEC_BATCH]
        x_buf = [work[:, 0:D_MODEL], raw[:, :]]
        g_row = work[:, D_MODEL:2 * D_MODEL]
        ss, var, rstd = small[:, 0:2], small[:, 2:3], small[:, 3:4]
        stage = [xn[:, TN * n:TN * n + TN] for n in range(3)]
        tmp_a = xn[:, 3 * TN:4 * TN]
        tmp_b = xn[:, 4 * TN:5 * TN]

        banks = [ctx.enter_context(nc.psum_tensor(f"p1_{i}", [P, 512], F32)) for i in range(8)]
        acc = banks[0:3]
        xt_bank = banks[3:7]
        ss_bank = banks[7]
        ub = banks[3:8]

        s_const = sem("s_const")
        s_x = [sem(f"s_x{i}") for i in range(2)]
        s_w = [sem(f"s_w{i}") for i in range(4)]
        s_ss = sem("s_ss")
        s_var = sem("s_var")
        s_rstd = sem("s_rstd")
        s_xn = sem("s_xn")
        s_xt = sem("s_xt")
        s_xhi = sem("s_xhi")
        s_xlo = sem("s_xlo")
        s_mh = sem("s_mh")
        s_whi = sem("s_whi")
        s_wready = sem("s_wready")
        s_wfree = sem("s_wfree")
        s_acc = sem("s_acc")
        s_staged = sem("s_staged")
        s_store = [sem(f"s_store{i}") for i in range(3)]
        s_sq = sem("s_sq")
        s_ssq = sem("s_ssq")
        s_v = sem("s_v")
        s_sd = sem("s_sd")
        s_nchain = sem("s_nchain")
        s_sig = sem("s_sig")
        s_schain = sem("s_schain")
        s_zero = sem("s_zero")
        s_zst = sem("s_zst")
        s_tab = sem("s_tab")
        s_win = sem("s_win")
        s_tload = sem("s_tload")
        s_tables = sem("s_tables")
        sa_dv = sem("sa_dv")
        sa_e = sem("sa_e")
        sa_k = sem("sa_k")
        sa_mask = sem("sa_mask")
        sa_max = sem("sa_max")
        sa_mk = sem("sa_mk")
        sa_neg = sem("sa_neg")
        sa_o = sem("sa_o")
        sa_out = sem("sa_out")
        sa_p = sem("sa_p")
        sa_pt = sem("sa_pt")
        sa_q = sem("sa_q")
        sa_s = sem("sa_s")
        sa_st = sem("sa_st")
        sa_t = sem("sa_t")
        sa_v = sem("sa_v")
        sa_vtok = sem("sa_vtok")
        sa_vtr = sem("sa_vtr")
        sb_av = sem("sb_av")
        sb_ck = [sem(f"sb_ck{i}") for i in range(2)]
        sb_cv = [sem(f"sb_cv{i}") for i in range(2)]
        sb_dv = sem("sb_dv")
        sb_e = sem("sb_e")
        sb_in = sem("sb_in")
        sb_ks = sem("sb_ks")
        sb_kt = sem("sb_kt")
        sb_neg = sem("sb_neg")
        sb_new = sem("sb_new")
        sb_oc = sem("sb_oc")
        sb_pc = sem("sb_pc")
        sb_pr = sem("sb_pr")
        sb_pt = sem("sb_pt")
        sb_s = sem("sb_s")
        sb_w = sem("sb_w")
        sb_xc = sem("sb_xc")
        sb_xt = sem("sb_xt")
        sd_ds = sem("sd_ds")
        sd_gp = sem("sd_gp")
        sd_in = [sem(f"sd_in{i}") for i in range(2)]
        sd_k = sem("sd_k")
        sd_o = sem("sd_o")
        sd_out = [sem(f"sd_out{i}") for i in range(2)]
        sd_q = sem("sd_q")
        sd_up = sem("sd_up")
        sl_a = sem("sl_a")
        sl_b = sem("sl_b")
        sl_cp = sem("sl_cp")
        sl_d = sem("sl_d")
        sl_dcp = sem("sl_dcp")
        sl_dg = sem("sl_dg")
        sl_ds = sem("sl_ds")
        sl_eb = sem("sl_eb")
        sl_ex = sem("sl_ex")
        sl_gt = sem("sl_gt")
        sl_ini = sem("sl_ini")
        sl_k = sem("sl_k")
        sl_kt = sem("sl_kt")
        sl_ktok = sem("sl_ktok")
        sl_la = sem("sl_la")
        sl_log = sem("sl_log")
        sl_lr = sem("sl_lr")
        sl_o = sem("sl_o")
        sl_og = sem("sl_og")
        sl_on = sem("sl_on")
        sl_p = sem("sl_p")
        sl_q = sem("sl_q")
        sl_qs = sem("sl_qs")
        sl_rs = sem("sl_rs")
        sl_sq = sem("sl_sq")
        sl_st = sem("sl_st")
        sl_up = sem("sl_up")
        sl_v = sem("sl_v")
        sl_var = sem("sl_var")
        sl_vtok = sem("sl_vtok")
        sl_vtr = sem("sl_vtr")
        sl_zz = sem("sl_zz")
        block = ctx.enter_context(nc.Block())
        w_v = w_in.rearrange("(k p) n -> p k n", p=P)

        def w_raw(k, n):
            return raw[:, k * P:k * P + 4 * P].rearrange("p (k n) -> p k n", k=4)[:, :, 0:n]

        RUNS = [(1, 13, Q0), (13, 1 + N_PLAIN, GQ0), (1 + N_PLAIN, J_GLA, GA0), (J_GLA, 1 + N_ITEMS, GG0)]

        @block.sync
        def _(sp):
            sp.dma_start(work[:, 2 * D_MODEL:2 * D_MODEL + M_ALL], tables).then_inc(s_tload, 16)
            sp.dma_start(consts_sb[:, :], consts[:, 0:C_MASK0]).then_inc(s_const, 16)
            sp.dma_start(g_row, norm_g[0:1, :].to_broadcast([P, D_MODEL])).then_inc(s_const, 16)
            for half in range(2):
                rows = slice(half * HEAD_DIM, half * HEAD_DIM + HEAD_DIM)
                sp.dma_start(gq_col[rows, 0:1], qg.rearrange("a d -> d a")).then_inc(s_const, 16)
                sp.dma_start(gq_col[rows, 1:2], kg.rearrange("a d -> d a")).then_inc(s_const, 16)

            def load_x(t, slot, src):
                sp.wait_ge(s_xn, t + 1)
                sp.dma_start(x_buf[slot], src).then_inc(s_x[slot], 16)

            with sp.Fori(0, NTP // 2) as i:
                for slot in range(2):
                    load_x(2 * i + slot, slot, x_p[ds((2 * i + slot) * P, P), :])
            load_x(NTP, 0, x_s)
            sp.dma_start(w_up_sb[0:RANK, :], w_up[0]).then_inc(s_tab, 16)
            sp.dma_start(w_up_sb[RANK:RANK + 1, :], b_gate).then_inc(s_tab, 16)
            for e in range(2):
                sp.dma_start(gn_col[:, e:e + 1], gla_g[:, e * P:e * P + P].rearrange("a p -> p a")).then_inc(s_tab, 16)
            sp.dma_start(sink_row[:, :], sinks.to_broadcast([P, N_HEADS])).then_inc(s_tab, 16)
            for half in range(2):
                for gp in range(2):
                    for r in range(GQA):
                        rows = slice(half * HEAD_DIM + r * DEC_SEQ, half * HEAD_DIM + r * DEC_SEQ + DEC_SEQ)
                        h = (2 * gp + half) * GQA + r
                        sp.dma_start(sink_dec[rows, gp:gp + 1],
                                     sinks[0:1, h:h + 1].to_broadcast([DEC_SEQ, 1])).then_inc(s_tab, 16)

            def load_w(j, col, n):
                for q in range(4):
                    if type(j) is int and j == 0:
                        sp.wait_ge(s_xn, NTP + 2)
                    else:
                        sp.wait_ge(s_wready, 4 * j + (q - 3))
                    sp.dma_start(w_raw(4 * q, n), w_v[:, 4 * q:4 * q + 4, ds(col, n)]).then_inc(s_w[q], 16)

            def store_item(j, row, n_rows):
                for n in range(NG):
                    sp.wait_ge(s_staged, j * NG + (n + 4))
                    sp.dma_start(h_t[ds(row, n_rows), PAD + n * TN:PAD + n * TN + TN],
                                 stage[n][0:n_rows, :]).then_inc(s_store[n], 16)

            load_w(0, LR0, RANK)
            sp.wait_ge(s_zero, 1)
            for r in range(K0 // P, GA0 // P):
                sp.dma_start(h_t[r * P:r * P + P, 0:PAD], xn[:, 5 * TN:5 * TN + PAD]).then_inc(s_zst, 16)
            load_w(1, Q0, P)
            store_item(0, LR0, RANK)
            for i, (j0, j1, col) in enumerate(RUNS):
                with sp.Fori(j0, j1 - 1) as j:
                    load_w(j + 1, (j - j0) * P + (col + P), P)
                    store_item(j, (j - j0) * P + col, P)
                if i + 1 < len(RUNS):
                    load_w(j1, RUNS[i + 1][2], P)
                store_item(j1 - 1, (j1 - 1 - j0) * P + col, P)
            sp.wait_ge(s_zst, 16 * (GA0 - K0) // P)
            old = CACHE - DEC_SEQ
            sp.dma_start(win_ks[:, 0:old, :], cache_k[:, DEC_SEQ:CACHE, :]).then_inc(s_win, 16)
            sp.dma_start(win_vs[:, 0:old, :], cache_v[:, DEC_SEQ:CACHE, :]).then_inc(s_win, 16)
            sp.wait_ge(s_win, 32)
            for n in range(NG):
                sp.wait_ge(s_store[n], 16 * (N_ITEMS + 1))

        def wait_acc(eng, j, n):
            if n == NG - 1:
                eng.wait_ge(s_wfree, 4 * j + 8)
            else:
                eng.wait_ge(s_acc, 2 * j + (n + 1))

        def split_hi(act, j, n=P):
            for k in range(0, KT, 4):
                act.wait_ge(s_w[k // 4], 16 * j + 16)
                act.wait_ge(s_wfree, 4 * j + (k // 4 + 1))
                act.activation(w_hi[:, k:k + 4, 0:n], w_raw(k, n), ACT.Copy).then_inc(s_whi, 1)

        def split_lo(dve, j, n=P):
            for k in range(0, KT, 4):
                dve.wait_ge(s_whi, 4 * j + (k // 4 + 1))
                dve.tensor_tensor(w_lo[:, k:k + 4, 0:n], w_raw(k, n), w_hi[:, k:k + 4, 0:n].bitcast(F32),
                                  ALU.subtract).then_inc(s_wready, 1)

        a_q = work[:, 0:1024].rearrange("p (c n) -> p c n", c=8)
        a_k = work[:, 1024:2048].rearrange("p (g n) -> p g n", g=N_KV)
        a_v = work[:, 2048:2560].rearrange("p (c n) -> p c n", c=2)
        a_vtok = work[:, 2560:3072].rearrange("p (k n) -> p k n", k=2)
        a_p = work[:, 3072:4096].rearrange("p (r n) -> p r n", r=GQA)
        a_pt = work[:, 4096:5120].rearrange("p (k n) -> p k n", k=2)
        a_o = work[0:HEAD_DIM, 5120:5632]
        a_mask = work[:, 5632:6144].rearrange("p (m n) -> p m n", m=2)
        a_mx, a_neg, a_sk, a_es, a_sum, a_den = (small[:, 8 + 4 * i:12 + 4 * i] for i in range(6))
        bank_s, bank_t, bank_o = ub[0:2], ub[2:4], ub[4]

        def attend_pe(pe, t):
            def values():
                pe.wait_ge(sa_v, 16 * t + 16)
                for kt in range(2):
                    for c in range(2):
                        mm = pe.transpose(bank_t[0][:, kt * 256 + c * P:kt * 256 + c * P + P],
                                          a_v[:, c, kt * P:kt * P + P], ident)
                mm.then_inc(sa_vtr, 1)

            def scores(g):
                pe.wait_ge(sa_q, 16 * t + 16)
                pe.wait_ge(sa_k, 32 * t + 32)
                pe.wait_ge(sa_max, 16 * t + (4 * g + 1))
                for half in range(2):
                    rows = slice(half * HEAD_DIM, half * HEAD_DIM + HEAD_DIM)
                    for i in range(2):
                        mm = pe.matmul(bank_s[half][:, i * 256:i * 256 + 256],
                                       a_q[rows, 2 * g + i, :], a_k[rows, g, :], start=True, stop=True)
                    mm.then_inc(sa_s, 1)

            def turn(g):
                pe.wait_ge(sa_p, 16 * t + (4 * g + 4))
                pe.wait_ge(sa_pt, 8 * t + (2 * g + 1))
                pe.wait_ge(sa_vtok, t + 1)
                for kt in range(2):
                    for r in range(GQA):
                        mm = pe.transpose(bank_t[kt][:, r * P:r * P + P], a_p[:, r, kt * P:kt * P + P], ident)
                    mm.then_inc(sa_t, 1)

            def outputs(g):
                pe.wait_ge(sa_pt, 8 * t + (2 * g + 3))
                pe.wait_ge(sa_out, 4 * t + (g + 1))
                for kt in range(2):
                    mm = pe.matmul(bank_o[0:HEAD_DIM, :], a_vtok[:, kt, g * HEAD_DIM:g * HEAD_DIM + HEAD_DIM],
                                   a_pt[:, kt, :], start=(kt == 0), stop=(kt == 1))
                mm.then_inc(sa_o, 1)

            def at(*stages):
                return lambda: [f(*a) for f, *a in stages]

            return {4: at((values,), (scores, 0)), 12: at((turn, 0), (scores, 1)), 14: at((outputs, 0)),
                    21: at((turn, 1), (scores, 2)), 23: at((outputs, 1)),
                    30: at((turn, 2), (scores, 3)), 32: at((outputs, 2)),
                    39: at((turn, 3)), 41: at((outputs, 3))}

        class attend_act:

            def __init__(self, act):
                self.act = act

            def load(self, t):
                act = self.act
                act.dma_start(a_q, h_t[Q0:K0, ds(t * P + PAD, P)].rearrange("(c p) n -> p c n", p=P))\
                   .then_inc(sa_q, 16)
                for half in range(2):
                    act.dma_start(a_k[half * HEAD_DIM:half * HEAD_DIM + HEAD_DIM, :, :],
                                  h_t[K0:V0, ds(t * P, 2 * P)].rearrange("(g p) n -> p g n", p=HEAD_DIM))\
                       .then_inc(sa_k, 16)
                act.dma_start(a_v, h_t[V0:GA0, ds(t * P, 2 * P)].rearrange("(c p) n -> p c n", p=P))\
                   .then_inc(sa_v, 16)

            def first(self):
                self.act.sem_inc(sa_pt, 1)
                self.act.sem_inc(sa_out, 1)
                for n in range(NG):
                    self.act.wait_ge(s_store[n], 16 * 13)
                self.act.wait_ge(s_zst, 16 * (GA0 - K0) // P)
                self.act.dma_start(a_mask, consts[:, C_MASK0:C_ALL].rearrange("p (m n) -> p m n", m=2))\
                    .then_inc(sa_mask, 16)
                self.act.dma_start(a_o[:, 0:2], consts[0:HEAD_DIM, 0:2]).then_inc(sa_st, 16)
                self.load(0)

            def exps(self, t, g):
                act = self.act
                act.wait_ge(sa_neg, 4 * t + (g + 1))
                act.activation(a_es, a_sk, ACT.Exp).then_inc(sa_e, 1)
                for r in range(GQA):
                    act.activation(a_p[:, r, :], a_p[:, r, :], ACT.Exp, bias=a_neg[:, r:r + 1],
                                   accum_out=a_sum[:, r:r + 1]).then_inc(sa_e, 1)

            def copy_probs(self, t, g):
                for kt in range(2):
                    self.act.wait_ge(sa_t, 8 * t + (2 * g + kt + 1))
                    self.act.activation(a_pt[:, kt, :], bank_t[kt][:, :], ACT.Copy).then_inc(sa_pt, 1)

            def copy_out(self, t, g):
                act = self.act
                act.wait_ge(sa_o, 4 * t + (g + 1))
                act.wait_ge(sa_st, 64 * t + 16 * (g + 1))
                act.activation(a_o, bank_o[0:HEAD_DIM, :], ACT.Copy).then_inc(sa_out, 1)
                act.wait_ge(sa_out, 4 * t + (g + 2))
                act.dma_start(o_t[g * 256:g * 256 + 256, ds(t * P, P)].rearrange("(r d) n -> d r n", d=HEAD_DIM),
                              a_o.rearrange("p (r n) -> p r n", r=GQA)).then_inc(sa_st, 16)

            def tile(self, t):
                def part_0():
                    self.act.wait_ge(sa_vtr, t + 1)
                    self.act.activation(a_vtok, bank_t[0][:, :].rearrange("p (k n) -> p k n", k=2), ACT.Copy)\
                        .then_inc(sa_vtok, 1)
                    self.exps(t, 0)
                    self.copy_probs(t, 0)
                    self.exps(t, 1)

                def part_1():
                    self.copy_out(t, 0)
                    self.copy_probs(t, 1)
                    self.exps(t, 2)
                    self.copy_out(t, 1)
                    self.copy_probs(t, 2)
                    self.exps(t, 3)

                def part_2():
                    self.copy_out(t, 2)
                    self.copy_probs(t, 3)
                    if not (type(t) is int and t == NTP - 1):
                        self.load(t + 1)
                    self.copy_out(t, 3)
                return part_0, part_1, part_2

        class attend_dve:

            def __init__(self, dve):
                self.dve = dve

            def first(self):
                self.dve.sem_inc(sa_max, 1)
                self.dve.sem_inc(sa_mk, 1)
                self.dve.wait_ge(sa_mask, 16)

            def softmax(self, t, g):
                dve = self.dve
                dve.wait_ge(sa_mk, t + 1)
                dve.wait_ge(sa_pt, 8 * t + (2 * g + 1))
                for r in (0, 2, 1, 3):
                    h = GQA * g + r
                    if r < 2:
                        dve.wait_ge(sa_s, 8 * t + (2 * g + r + 1))
                        dve.nop(nofuse=True)
                    dve.tensor_tensor_reduce(
                        out=a_p[:, r, :], in0=bank_s[r % 2][:, (r // 2) * 256:(r // 2) * 256 + 256],
                        in1=a_mask[:, 0, :], scale=1.0, scalar=sink_row[:, h:h + 1], op0=ALU.add, op1=ALU.max,
                        accum_out=a_mx[:, r:r + 1]).then_inc(sa_max, 1)
                dve.wait_ge(sa_max, 16 * t + (4 * g + 5))
                dve.tensor_scalar(a_neg, a_mx, -1.0, None, ALU.mult).then_inc(sa_dv, 1)
                dve.wait_ge(sa_dv, 12 * t + (3 * g + 1))
                dve.tensor_tensor(a_sk, sink_row[:, GQA * g:GQA * g + GQA], a_neg, ALU.add).then_inc(sa_neg, 1)
                dve.wait_ge(sa_e, 20 * t + (5 * g + 5))
                dve.tensor_tensor(a_den, a_sum, a_es, ALU.add).then_inc(sa_dv, 1)
                dve.wait_ge(sa_dv, 12 * t + (3 * g + 2))
                dve.reciprocal(a_den, a_den).then_inc(sa_dv, 1)
                dve.wait_ge(sa_dv, 12 * t + (3 * g + 3))
                for r in range(GQA):
                    dve.tensor_scalar(a_p[:, r, :], a_p[:, r, :], a_den[:, r:r + 1], None, ALU.mult)\
                       .then_inc(sa_p, 1)

            def tile(self, t):
                def part_0():
                    self.softmax(t, 0)
                    self.softmax(t, 1)

                def part_1():
                    self.softmax(t, 2)
                    self.softmax(t, 3)

                def part_2():
                    self.dve.tensor_copy(a_mask[:, 0, :], a_mask[:, 1, :]).then_inc(sa_mk, 1)
                return part_0, part_1, part_2

        def four(x):
            return x.rearrange("p (h n) -> p h n", h=N_GLA)

        l_q, l_k = work[:, 0:512], work[:, 512:1024]
        l_v = work[:, 1024:2048]
        l_vtok = work[:, 2048:3072]
        l_b = work[:, 3072:3584]
        l_e = [work[:, 3584:4096], work[:, 4096:4608]]
        l_z = [work[:, 4608:5120], work[:, 5120:5632]]
        l_att = work[:, 5632:6144]
        l_qe = work[:, 6144:6656]
        l_ktok = work[:, 6656:7168]
        l_s = work[:, 7168:8192]
        l_og = work[:, 8192:9216]
        l_o = work[:, 3584:4608]
        l_eb = small[:, 40:72]
        l_ss, l_var, l_rstd = small[:, 76:80], small[:, 80:84], small[:, 84:88]
        NZ = 2 + len(LEVELS)

        def halves(x, s):
            return x.rearrange("p (n two s) -> p n two s", two=2, s=s)

        def linear_stages(pe, t, dec=False):
            levels = DEC_LEVELS if dec else LEVELS

            def logits():
                pe.wait_ge(sl_lr, 16 * t + 16)
                pe.wait_ge(sl_up, 4 * t + 1)
                for h in range(N_GLA):
                    mm = pe.matmul(ub[0][:, h * P:h * P + P], w_up_sb[:, h * P:h * P + P], lr[:, :],
                                   start=True, stop=True)
                mm.then_inc(sl_log, 1)

            def values():
                pe.wait_ge(sl_v, 16 * t + 16)
                pe.wait_ge(sl_on, 4 * t + 1)
                for c in range(8):
                    mm = pe.transpose(ub[1 + c // 4][:, (c % 4) * P:(c % 4) * P + P], l_v[:, c * P:c * P + P], ident)
                    if c % 4 == 3:
                        mm.then_inc(sl_vtr, 1)

            def diagonal():
                pe.wait_ge(sl_qs, t + 1)
                pe.wait_ge(sl_k, 16 * t + 16)
                pe.wait_ge(sl_la, t + 1)
                for h in range(N_GLA):
                    hs = slice(h * P, h * P + P)
                    mm = pe.matmul(ub[0][:, hs], l_k[:, hs], l_q[:, hs], start=True, stop=True)
                mm.then_inc(sl_dg, 1)

            def keys():
                pe.wait_ge(sl_zz, NZ * t + 2)
                pe.wait_ge(sl_og, 4 * t + 1)
                for h in range(N_GLA):
                    mm = pe.transpose(ub[3][:, h * P:h * P + P], l_z[0][:, h * P:h * P + P], ident)
                mm.then_inc(sl_kt, 1)

            def level(i):
                s = levels[i]
                pe.wait_ge(sl_zz, NZ * t + (i + 3))
                if i == 1:
                    pe.wait_ge(sl_ktok, t + 1)
                if i >= 2:
                    pe.wait_ge(sl_cp, len(LEVELS) * t + (i - 1))
                for h in range(N_GLA):
                    z = l_z[(i + 1) % 2][:, h * P:h * P + P]
                    mm = pe.matmul(ub[4 - i % 2][:, h * 64:h * 64 + 64], z, halves(z, s)[:, :, 1, :],
                                   start=True, stop=True)
                mm.then_inc(sl_p, 1)

            def outputs():
                pe.wait_ge(sl_cp, len(LEVELS) * t + len(levels))
                pe.wait_ge(sl_dcp, t + 1)
                pe.wait_ge(sl_vtok, 2 * t + 2)
                for h in range(N_GLA):
                    hs = slice(h * P, h * P + P)
                    out = ub[1 + h // 2][:, (h % 2) * DV:(h % 2) * DV + DV]
                    pe.matmul(out, l_att[:, hs], l_vtok[:, h * DV:h * DV + DV], start=True, stop=False)
                    mm = pe.matmul(out, l_qe[:, hs], l_s[:, h * DV:h * DV + DV], start=False, stop=True)
                    if h % 2:
                        mm.then_inc(sl_o, 1)
                pe.wait_ge(sl_ktok, t + 1)
                for h in range(N_GLA):
                    hs = slice(h * P, h * P + P)
                    mm = pe.matmul(ub[4 * (h // 2)][:, (h % 2) * DV:(h % 2) * DV + DV], l_ktok[:, hs],
                                   l_vtok[:, h * DV:h * DV + DV], start=True, stop=True)
                    if h % 2:
                        mm.then_inc(sl_ds, 1)

            def turn():
                pe.wait_ge(sl_up, 4 * t + 5)
                for c in range(8):
                    if c % 2 == 0:
                        pe.wait_ge(sl_on, 4 * t + (c // 2 + 2))
                    mm = pe.transpose(ub[3 + c // 4][:, (c % 4) * P:(c % 4) * P + P], l_o[:, c * P:c * P + P], ident)
                    if c % 4 == 3:
                        mm.then_inc(sl_gt, 1)
            return logits, values, diagonal, keys, level, outputs, turn

        def linear_pe(pe, t):
            logits, values, diagonal, keys, level, outputs, turn = linear_stages(pe, t)
            stages = {2: lambda: (logits(), values()), 5: diagonal, 12: keys,
                      34: lambda: level(len(LEVELS) - 1), 38: outputs, 46: turn}
            for i in range(len(LEVELS) - 1):
                stages[13 + 3 * i] = lambda i=i: level(i)
            return stages

        class linear_act:
            def __init__(self, act):
                self.act = act

            def load(self, t):
                act = self.act
                cols = ds(t * P + PAD, P)
                act.dma_start(lr[0:RANK, :], h_t[LR0:IN_TOTAL, cols]).then_inc(sl_lr, 16)
                act.dma_start(four(l_q), h_t[GQ0:GK0, cols].rearrange("(c p) n -> p c n", p=P)).then_inc(sl_q, 16)
                act.dma_start(four(l_k), h_t[GK0:GV0, cols].rearrange("(c p) n -> p c n", p=P)).then_inc(sl_k, 16)
                act.dma_start(l_v.rearrange("p (c n) -> p c n", c=8),
                              h_t[GV0:GG0, cols].rearrange("(c p) n -> p c n", p=P)).then_inc(sl_v, 16)

            def first(self):
                act = self.act
                act.wait_ge(sa_st, 16 * (4 * NTP + 1))
                act.wait_ge(sl_ini, 3)
                for n in range(NG):
                    act.wait_ge(s_store[n], 16 * (1 + N_PLAIN))
                act.dma_start(l_og[:, 0:2], consts[:, 0:2]).then_inc(sl_st, 16)
                self.load(0)
                act.sem_inc(sl_og, 1)

            def exp(self, t, i, out, in_, scale):
                self.act.activation(out, in_, ACT.Exp, scale=scale / TAU).then_inc(sl_ex, 1)

            def gates(self, t, dec=False):
                act = self.act
                act.wait_ge(sl_log, t + 1)
                act.activation(l_e[0], ub[0][:, :], ACT.Abs).then_inc(sl_a, 1)
                act.wait_ge(sl_a, 3 * t + 1)
                act.activation(l_e[0], l_e[0], ACT.Exp, scale=-1.0).then_inc(sl_a, 1)
                act.wait_ge(sl_a, 3 * t + 2)
                act.activation(l_e[0], l_e[0], ACT.Ln, bias=1.0).then_inc(sl_a, 1)
                for i in range(2):
                    act.wait_ge(sl_vtr, 2 * t + (i + 1))
                    act.activation(l_vtok[:, i * 512:i * 512 + 512], ub[1 + i][:, :], ACT.Copy).then_inc(sl_vtok, 1)
                act.wait_ge(sl_b, t + 1)
                self.exp(t, 0, l_e[0], l_b, 1.0)
                n = DEC_SEQ if dec else P
                act.activation(l_eb[:, 0:4 * P // n], l_b.rearrange("p (m n) -> p m n", n=n)[:, :, n - 1],
                               ACT.Exp, scale=1.0 / TAU).then_inc(sl_eb, 1)
                act.wait_ge(sl_d, (NZ - 1) * t + 1)
                self.exp(t, 1, l_e[1], l_e[1], -1.0)

            def keys(self, t):
                self.act.wait_ge(sl_kt, t + 1)
                self.act.activation(l_ktok, ub[3][:, :], ACT.Copy).then_inc(sl_ktok, 1)

            def level(self, t, i, s):
                self.act.wait_ge(sl_d, (NZ - 1) * t + (i + 2))
                e = halves(l_e[i % 2], s)
                self.act.activation(e[:, :, 0, :], e[:, :, 0, :], ACT.Exp, scale=-1.0 / TAU)
                self.exp(t, i + 2, e[:, :, 1, :], e[:, :, 1, :], 1.0)

            def squares(self, t, nz):
                act = self.act
                act.wait_ge(sl_zz, NZ * t + nz)
                for h in range(N_GLA):
                    act.wait_ge(sl_o, 2 * t + (h // 2 + 1))
                    act.activation(l_o[:, h * DV:h * DV + DV], ub[1 + h // 2][:, (h % 2) * DV:(h % 2) * DV + DV],
                                   ACT.Square, accum_out=l_ss[:, h:h + 1]).then_inc(sl_sq, 1)

            def leave(self, t):
                act = self.act
                act.wait_ge(sl_st, 16 * t + 16)
                og = l_og.rearrange("p (h e n) -> p h e n", e=2, n=P)
                for i in range(2):
                    act.wait_ge(sl_gt, 2 * t + (i + 1))
                    bank = ub[3 + i][:, :].rearrange("p (h e n) -> p h e n", e=2, n=P)
                    for e in range(2):
                        act.activation(og[:, 2 * i:2 * i + 2, e, :], bank[:, :, e, :], ACT.Copy,
                                       scale=gn_col[:, e:e + 1]).then_inc(sl_og, 1)
                act.wait_ge(sl_og, 4 * t + 5)
                act.dma_start(o_t[D_MODEL // 2:D_MODEL, ds(t * P, P)].rearrange("(c p) n -> p c n", p=P),
                              l_og.rearrange("p (c n) -> p c n", c=8)).then_inc(sl_st, 16)

            def tile(self, t):
                def part_0():
                    self.gates(t)
                    self.level(t, 0, LEVELS[0])
                    self.keys(t)
                    self.level(t, 1, LEVELS[1])

                def part_1():
                    for i in range(2, 6):
                        self.level(t, i, LEVELS[i])

                def part_2():
                    self.level(t, 6, LEVELS[6])
                    self.squares(t, NZ)
                    self.load(t + 1)
                    self.leave(t)
                return part_0, part_1, part_2

        class linear_dve:
            def __init__(self, dve):
                self.dve = dve

            def first(self):
                dve = self.dve
                dve.wait_ge(sa_out, 4 * NTP + 1)
                dve.wait_ge(sa_mk, NTP + 1)
                dve.memset(l_s, 0.0).then_inc(sl_ini, 1)
                dve.memset(l_att, 0.0).then_inc(sl_ini, 1)
                dve.memset(lr[:, :], 1.0).then_inc(sl_ini, 1)
                dve.wait_ge(sl_ini, 3)
                dve.sem_inc(sl_up, 1)
                dve.sem_inc(sl_on, 1)

            def copy_diagonal(self, t):
                dve = self.dve
                dve.wait_ge(sl_dg, t + 1)
                dve.nop(nofuse=True)
                dve.copy_predicated(l_att, tables_sb[:, M_DIAG:M_DIAG + 512], ub[0][:, :]).then_inc(sl_dcp, 1)

            def gates(self, t, dec=False):
                dve = self.dve
                dve.wait_ge(sl_q, 16 * t + 16)
                dve.tensor_scalar(l_q, l_q, DK ** -0.5, None, ALU.mult).then_inc(sl_qs, 1)
                dve.wait_ge(sl_a, 3 * t + 3)
                dve.scalar_tensor_tensor(out=l_e[1], in0=ub[0][:, :], scalar=0.0, in1=l_e[0], op0=ALU.min,
                                         op1=ALU.subtract).then_inc(sl_la, 1)
                dve.wait_ge(sl_la, t + 1)
                m = M_SCAN_DEC if dec else M_SCAN
                dve.tensor_tensor_scan(l_b, tables_sb[:, m:m + 512], l_e[1], 0.0, ALU.mult, ALU.add)\
                   .then_inc(sl_b, 1)
                self.copy_diagonal(t)
                dve.wait_ge(sl_ex, NZ * t + 1)
                dve.wait_ge(sl_qs, t + 1)
                dve.tensor_tensor(l_qe, l_q, l_e[0], ALU.mult).then_inc(sl_zz, 1)
                dve.wait_ge(sl_ex, NZ * t + 2)
                dve.wait_ge(sl_k, 16 * t + 16)
                dve.tensor_tensor(l_z[0], l_k, l_e[1], ALU.mult).then_inc(sl_zz, 1)

            def level(self, t, i, s):
                dve = self.dve
                dve.wait_ge(sl_ex, NZ * t + (i + 3))
                if i == 1:
                    dve.wait_ge(sl_kt, t + 1)
                if i >= 2:
                    dve.wait_ge(sl_p, len(LEVELS) * t + (i - 1))
                z, e, q, k = (halves(x, s) for x in (l_z[(i + 1) % 2], l_e[i % 2], l_q, l_k))
                dve.tensor_tensor(z[:, :, 0, :], k[:, :, 0, :], e[:, :, 0, :], ALU.mult)
                dve.tensor_tensor(z[:, :, 1, :], q[:, :, 1, :], e[:, :, 1, :], ALU.mult).then_inc(sl_zz, 1)

            def take(self, t, i, s):
                dve = self.dve
                if i:
                    dve.wait_ge(sl_cp, len(LEVELS) * t + i)
                else:
                    dve.wait_ge(sl_dcp, t + 1)
                dve.wait_ge(sl_p, len(LEVELS) * t + (i + 1))
                dve.nop(nofuse=True)
                m = LEVELS.index(s) * 256
                dve.copy_predicated(halves(l_att, s)[:, :, 1, :],
                                    tables_sb[:, m:m + 256].rearrange("p (n s) -> p n s", s=s),
                                    ub[4 - i % 2][:, 0:256].rearrange("p (n s) -> p n s", s=s)).then_inc(sl_cp, 1)

            def variance(self, t):
                dve = self.dve
                dve.wait_ge(sl_sq, 4 * t + 4)
                dve.tensor_scalar(l_var, l_ss, 1.0 / DV, EPS, ALU.mult, ALU.add).then_inc(sl_var, 1)

            def scale_out(self, t):
                dve = self.dve
                dve.wait_ge(sl_rs, t + 1)
                for h in range(N_GLA):
                    dve.tensor_scalar(l_o[:, h * DV:h * DV + DV],
                                      ub[1 + h // 2][:, (h % 2) * DV:(h % 2) * DV + DV],
                                      l_rstd[:, h:h + 1], None, ALU.mult).then_inc(sl_on, 1)

            def state(self, t):
                dve = self.dve
                dve.wait_ge(sl_eb, t + 1)
                for h in range(N_GLA):
                    dve.wait_ge(sl_ds, 2 * t + (h // 2 + 1))
                    sh = l_s[:, h * DV:h * DV + DV]
                    dve.scalar_tensor_tensor(out=sh, in0=sh, scalar=l_eb[:, h:h + 1],
                                             in1=ub[4 * (h // 2)][:, (h % 2) * DV:(h % 2) * DV + DV],
                                             op0=ALU.mult, op1=ALU.add).then_inc(sl_up, 1)

            def tile(self, t):
                def part_0():
                    self.gates(t)
                    self.level(t, 0, LEVELS[0])
                    self.level(t, 1, LEVELS[1])
                    self.take(t, 0, LEVELS[0])

                def part_1():
                    for i in range(2, 6):
                        self.level(t, i, LEVELS[i])
                        self.take(t, i - 1, LEVELS[i - 1])

                def part_2():
                    self.level(t, 6, LEVELS[6])
                    self.take(t, 5, LEVELS[5])
                    self.take(t, 6, LEVELS[6])
                    self.variance(t)
                    self.state(t)
                    self.scale_out(t)
                return part_0, part_1, part_2

        def linear_pool(pool, t, levels, n):
            pool.wait_ge(sl_b, t + 1)
            b = l_b.rearrange("p (m n) -> p m n", n=n)
            pool.tensor_tensor(l_e[1].rearrange("p (m n) -> p m n", n=n), b,
                               b[:, :, n - 1:n].to_broadcast([P, 4 * P // n, n]), ALU.subtract).then_inc(sl_d, 1)
            for i, s in enumerate(levels):
                pool.wait_ge(sl_zz, NZ * t + (i + 1))
                b = l_b.rearrange("p (m n) -> p m n", n=2 * s)
                pool.tensor_tensor(l_e[i % 2].rearrange("p (m n) -> p m n", n=2 * s), b,
                                   b[:, :, s - 1:s].to_broadcast([P, 2 * P // s, 2 * s]), ALU.subtract)\
                    .then_inc(sl_d, 1)
            pool.wait_ge(sl_var, t + 1)
            pool.tensor_tensor(l_rstd, l_var, mhalf[:, :], ALU.pow).then_inc(sl_rs, 1)

        T = NTP
        d_s = [raw[:, :], xn[:, :]]
        d_q = [work[:, 3584:4608], work[:, 4608:5632]]
        d_q_own = [work[:, 3584:4736].rearrange("p (s m) -> p s m", m=P + DEC_SEQ)[:, :, 0:DEC_SEQ],
                   work[:, 4608:5760].rearrange("p (s m) -> p s m", m=P + DEC_SEQ)[:, :, 0:DEC_SEQ]]
        d_k = [l_v, l_s]
        d_bank = [banks[0], banks[1], banks[2], ub[3]]

        def decode_pe(pe):
            logits, values, diagonal, keys, level, outputs, turn = linear_stages(pe, T, dec=True)
            logits()
            values()
            diagonal()
            keys()
            for i in range(len(DEC_LEVELS)):
                level(i)
            pe.wait_ge(sl_cp, len(LEVELS) * T + len(DEC_LEVELS))
            pe.wait_ge(sl_dcp, T + 1)
            pe.wait_ge(sl_vtok, 2 * T + 2)
            pe.wait_ge(s_staged, NG * (N_ITEMS + 2))
            for h in range(N_GLA):
                out = ub[1 + h // 2][:, (h % 2) * DV:(h % 2) * DV + DV]
                vh = l_vtok[:, h * DV:h * DV + DV]
                pe.wait_ge(sd_q, 2 + h + 1)
                pe.wait_ge(sd_in[h % 2], 16 * (h // 2 + 1))
                pe.matmul(out, l_att[:, h * P:h * P + P], vh, start=True, stop=False)
                for s in range(DEC_BATCH):
                    mm = pe.matmul(out, d_q[h % 2][:, s * P:s * P + P], d_s[h % 2][:, s * DV:s * DV + DV],
                                   start=False, stop=(s == DEC_BATCH - 1))
                mm.then_inc(sd_o, 1)
                pe.wait_ge(sd_k, h + 1)
                for i in range(4):
                    if h:
                        pe.wait_ge(sd_up, 8 * (h - 1) + 2 * i + 2)
                    for s in (2 * i, 2 * i + 1):
                        mm = pe.matmul(d_bank[i][:, (s % 2) * DV:(s % 2) * DV + DV],
                                       d_k[h % 2][:, s * P:s * P + P], vh, start=True, stop=True)
                    mm.then_inc(sd_ds, 1)
            pe.wait_ge(sd_up, 8 * N_GLA)
            for c in range(8):
                if c % 2 == 0:
                    pe.wait_ge(sl_on, 4 * T + (c // 2 + 2))
                mm = pe.transpose(ub[3 + c // 4][:, (c % 4) * P:(c % 4) * P + P], l_o[:, c * P:c * P + P], ident)
                if c % 4 == 3:
                    mm.then_inc(sl_gt, 1)

        def decode_act(act, lin):
            act.wait_ge(sl_up, 4 * NTP + 1)
            act.dma_start(gla_p.rearrange("h d e -> d h e"), l_s.rearrange("p (h e) -> p h e", h=N_GLA))\
               .then_inc(sd_gp, 16)
            act.wait_ge(s_wready, 4 * (N_ITEMS + 1))
            for n in range(NG):
                act.wait_ge(s_store[n], 16 * (N_ITEMS + 1))

            def load(h):
                act.dma_start(d_s[h % 2].rearrange("p (s e) -> p s e", s=DEC_BATCH),
                              state[:, h].rearrange("s d e -> d s e")).then_inc(sd_in[h % 2], 16)

            load(0)
            load(1)
            lin.gates(T, dec=True)
            lin.level(T, 0, DEC_LEVELS[0])
            lin.keys(T)
            for i in range(1, len(DEC_LEVELS)):
                lin.level(T, i, DEC_LEVELS[i])
            for h in range(N_GLA):
                act.wait_ge(sd_up, 8 * h + 8)
                act.dma_start(gla_s[:, h].rearrange("s d e -> d s e"),
                              d_s[h % 2].rearrange("p (s e) -> p s e", s=DEC_BATCH)).then_inc(sd_out[h % 2], 16)
                if h + 2 < N_GLA:
                    act.wait_ge(sd_out[h % 2], 16 * (h // 2 + 1))
                    load(h + 2)
            act.wait_ge(sd_o, N_GLA)
            for h in range(N_GLA):
                act.activation(l_o[:, h * DV:h * DV + DV], ub[1 + h // 2][:, (h % 2) * DV:(h % 2) * DV + DV],
                               ACT.Square, accum_out=l_ss[:, h:h + 1]).then_inc(sl_sq, 1)
            lin.leave(T)
            for h in range(2):
                act.wait_ge(sd_out[h], 32)
            act.wait_ge(sl_st, 16 * (NT + 1))

        def decode_dve(dve, lin):
            dve.memset(l_att, 0.0).then_inc(sl_ini, 1)
            dve.wait_ge(sl_ini, 4)
            lin.gates(T, dec=True)
            lin.level(T, 0, DEC_LEVELS[0])
            for i in range(1, len(DEC_LEVELS)):
                lin.level(T, i, DEC_LEVELS[i])
                lin.take(T, i - 1, DEC_LEVELS[i - 1])
            lin.take(T, len(DEC_LEVELS) - 1, DEC_LEVELS[-1])
            for i in range(2):
                dve.memset(d_q[i], 0.0).then_inc(sd_q, 1)
            dve.wait_ge(sd_q, 2)
            dve.wait_ge(sl_ktok, T + 1)
            dve.wait_ge(sd_gp, 16)
            dve.wait_ge(sl_eb, T + 1)
            for h in range(N_GLA):
                if h >= 2:
                    dve.wait_ge(sd_o, h - 1)
                dve.tensor_copy(d_q_own[h % 2], l_qe[:, h * P:h * P + P].rearrange("p (s n) -> p s n", n=DEC_SEQ))\
                   .then_inc(sd_q, 1)
                if h >= 2:
                    dve.wait_ge(sd_ds, 4 * (h - 1))
                for s in range(DEC_BATCH):
                    ins = dve.tensor_scalar(d_k[h % 2][:, s * P:s * P + P], l_ktok[:, h * P:h * P + P],
                                            seq_col[:, s:s + 1], None, ALU.mult)
                ins.then_inc(sd_k, 1)
                if h >= 1:
                    update(dve, h - 1)
            update(dve, N_GLA - 1)
            lin.variance(T)
            lin.scale_out(T)

        def update(dve, h):
            for s in range(DEC_BATCH):
                dve.wait_ge(sd_ds, 4 * h + s // 2 + 1)
                m = h * DEC_BATCH + s
                sh = d_s[h % 2][:, s * DV:s * DV + DV]
                dve.scalar_tensor_tensor(out=sh, in0=sh, scalar=l_eb[:, m:m + 1],
                                         in1=d_bank[s // 2][:, (s % 2) * DV:(s % 2) * DV + DV],
                                         op0=ALU.mult, op1=ALU.add).then_inc(sd_up, 1)

        KEYS = CACHE + DEC_SEQ
        b_q = work[:, 0:1024].rearrange("p (g r n) -> p g r n", g=2, r=GQA)
        b_kn = work[:, 1024:1280].rearrange("p (c n) -> p c n", c=2)
        b_vn = work[:, 1280:1536].rearrange("p (c n) -> p c n", c=2)
        b_ck = [work[:, 1536:1792], work[:, 1792:2048]]
        b_cv = [work[:, 2048:2304], work[:, 2304:2560]]
        b_ks = work[:, 2560:2848].rearrange("p (g n) -> p g n", g=2)
        b_p = work[:, 2848:3136].rearrange("p (g n) -> p g n", g=2)
        b_ptc = work[:, 3136:3392]
        b_ptn = work[0:DEC_SEQ, 3392:3648]
        b_vnew = work[0:DEC_SEQ, 3648:3904]
        b_qb = work[:, 3904:4032].rearrange("p (g n) -> p g n", g=2)
        b_vb = work[:, 4032:4064].rearrange("p (c n) -> p c n", c=2)
        b_o = work[0:HEAD_DIM, 4064:6112].rearrange("p (h n) -> p h n", h=N_HEADS)
        b_ex = [work[:, 6112 + 256 * i:6368 + 256 * i] for i in range(4)]
        b_kp = work[:, 7136:7392].rearrange("p (c n) -> p c n", c=2)
        b_vp = work[:, 7392:7648].rearrange("p (c n) -> p c n", c=2)
        b_mx, b_mn, b_neg, b_sk, b_es, b_sum, b_den = (small[:, 8 + 2 * i:10 + 2 * i] for i in range(7))
        kb, vb, sb_, pb, nb, ob = banks[0:6]

        def sequences(eng, body, last):
            with eng.Fori(0, DEC_BATCH // 2 - 1) as i:
                for slot in range(2):
                    body(2 * i + slot, slot, 16 * i + 16, False)
            for slot in range(2):
                body(DEC_BATCH - 2 + slot, slot, 16 * (DEC_BATCH // 2), True)

        def cached_pe(pe):
            pe.wait_ge(sb_in, 16 * 8)
            pe.wait_ge(sl_og, 4 * NT + 1)
            for i, x in enumerate((b_kp, b_vp, b_kn, b_vn)):
                for c in range(2):
                    mm = pe.transpose(ub[i][:, c * P:c * P + P], x[:, c, :], ident)
                mm.then_inc(sb_xt, 1)
            pe.wait_ge(sb_xc, 4)

            def body(b, slot, m, last):
                pe.wait_ge(sb_ck[slot], m)
                pe.wait_ge(sb_new, b + 1)
                for gp in range(2):
                    pe.transpose(kb[:, gp * P:gp * P + P], b_ck[slot][:, gp * P:gp * P + P], ident)
                for c in range(2):
                    mm = pe.transpose(vb[0:DEC_SEQ, c * P:c * P + P], b_vb[:, c, :], ident)
                mm.then_inc(sb_kt, 1)
                pe.wait_ge(sb_ks, b + 1)
                pe.nop(nofuse=True)
                for gp in range(2):
                    for half in range(2):
                        rows = slice(half * HEAD_DIM, half * HEAD_DIM + HEAD_DIM)
                        mm = pe.matmul(sb_[rows, gp * KEYS:gp * KEYS + KEYS], b_qb[rows, gp, :], b_ks[rows, gp, :],
                                       start=True, stop=True)
                mm.then_inc(sb_s, 1)
                pe.wait_ge(sb_pr, 2 * b + 2)
                for gp in range(2):
                    pe.transpose(pb[:, gp * P:gp * P + P], b_p[:, gp, 0:CACHE], ident)
                for gp in range(2):
                    mm = pe.transpose(nb[0:DEC_SEQ, gp * P:gp * P + P], b_p[:, gp, CACHE:KEYS], ident)
                mm.then_inc(sb_pt, 1)
                pe.wait_ge(sb_cv[slot], m)
                pe.wait_ge(sb_pc, b + 1)
                pe.wait_ge(sb_oc, b + 1)
                for g in range(N_KV):
                    cols = slice((g // 2) * P + (g % 2) * HEAD_DIM, (g // 2) * P + (g % 2) * HEAD_DIM + HEAD_DIM)
                    dims = slice(g * HEAD_DIM, g * HEAD_DIM + HEAD_DIM)
                    pe.matmul(ob[0:HEAD_DIM, dims], b_cv[slot][:, dims], b_ptc[:, cols], start=True, stop=False)
                    mm = pe.matmul(ob[0:HEAD_DIM, dims], b_vnew[:, dims], b_ptn[:, cols], start=False, stop=True)
                mm.then_inc(sb_av, 1)

            sequences(pe, body, None)

        def cached_act(act):
            q_v = h_t[Q0:K0, PAD + SEQ:PAD + TOK].rearrange("(g f r d) n -> f d g r n", g=2, f=2, r=GQA)
            for half in range(2):
                for gp in range(2):
                    act.dma_start(b_q[half * HEAD_DIM:half * HEAD_DIM + HEAD_DIM, gp], q_v[half][:, gp])\
                       .then_inc(sb_in, 16)
            for x, row, col in ((b_kn, K0, PAD + SEQ), (b_vn, V0, PAD + SEQ),
                                (b_kp, K0, PAD + SEQ - P), (b_vp, V0, PAD + SEQ - P)):
                act.dma_start(x, h_t[row:row + 256, col:col + P].rearrange("(c p) n -> p c n", p=P))\
                   .then_inc(sb_in, 16)

            def load(b, slot):
                act.dma_start(b_ck[slot], cache_k[ds(b, 1)].rearrange("a t n -> (a t) n")).then_inc(sb_ck[slot], 16)
                act.dma_start(b_cv[slot], cache_v[ds(b, 1)].rearrange("a t n -> (a t) n")).then_inc(sb_cv[slot], 16)

            load(0, 0)
            load(1, 1)
            for i in range(4):
                act.wait_ge(sb_xt, i + 1)
                act.activation(b_ex[i], ub[i][:, 0:256], ACT.Copy).then_inc(sb_xc, 1)
            act.wait_ge(sb_xc, 4)
            act.dma_start(win_kp, b_ex[0]).then_inc(sb_w, 16)
            act.dma_start(win_vp, b_ex[1]).then_inc(sb_w, 16)
            act.dma_start(win_ks[:, CACHE - DEC_SEQ:CACHE, :], b_ex[2]).then_inc(sb_w, 16)
            act.dma_start(win_vs[:, CACHE - DEC_SEQ:CACHE, :], b_ex[3]).then_inc(sb_w, 16)
            act.sem_inc(sb_oc, 1)

            def body(b, slot, m, last):
                act.wait_ge(sb_kt, b + 1)
                act.activation(b_ks[:, :, 0:CACHE], kb[:, 0:256].rearrange("p (g n) -> p g n", g=2), ACT.Copy)
                act.activation(b_vnew, vb[0:DEC_SEQ, 0:256], ACT.Copy).then_inc(sb_ks, 1)
                act.wait_ge(sb_neg, b + 1)
                act.activation(b_es, b_sk, ACT.Exp)
                for gp in range(2):
                    act.activation(b_p[:, gp, :], sb_[:, gp * KEYS:gp * KEYS + KEYS], ACT.Exp,
                                   bias=b_neg[:, gp:gp + 1], accum_out=b_sum[:, gp:gp + 1]).then_inc(sb_e, 1)
                act.wait_ge(sb_pt, b + 1)
                act.activation(b_ptc, pb[:, 0:256], ACT.Copy)
                act.activation(b_ptn, nb[0:DEC_SEQ, 0:256], ACT.Copy).then_inc(sb_pc, 1)
                act.wait_ge(sb_av, b + 2)
                act.activation(b_o[:, :, ds(b * DEC_SEQ, DEC_SEQ)],
                               ob[0:HEAD_DIM, 0:256].rearrange("p (h n) -> p h n", h=N_HEADS), ACT.Copy)\
                   .then_inc(sb_oc, 1)
                if not last:
                    load(b + 2, slot)

            sequences(act, body, None)
            act.wait_ge(sb_oc, DEC_BATCH + 1)
            act.dma_start(o_t[0:D_MODEL // 2, SEQ:TOK].rearrange("(h d) n -> d h n", d=HEAD_DIM), b_o)\
               .then_inc(sb_w, 16)
            act.wait_ge(sb_w, 16 * 5)

        def cached_dve(dve):
            dve.wait_ge(sb_in, 16 * 8)
            dve.sem_inc(sb_av, 1)

            def body(b, slot, m, last):
                tok = ds(b * DEC_SEQ, DEC_SEQ)
                dve.wait_ge(sb_av, b + 1)
                dve.tensor_copy(b_qb.rearrange("p g (r n) -> p g r n", r=GQA), b_q[:, :, :, tok])
                dve.tensor_copy(b_vb, b_vn[:, :, tok])
                dve.tensor_copy(b_ks[:, :, CACHE:KEYS], b_kn[:, :, tok]).then_inc(sb_new, 1)
                dve.wait_ge(sb_s, b + 1)
                dve.tensor_reduce(b_mx, sb_[:, 0:2 * KEYS].rearrange("p (g n) -> p g n", g=2), AX.X, ALU.max)\
                   .then_inc(sb_dv, 1)
                dve.wait_ge(sb_dv, 5 * b + 1)
                dve.tensor_tensor(b_mn, b_mx, sink_dec[:, :], ALU.max).then_inc(sb_dv, 1)
                dve.wait_ge(sb_dv, 5 * b + 2)
                dve.tensor_scalar(b_neg, b_mn, -1.0, None, ALU.mult).then_inc(sb_dv, 1)
                dve.wait_ge(sb_dv, 5 * b + 3)
                dve.tensor_tensor(b_sk, sink_dec[:, :], b_neg, ALU.add).then_inc(sb_neg, 1)
                dve.wait_ge(sb_e, 2 * b + 2)
                dve.tensor_tensor(b_den, b_sum, b_es, ALU.add).then_inc(sb_dv, 1)
                dve.wait_ge(sb_dv, 5 * b + 4)
                dve.reciprocal(b_den, b_den).then_inc(sb_dv, 1)
                dve.wait_ge(sb_dv, 5 * b + 5)
                for gp in range(2):
                    dve.tensor_scalar(b_p[:, gp, :], b_p[:, gp, :], b_den[:, gp:gp + 1], None, ALU.mult)\
                       .then_inc(sb_pr, 1)

            sequences(dve, body, None)

        @block.gpsimd
        def _(pool):
            pool.memset(mhalf[:, :], -0.5).then_inc(s_mh, 1)
            pool.wait_ge(s_tload, 16)
            pool.tensor_copy(tables_sb[:, :], work[:, 2 * D_MODEL:2 * D_MODEL + M_ALL]).then_inc(s_tables, 1)
            pool.wait_ge(s_mh, 1)
            with pool.Fori(0, NT) as t:
                pool.wait_ge(s_var, t + 1)
                pool.tensor_tensor(rstd, var, mhalf[:, 0:1], ALU.pow).then_inc(s_rstd, 1)
            with pool.Fori(0, NTP) as t:
                linear_pool(pool, t, LEVELS, P)
            linear_pool(pool, T, DEC_LEVELS, DEC_SEQ)

        @block.scalar
        def _(act):
            act.sem_inc(s_wfree, 4)
            act.sem_inc(s_staged, 3)
            act.wait_ge(s_const, 16 * 6)

            def x_tile(t, slot, m):
                act.wait_ge(s_x[slot], m)
                act.wait_ge(s_xt, 4 * t + 4)
                act.activation(xn[:, :], x_buf[slot], ACT.Square, accum_out=ss[:, slot:slot + 1])\
                   .then_inc(s_ss, 1)
                for b in range(4):
                    act.wait_ge(s_xt, 4 * t + (b + 5))
                    act.activation(x_hi[:, 4 * b:4 * b + 4, ds(t * P, P)],
                                   xt_bank[b][:, :].rearrange("p (k n) -> p k n", k=4), ACT.Copy)\
                       .then_inc(s_xhi, 1)

            act.sem_inc(s_xt, 4)
            with act.Fori(0, NTP // 2) as i:
                for slot in range(2):
                    x_tile(2 * i + slot, slot, 16 * i + 16)
            x_tile(NTP, 0, 16 * (NTP // 2 + 1))

            def item_norm_b(j, n):
                wait_acc(act, j, n)
                act.wait_ge(s_ssq, (j - 1) * NG + (n + 1))
                act.activation(tmp_a, acc[n][:, 0:TN], ACT.Square).then_inc(s_sq, 1)
                act.wait_ge(s_v, (j - 1) * NG + (n + 2))
                act.activation(tmp_b, tmp_b, ACT.Sqrt).then_inc(s_sd, 1)

            def item_silu(j, n):
                wait_acc(act, j, n)
                act.wait_ge(s_staged, j * NG + (n + 3))
                act.activation(tmp_a, acc[n][:, 0:TN], ACT.Exp, scale=-1.0).then_inc(s_sig, 1)

            def nothing(j, n):
                pass

            def item(j, before, now, unit=(lambda: None, lambda: None, lambda: None)):
                split_hi(act, j)
                before(j - 1, 2)
                unit[0]()
                now(j, 0)
                unit[1]()
                now(j, 1)
                unit[2]()

            act.sem_inc(s_ssq, 1)
            split_hi(act, 0, RANK)
            item(1, nothing, item_norm_b)
            with act.Fori(2, 1 + N_QK) as j:
                item(j, item_norm_b, item_norm_b)
            item(1 + N_QK, item_norm_b, nothing)
            with act.Fori(2 + N_QK, 1 + N_PLAIN) as j:
                item(j, nothing, nothing)
            attend = attend_act(act)
            act.wait_ge(s_tab, 16 * 21)
            act.wait_ge(s_tables, 1)
            attend.first()
            item(1 + N_PLAIN, nothing, item_silu, attend.tile(0))
            with act.Fori(2 + N_PLAIN, J_GLA - 1) as j:
                item(j, item_silu, item_silu, attend.tile(j - (1 + N_PLAIN)))
            item(J_GLA - 1, item_silu, item_silu, attend.tile(NTP - 1))
            linear = linear_act(act)
            linear.first()
            with act.Fori(J_GLA, 1 + N_ITEMS) as j:
                item(j, item_silu, item_silu, linear.tile(j - J_GLA))
            item_silu(N_ITEMS, 2)
            decode_act(act, linear)
            cached_act(act)

        @block.tensor
        def _(pe):
            pe.wait_ge(s_const, 16 * 6)

            with pe.Fori(0, NT) as t:
                pe.wait_ge(s_xn, t + 3)
                for b in range(4):
                    pe.wait_ge(s_xlo, 4 * t + (b + 1))
                    for k in range(4):
                        c = (4 * b + k) * P
                        mm = pe.transpose(xt_bank[b][:, k * P:k * P + P], xn[:, c:c + P], ident)
                    mm.then_inc(s_xt, 1)

            def item(j, cols, norm=False, norm_before=False, stages={}):
                for n in range(NG):
                    pe.wait_ge(s_staged, NG * j + (n + 1))
                    for k in range(KT):
                        if n * KT + k in stages:
                            stages[n * KT + k]()
                        if n == 0 and k % 4 == 0:
                            pe.wait_ge(s_wready, 4 * j + (k // 4 + 1))
                        if n > 0 and k == 4 and norm:
                            sum_squares(j, n - 1)
                        if n == 0 and k == 4 and norm_before:
                            sum_squares(j - 1, NG - 1)
                        tok = slice(n * TN, n * TN + TN)
                        out = acc[n][0:cols, 0:TN]
                        pe.matmul(out, w_lo[:, k, 0:cols], x_hi[:, k, tok], start=(k == 0), stop=False)
                        pe.matmul(out, w_hi[:, k, 0:cols], x_lo[:, k, tok], start=False, stop=False)
                        mm = pe.matmul(out, w_hi[:, k, 0:cols], x_hi[:, k, tok], start=False,
                                       stop=(k == KT - 1))
                        if n == NG - 1 and k % 4 == 3:
                            mm.then_inc(s_wfree, 1)
                    if n < NG - 1:
                        mm.then_inc(s_acc, 1)

            def sum_squares(j, n):
                pe.wait_ge(s_sq, (j - 1) * NG + (n + 1))
                pe.wait_ge(s_v, (j - 1) * NG + (n + 1))
                pe.matmul(ss_bank[:, 0:TN], ones_pair, tmp_a, start=True, stop=True).then_inc(s_ssq, 1)

            item(0, RANK)
            item(1, P, norm=True)
            with pe.Fori(2, 1 + N_QK) as j:
                item(j, P, norm=True, norm_before=True)
            item(1 + N_QK, P, norm_before=True)
            with pe.Fori(2 + N_QK, 1 + N_PLAIN) as j:
                item(j, P)
            pe.wait_ge(s_tab, 16 * 21)
            with pe.Fori(1 + N_PLAIN, J_GLA) as j:
                item(j, P, stages=attend_pe(pe, j - (1 + N_PLAIN)))
            with pe.Fori(J_GLA, 1 + N_ITEMS) as j:
                item(j, P, stages=linear_pe(pe, j - J_GLA))
            decode_pe(pe)
            cached_pe(pe)

        @block.vector
        def _(dve):
            dve.sem_inc(s_xn, 2)
            dve.sem_inc(s_v, 1)
            dve.sem_inc(s_xlo, 4)
            dve.wait_ge(s_const, 16 * 6)
            dve.tensor_scalar(gq_col[:, 0:1], gq_col[:, 0:1], HEAD_DIM ** -0.5, None, ALU.mult)\
               .then_inc(s_nchain, 1)

            def x_tile(t, slot):
                dve.wait_ge(s_ss, t + 1)
                dve.tensor_scalar(var[:, :], ss[:, slot:slot + 1], 1.0 / D_MODEL, EPS, ALU.mult, ALU.add)\
                   .then_inc(s_var, 1)
                dve.wait_ge(s_rstd, t + 1)
                dve.scalar_tensor_tensor(out=xn[:, :], in0=x_buf[slot], scalar=rstd[:, 0:1],
                                         in1=g_row, op0=ALU.mult, op1=ALU.mult).then_inc(s_xn, 1)
                for b in range(4):
                    dve.wait_ge(s_xhi, 4 * t + (b + 1))
                    dst = x_lo[:, 4 * b:4 * b + 4, ds(t * P, P)]
                    dve.tensor_tensor(dst, xt_bank[b][:, :].rearrange("p (k n) -> p k n", k=4),
                                      x_hi[:, 4 * b:4 * b + 4, ds(t * P, P)].bitcast(F32),
                                      ALU.subtract).then_inc(s_xlo, 1)

            with dve.Fori(0, NTP // 2) as i:
                for slot in range(2):
                    x_tile(2 * i + slot, slot)
            x_tile(NTP, 0)
            dve.wait_ge(s_xt, 4 * NT + 4)
            dve.memset(xn[:, 5 * TN:5 * TN + PAD], 0.0).then_inc(s_zero, 1)

            def staging_free(j, n):
                dve.wait_ge(s_store[n], 16 * j)

            def done(ins):
                ins.then_inc(s_staged, 1)

            def plain(j, n, rows=P, first=False):
                wait_acc(dve, j, n)
                if not first:
                    staging_free(j, n)
                done(dve.tensor_copy(stage[n][0:rows, :], acc[n][0:rows, 0:TN]))

            def normed(which):
                def run(j, n):
                    dve.wait_ge(s_ssq, (j - 1) * NG + (n + 2))
                    dve.tensor_scalar(tmp_b, ss_bank[:, 0:TN], 1.0 / HEAD_DIM, EPS, ALU.mult, ALU.add)\
                       .then_inc(s_v, 1)
                    dve.wait_ge(s_sd, (j - 1) * NG + (n + 1))
                    staging_free(j, n)
                    dve.reciprocal(stage[n], tmp_b).then_inc(s_nchain, 1)
                    dve.wait_ge(s_nchain, (j - 1) * NG + (n + 2))
                    done(dve.scalar_tensor_tensor(out=stage[n], in0=acc[n][:, 0:TN],
                                                  scalar=gq_col[:, which:which + 1], in1=stage[n],
                                                  op0=ALU.mult, op1=ALU.mult))
                return run

            def silu(j, n):
                base = (j - (1 + N_PLAIN)) * (2 * NG) + 2 * n
                dve.wait_ge(s_sig, (j - (1 + N_PLAIN)) * NG + (n + 1))
                dve.tensor_scalar(tmp_a, tmp_a, 1.0, None, ALU.add).then_inc(s_schain, 1)
                dve.wait_ge(s_schain, base + 1)
                dve.reciprocal(tmp_a, tmp_a).then_inc(s_schain, 1)
                dve.wait_ge(s_schain, base + 2)
                staging_free(j, n)
                done(dve.tensor_tensor(stage[n], acc[n][:, 0:TN], tmp_a, ALU.mult))

            def item(j, before, now, unit=(lambda: None, lambda: None, lambda: None)):
                split_lo(dve, j)
                before(j - 1, 2)
                unit[0]()
                now(j, 0)
                unit[1]()
                now(j, 1)
                unit[2]()

            q, k = normed(0), normed(1)
            split_lo(dve, 0, RANK)
            plain(0, 0, RANK, True)
            plain(0, 1, RANK, True)
            split_lo(dve, 1)
            plain(0, 2, RANK, True)
            q(1, 0)
            q(1, 1)
            n_q = (K0 - Q0) // P
            with dve.Fori(2, 1 + n_q) as j:
                item(j, q, q)
            item(n_q + 1, q, k)
            item(n_q + 2, k, k)
            item(n_q + 3, k, plain)
            with dve.Fori(n_q + 4, 1 + N_PLAIN) as j:
                item(j, plain, plain)
            attend = attend_dve(dve)
            dve.wait_ge(s_tab, 16 * 21)
            dve.wait_ge(s_tables, 1)
            attend.first()
            item(1 + N_PLAIN, plain, silu, attend.tile(0))
            with dve.Fori(2 + N_PLAIN, J_GLA) as j:
                item(j, silu, silu, attend.tile(j - (1 + N_PLAIN)))
            linear = linear_dve(dve)
            linear.first()
            with dve.Fori(J_GLA, 1 + N_ITEMS) as j:
                item(j, silu, silu, linear.tile(j - J_GLA))
            silu(N_ITEMS, 2)
            decode_dve(dve, linear)
            cached_dve(dve)


def project_out(nc, sem, dram):
    x_p, x_s, w_out, h_t, o_t, y_p, y_s = dram
    with ExitStack() as ctx:
        def sb(name, shape, dt=F32):
            return ctx.enter_context(nc.sbuf_tensor(name, shape, dt))

        m_hi = sb("m_hi", [P, KT, TOK], F32R)
        m_lo = sb("m_lo", [P, KT, TOK], F32R)
        w_raw = sb("wo_raw", [P, KT, WCH])
        w_hi = sb("wo_hi", [P, KT, WCH], F32R)
        w_lo = sb("wo_lo", [P, KT, WCH], F32R)
        parts = sb("parts", [P, 3, 2, TN])
        x_res = sb("x_res", [P, 3, WCH])
        y_sb = sb("y_sb", [P, 3, WCH])
        acc = [ctx.enter_context(nc.psum_tensor(f"p2_{i}", [P, 512], F32)) for i in range(3)]

        t_part = [sem(f"t_part{i}") for i in range(3)]
        t_mul = sem("t_mul")
        t_mhi = sem("t_mhi")
        t_mlo = sem("t_mlo")
        t_w = [sem(f"t_w{i}") for i in range(4)]
        t_whi = sem("t_whi")
        t_wready = sem("t_wready")
        t_wfree = sem("t_wfree")
        t_x = [sem(f"t_x{i}") for i in range(3)]
        t_acc = sem("t_acc")
        t_y = sem("t_y")
        t_st = [sem(f"t_st{i}") for i in range(3)]
        block = ctx.enter_context(nc.Block())
        w_v = w_out.rearrange("(k p) n -> p k n", p=P)

        def load_w(eng, c):
            for q in range(4):
                eng.wait_ge(t_wready, 4 * c + (q + 1))
                eng.dma_start(w_raw[:, 4 * q:4 * q + 4, :], w_v[:, 4 * q:4 * q + 4, ds(c * WCH, WCH)])\
                   .then_inc(t_w[q], 16)

        def rows_of(p, s, t, c):
            if t < NTP:
                return p[t * P:t * P + P, ds(c * WCH, WCH)]
            return s[:, ds(c * WCH, WCH)]

        @block.sync
        def _(sp):
            for q in range(4):
                sp.dma_start(w_raw[:, 4 * q:4 * q + 4, :], w_v[:, 4 * q:4 * q + 4, 0:WCH]).then_inc(t_w[q], 16)

            def load_parts(k, gate_row):
                for n in range(NG):
                    sp.wait_ge(t_mlo, NG * k + (n + 1))
                    tok = slice(n * TN, n * TN + TN)
                    sp.dma_start(parts[:, n, 0, :], o_t[ds(k * P, P), tok]).then_inc(t_part[n], 16)
                    sp.dma_start(parts[:, n, 1, :], h_t[ds(gate_row, P), PAD + n * TN:PAD + n * TN + TN])\
                      .then_inc(t_part[n], 16)

            with sp.Fori(0, KT // 2) as k:
                load_parts(k, k * P + GA0)
            with sp.Fori(KT // 2, KT) as k:
                load_parts(k, k * P + (GG0 - KT // 2 * P))

            with sp.Fori(0, NCH) as c:
                for t in range(NT):
                    sp.wait_ge(t_y, NT * c + (t + 1))
                    sp.dma_start(x_res[:, t % 3, :], rows_of(x_p, x_s, t, c)).then_inc(t_x[t % 3], 16)

        @block.scalar
        def _(act):
            act.sem_inc(t_wfree, 4)
            act.sem_inc(t_mlo, 3)

            def split(c):
                for q in range(4):
                    act.wait_ge(t_w[q], 16 * c + 16)
                    act.wait_ge(t_wfree, 4 * c + (q + 1))
                    act.activation(w_hi[:, 4 * q:4 * q + 4, :], w_raw[:, 4 * q:4 * q + 4, :], ACT.Copy)\
                       .then_inc(t_whi, 1)

            def store(c, t):
                act.wait_ge(t_y, NT * c + (t + 4))
                act.dma_start(rows_of(y_p, y_s, t, c), y_sb[:, t % 3, :]).then_inc(t_st[t % 3], 16)

            split(0)
            with act.Fori(0, KT) as k:
                for n in range(NG):
                    act.wait_ge(t_mul, NG * k + (n + 1))
                    act.activation(m_hi[:, ds(k, 1), n * TN:n * TN + TN].rearrange("p a n -> p (a n)"),
                                   parts[:, n, 0, :], ACT.Copy).then_inc(t_mhi, 1)
            with act.Fori(0, NCH - 1) as c:
                load_w(act, c + 1)
                for t in range(NT - 1):
                    store(c, t)
                split(c + 1)
                store(c, NT - 1)
            for t in range(NT):
                store(NCH - 1, t)
            for i in range(3):
                act.wait_ge(t_st[i], 16 * NCH * NT // 3)

        @block.tensor
        def _(pe):
            pe.wait_ge(t_mlo, NG * KT + 3)
            with pe.Fori(0, NCH) as c:
                for t in range(NT):
                    pe.wait_ge(t_y, NT * c + (t + 1))
                    out = acc[t % 3][:, 0:WCH]
                    tok = slice(t * P, t * P + P)
                    for k in range(KT):
                        if t == 0 and k % 4 == 0:
                            pe.wait_ge(t_wready, 4 * c + (k // 4 + 5))
                        pe.matmul(out, m_lo[:, k, tok], w_hi[:, k, :], start=(k == 0), stop=False)
                        pe.matmul(out, m_hi[:, k, tok], w_lo[:, k, :], start=False, stop=False)
                        mm = pe.matmul(out, m_hi[:, k, tok], w_hi[:, k, :], start=False, stop=(k == KT - 1))
                        if t == NT - 1 and k % 4 == 3:
                            mm.then_inc(t_wfree, 1)
                    if t < NT - 1:
                        mm.then_inc(t_acc, 1)

        @block.vector
        def _(dve):
            dve.sem_inc(t_y, 3)
            dve.sem_inc(t_wready, 4)

            def split(c):
                for q in range(4):
                    dve.wait_ge(t_whi, 4 * c + (q + 1))
                    dve.tensor_tensor(w_lo[:, 4 * q:4 * q + 4, :], w_raw[:, 4 * q:4 * q + 4, :],
                                      w_hi[:, 4 * q:4 * q + 4, :].bitcast(F32), ALU.subtract).then_inc(t_wready, 1)

            split(0)

            def multiply(k, n):
                dve.wait_ge(t_part[n], 32 * k + 32)
                dve.tensor_tensor(parts[:, n, 0, :], parts[:, n, 0, :], parts[:, n, 1, :], ALU.mult)\
                   .then_inc(t_mul, 1)

            def low(k, n):
                dve.wait_ge(t_mhi, NG * k + (n + 1))
                m = (slice(None), ds(k, 1), slice(n * TN, n * TN + TN))
                dve.tensor_tensor(m_lo[m].rearrange("p a n -> p (a n)"), parts[:, n, 0, :],
                                  m_hi[m].rearrange("p a n -> p (a n)").bitcast(F32), ALU.subtract)\
                   .then_inc(t_mlo, 1)

            with dve.Fori(0, KT) as k:
                multiply(k, 0)
                multiply(k, 1)
                low(k, 0)
                multiply(k, 2)
                low(k, 1)
                low(k, 2)

            def add(c, t, first=False):
                if t == NT - 1:
                    dve.wait_ge(t_wfree, 4 * c + 8)
                else:
                    dve.wait_ge(t_acc, (NT - 1) * c + (t + 1))
                dve.wait_ge(t_x[t % 3], 48 * c + (16 * (t // 3) + 16))
                if not (first and t < 3):
                    dve.wait_ge(t_st[t % 3], 48 * c + 16 * (t // 3))
                dve.tensor_tensor(y_sb[:, t % 3, :], acc[t % 3][:, 0:WCH], x_res[:, t % 3, :], ALU.add)\
                   .then_inc(t_y, 1)

            for t in range(NT):
                if t == NT - 1:
                    split(1)
                add(0, t, True)
            with dve.Fori(1, NCH - 1) as c:
                for t in range(NT):
                    if t == NT - 1:
                        split(c + 1)
                    add(c, t)
            for t in range(NT):
                add(NCH - 1, t)


def hybrid_step(nc, x_p, x_s, cache_k, cache_v, state, norm_g, w_in, w_up, b_gate, qg, kg, sinks, gla_g, w_out,
                consts, tables, y_p, y_s, win_kp, win_vp, gla_p, win_ks, win_vs, gla_s):
    flat = "a b t g d -> (a b) t (g d)"
    h_t = nc.dram_tensor("h_t", [IN_TOTAL, PAD + TOK], F32, kind="Internal").ap()
    o_t = nc.dram_tensor("o_t", [D_MODEL, TOK], F32, kind="Internal").ap()
    x_p = x_p.rearrange("a t d -> (a t) d")
    x_s = x_s.rearrange("b t d -> (b t) d")
    with ExitStack() as ctx:
        def sem(name):
            return ctx.enter_context(nc.semaphore(name))

        project_in(nc, sem, (x_p, x_s, cache_k.rearrange(flat), cache_v.rearrange(flat), state[0], norm_g,
                             w_in[0], w_up, b_gate, qg, kg, sinks, gla_g, consts, tables,
                             win_kp.rearrange(flat)[0], win_vp.rearrange(flat)[0], gla_p[0, 0],
                             win_ks.rearrange(flat), win_vs.rearrange(flat), gla_s[0], h_t, o_t))
        project_out(nc, sem, (x_p, x_s, w_out[0], h_t, o_t, y_p.rearrange("a t d -> (a t) d"),
                              y_s.rearrange("b t d -> (b t) d")))


def shape_constants():
    import numpy as np

    c = np.zeros((P, C_ALL), np.float32)
    c[:, C_IDENT:C_IDENT + P] = np.eye(P)
    c[:, C_PAIR:C_PAIR + P] = np.kron(np.eye(2), np.ones((HEAD_DIM, HEAD_DIM)))
    c[:, C_SEQ:C_SEQ + DEC_BATCH] = np.kron(np.eye(DEC_BATCH), np.ones((DEC_SEQ, 1)))
    mask = np.zeros((P, 2 * P), np.float32)
    mask[:CHUNK, 3 * CHUNK:] = MASKED
    mask[CHUNK:, :CHUNK] = MASKED
    c[:, C_MASK:] = mask
    mask = mask.copy()
    mask[:, :P] = MASKED
    c[:, C_MASK0:C_MASK] = mask
    m = np.zeros((P, M_ALL), np.float32)
    for i, s in enumerate(LEVELS):
        n = P // (2 * s)
        pairs = np.kron(np.eye(n), np.concatenate([np.ones((s, s)), np.zeros((s, s))]))
        m[:, i * 256:i * 256 + 256] = np.tile(pairs, (1, N_GLA))
    m[:, M_DIAG:M_SCAN] = np.tile(np.eye(P), (1, N_GLA))
    m[:, M_SCAN:M_SCAN_DEC] = np.arange(4 * P) % P > 0
    m[:, M_SCAN_DEC:] = np.arange(4 * P) % DEC_SEQ > 0
    return c, m


_INS = ["x_prompt", "x_sample", "cache_k", "cache_v", "state_gla", "norm_g", "w_in", "w_gate_up", "b_gate",
        "q_norm_g", "k_norm_g", "sinks", "gla_norm_g", "w_out"]
_OUTS = [(1, SEQ, D_MODEL), (DEC_BATCH, DEC_SEQ, D_MODEL),
         (1, 1, CACHE, N_KV, HEAD_DIM), (1, 1, CACHE, N_KV, HEAD_DIM), (1, 1, N_GLA, DK, DV),
         (1, DEC_BATCH, CACHE, N_KV, HEAD_DIM), (1, DEC_BATCH, CACHE, N_KV, HEAD_DIM),
         (1, DEC_BATCH, N_GLA, DK, DV)]


def kernel(**inputs):
    import numpy as _np
    import concourse.bacc as _bacc
    from concourse import mybir as _mybir
    from concourse.bass_utils import run_bass_kernel_spmd as _run

    nc = _bacc.Bacc("TRN2", target_bir_lowering=False, num_devices=1, dynamic_dma_scratch_size=1024)
    consts, tables = shape_constants()
    arrays, args = {}, []
    for name in _INS + ["consts", "tables"]:
        a = consts if name == "consts" else tables if name == "tables" else _np.ascontiguousarray(inputs[name])
        arrays[f"in_{name}"] = a
        args.append(nc.dram_tensor(f"in_{name}", a.shape, _mybir.dt.from_np(a.dtype), kind="ExternalInput").ap())
    for i, shape in enumerate(_OUTS):
        args.append(nc.dram_tensor(f"out_{i}", shape, F32, kind="ExternalOutput").ap())
    hybrid_step(nc, *args)
    r = _run(nc, [arrays], core_ids=[0])
    return tuple(r.results[0][f"out_{i}"] for i in range(len(_OUTS)))
```

```python
from contextlib import ExitStack

import concourse.bass as bass
from concourse import mybir

P = 128
D_MODEL = 2048
SEQ = 1024
DEC_BATCH = 8
DEC_SEQ = 16
CACHE = 128
HEAD_DIM = 64
N_HEADS = 16
N_KV = 4
GQA = N_HEADS // N_KV
N_GLA = 4
DK = 128
DV = 256
RANK = 16
TAU = 16.0
EPS = 1e-6
CHUNK = 64

TOK = SEQ + DEC_BATCH * DEC_SEQ
NT = TOK // P
NTP = SEQ // P
KT = D_MODEL // P
TN = 384
NG = TOK // TN
PAD = P

Q0, K0, V0, GA0, GQ0, GK0, GV0, GG0, LR0 = 0, 1024, 1280, 1536, 2560, 3072, 3584, 4608, 5632
IN_TOTAL = LR0 + RANK

N_QK = (V0 - Q0) // P
N_PLAIN = (GA0 - Q0 + GG0 - GQ0) // P
N_ITEMS = (IN_TOTAL - RANK) // P
J_ATT = 1 + (GA0 - Q0) // P
J_DEC = J_ATT + NTP
J_GLA = 1 + N_PLAIN
J_LEV = J_GLA + NTP
WCH = 256
NCH = D_MODEL // WCH
LEVELS = (64, 32, 16, 8, 4, 2, 1)
DEC_LEVELS = (8, 4, 2, 1)

F32 = mybir.dt.float32
F32R = mybir.dt.float32r
U8 = mybir.dt.uint8
ALU = mybir.AluOpType
ACT = mybir.ActivationFunctionType
AX = mybir.AxisListType
ds = bass.ds


C_IDENT, C_PAIR, C_SEQ, C_MASK0 = 0, P, 2 * P, 2 * P + DEC_BATCH
C_MASK = C_MASK0 + 2 * P
C_ALL = C_MASK + 2 * P
M_DIAG = len(LEVELS) * 256
M_SCAN = M_DIAG + 4 * P
M_SCAN_DEC = M_SCAN + 4 * P
M_ALL = M_SCAN_DEC + 4 * P
MASKED = -1.0e30


def project_in(nc, sem, dram):
    (x_p, x_s, cache_k, cache_v, state, norm_g, w_in, w_up, b_gate, qg, kg, sinks, gla_g, consts, tables,
     win_kp, win_vp, gla_p, win_ks, win_vs, gla_s, h_t, o_t) = dram
    with ExitStack() as ctx:
        def sb(name, shape, dt=F32):
            return ctx.enter_context(nc.sbuf_tensor(name, shape, dt))

        x_hi = sb("x_hi", [P, KT, TOK], F32R)
        x_lo = sb("x_lo", [P, KT, TOK], F32R)
        raw = sb("raw", [P, D_MODEL])
        w_hi = sb("w_hi", [P, KT, P], F32R)
        w_lo = sb("w_lo", [P, KT, P], F32R)
        xn = sb("xn", [P, D_MODEL])
        work = sb("work", [P, 9216])
        consts_sb = sb("consts_sb", [P, C_MASK0])
        tables_sb = sb("tables_sb", [P, M_ALL], U8)
        w_up_sb = sb("w_up_sb", [RANK + 1, N_GLA * DK])
        lr = sb("lr", [RANK + 1, P])
        sink_row = sb("sink_row", [P, N_HEADS])
        sink_dec = sb("sink_dec", [P, 2])
        gq_col = sb("gq_col", [P, 2])
        gn_col = sb("gn_col", [P, 2])
        small = sb("small", [P, 96])
        mhalf = sb("mhalf", [P, 1])
        zeros = sb("zeros", [P, P])
        ident = consts_sb[:, C_IDENT:C_IDENT + P]
        ones_pair = consts_sb[:, C_PAIR:C_PAIR + P]
        seq_col = consts_sb[:, C_SEQ:C_SEQ + DEC_BATCH]
        x_buf = [work[:, 0:D_MODEL], raw[:, :], xn[:, :]]
        g_row = work[:, D_MODEL:2 * D_MODEL]
        squares = work[:, 2 * D_MODEL:3 * D_MODEL]
        lr_raw = work[:, 4 * D_MODEL:4 * D_MODEL + KT * RANK].rearrange("p (k n) -> p k n", n=RANK)
        ss, var, rstd = small[:, 0:2], small[:, 2:3], small[:, 3:4]
        stage = [xn[:, TN * n:TN * n + TN] for n in range(3)]
        tmp_a = xn[:, 3 * TN:4 * TN]
        tmp_b = xn[:, 4 * TN:5 * TN]

        banks = [ctx.enter_context(nc.psum_tensor(f"p1_{i}", [P, 512], F32)) for i in range(8)]
        acc = banks[0:3]
        xt_bank = banks[3:7]
        ss_bank = banks[7]
        ub = banks[3:8]

        s_const = sem("s_const")
        s_x = [sem(f"s_x{i}") for i in range(3)]
        s_w = [sem(f"s_w{i}") for i in range(4)]
        s_ss = sem("s_ss")
        s_var = sem("s_var")
        s_rstd = sem("s_rstd")
        s_xn = sem("s_xn")
        s_xt = sem("s_xt")
        s_xhi = sem("s_xhi")
        s_xlo = sem("s_xlo")
        s_mh = sem("s_mh")
        s_whi = sem("s_whi")
        s_wready = sem("s_wready")
        s_wfree = sem("s_wfree")
        s_acc = sem("s_acc")
        s_staged = sem("s_staged")
        s_store = [sem(f"s_store{i}") for i in range(3)]
        s_sq = sem("s_sq")
        s_ssq = sem("s_ssq")
        s_v = sem("s_v")
        s_sd = sem("s_sd")
        s_nchain = sem("s_nchain")
        s_sig = sem("s_sig")
        s_schain = sem("s_schain")
        s_zero = sem("s_zero")
        s_zst = sem("s_zst")
        s_tab = sem("s_tab")
        s_win = sem("s_win")
        s_tload = sem("s_tload")
        s_tables = sem("s_tables")
        sa_dv = sem("sa_dv")
        sa_e = sem("sa_e")
        sa_k = sem("sa_k")
        sa_mask = sem("sa_mask")
        sa_max = sem("sa_max")
        sa_mk = sem("sa_mk")
        sa_neg = sem("sa_neg")
        sa_o = sem("sa_o")
        sa_out = sem("sa_out")
        sa_p = sem("sa_p")
        sa_pt = sem("sa_pt")
        sa_q = sem("sa_q")
        sa_s = sem("sa_s")
        sa_st = sem("sa_st")
        sa_t = sem("sa_t")
        sa_v = sem("sa_v")
        sa_vtok = sem("sa_vtok")
        sa_vtr = sem("sa_vtr")
        sb_av = sem("sb_av")
        sb_ck = sem("sb_ck")
        sb_cv = sem("sb_cv")
        sb_dv = sem("sb_dv")
        sb_e = sem("sb_e")
        sb_in = sem("sb_in")
        sb_ks = sem("sb_ks")
        sb_kt = sem("sb_kt")
        sb_neg = sem("sb_neg")
        sb_new = sem("sb_new")
        sb_oc = sem("sb_oc")
        sb_pc = sem("sb_pc")
        sb_pr = sem("sb_pr")
        sb_pt = sem("sb_pt")
        sb_s = sem("sb_s")
        sb_w = sem("sb_w")
        sb_xc = sem("sb_xc")
        sb_xt = sem("sb_xt")
        sd_ds = sem("sd_ds")
        sd_gp = sem("sd_gp")
        sd_in = [sem(f"sd_in{i}") for i in range(2)]
        sd_k = sem("sd_k")
        sd_o = sem("sd_o")
        sd_out = [sem(f"sd_out{i}") for i in range(2)]
        sd_q = sem("sd_q")
        sd_up = sem("sd_up")
        sl_a = sem("sl_a")
        sl_b = sem("sl_b")
        sl_cp = sem("sl_cp")
        sl_d = sem("sl_d")
        sl_dcp = sem("sl_dcp")
        sl_dg = sem("sl_dg")
        sl_ds = sem("sl_ds")
        sl_eb = sem("sl_eb")
        sl_ex = sem("sl_ex")
        sl_gt = sem("sl_gt")
        sl_ini = sem("sl_ini")
        sl_k = sem("sl_k")
        sl_kt = sem("sl_kt")
        sl_ktok = sem("sl_ktok")
        sl_la = sem("sl_la")
        sl_lnv = sem("sl_lnv")
        sl_log = sem("sl_log")
        sl_lr = sem("sl_lr")
        sl_nt = sem("sl_nt")
        sl_o = sem("sl_o")
        sl_og = sem("sl_og")
        sl_on = sem("sl_on")
        sl_p = sem("sl_p")
        sl_q = sem("sl_q")
        sl_rs = sem("sl_rs")
        sl_sq = sem("sl_sq")
        sl_st = sem("sl_st")
        sl_up = sem("sl_up")
        sl_v = sem("sl_v")
        sl_var = sem("sl_var")
        sl_vtok = sem("sl_vtok")
        sl_vtr = sem("sl_vtr")
        sl_zz = sem("sl_zz")
        block = ctx.enter_context(nc.Block())
        w_v = w_in.rearrange("(k p) n -> p k n", p=P)

        def w_raw(k, n):
            if n == RANK:
                return lr_raw[:, k:k + 4, :]
            return raw[:, k * P:k * P + 4 * P].rearrange("p (k n) -> p k n", k=4)

        RUNS = [(1, J_ATT, Q0), (J_ATT, J_GLA, GQ0), (J_GLA, J_LEV, GA0), (J_LEV, 1 + N_ITEMS, GG0)]

        @block.sync
        def _(sp):
            def load_x(t):
                if t >= 3:
                    sp.wait_ge(s_xt, 4 * (t - 2) + 4)
                sp.dma_start(x_buf[t % 3], x_p[t * P:t * P + P, :] if t < NTP else x_s).then_inc(s_x[t % 3], 16)

            load_x(0)
            sp.dma_start(g_row, norm_g[0:1, :].to_broadcast([P, D_MODEL])).then_inc(s_const, 16)
            sp.dma_start(consts_sb[:, :], consts[:, 0:C_MASK0]).then_inc(s_const, 16)
            load_x(1)
            load_x(2)
            for half in range(2):
                rows = slice(half * HEAD_DIM, half * HEAD_DIM + HEAD_DIM)
                sp.dma_start(gq_col[rows, 0:1], qg.rearrange("a d -> d a")).then_inc(s_const, 16)
                sp.dma_start(gq_col[rows, 1:2], kg.rearrange("a d -> d a")).then_inc(s_const, 16)
            for q in range(4):
                sp.dma_start(w_raw(4 * q, RANK), w_v[:, 4 * q:4 * q + 4, LR0:LR0 + RANK]).then_inc(s_w[q], 16)
            for t in range(3, NT):
                load_x(t)
            sp.dma_start(w_up_sb[0:RANK, :], w_up[0]).then_inc(s_tab, 16)
            sp.dma_start(w_up_sb[RANK:RANK + 1, :], b_gate).then_inc(s_tab, 16)
            for e in range(2):
                sp.dma_start(gn_col[:, e:e + 1], gla_g[:, e * P:e * P + P].rearrange("a p -> p a")).then_inc(s_tab, 16)
            sp.dma_start(sink_row[:, :], sinks.to_broadcast([P, N_HEADS])).then_inc(s_tab, 16)
            for half in range(2):
                for gp in range(2):
                    for r in range(GQA):
                        rows = slice(half * HEAD_DIM + r * DEC_SEQ, half * HEAD_DIM + r * DEC_SEQ + DEC_SEQ)
                        h = (2 * gp + half) * GQA + r
                        sp.dma_start(sink_dec[rows, gp:gp + 1],
                                     sinks[0:1, h:h + 1].to_broadcast([DEC_SEQ, 1])).then_inc(s_tab, 16)

            def load_w(j, col, n):
                for q in range(4):
                    if type(j) is int and j == 1:
                        sp.wait_ge(s_xt, 4 * NTP + 4)
                    else:
                        sp.wait_ge(s_wready, 4 * j + (q - 3))
                    sp.dma_start(w_raw(4 * q, n), w_v[:, 4 * q:4 * q + 4, ds(col, n)]).then_inc(s_w[q], 16)

            def store_item(j, row, n_rows):
                for n in range(NG):
                    sp.wait_ge(s_staged, j * NG + (n + 4))
                    sp.dma_start(h_t[ds(row, n_rows), PAD + n * TN:PAD + n * TN + TN],
                                 stage[n][0:n_rows, :]).then_inc(s_store[n], 16)

            load_w(1, Q0, P)
            sp.wait_ge(s_ss, NT)
            sp.dma_start(work[:, 2 * D_MODEL:2 * D_MODEL + M_ALL], tables).then_inc(s_tload, 16)
            sp.wait_ge(s_zero, 1)
            for r in range(K0 // P, GA0 // P):
                sp.dma_start(h_t[r * P:r * P + P, 0:PAD], xn[:, 5 * TN:5 * TN + PAD]).then_inc(s_zst, 16)
            store_item(0, LR0, RANK)
            for i, (j0, j1, col) in enumerate(RUNS):
                with sp.Fori(j0, j1 - 1) as j:
                    load_w(j + 1, (j - j0) * P + (col + P), P)
                    store_item(j, (j - j0) * P + col, P)
                if i + 1 < len(RUNS):
                    load_w(j1, RUNS[i + 1][2], P)
                store_item(j1 - 1, (j1 - 1 - j0) * P + col, P)
            sp.wait_ge(s_zst, 16 * (GA0 - K0) // P)
            old = CACHE - DEC_SEQ
            sp.dma_start(win_ks[:, 0:old, :], cache_k[:, DEC_SEQ:CACHE, :]).then_inc(s_win, 16)
            sp.dma_start(win_vs[:, 0:old, :], cache_v[:, DEC_SEQ:CACHE, :]).then_inc(s_win, 16)
            sp.wait_ge(s_win, 32)
            for n in range(NG):
                sp.wait_ge(s_store[n], 16 * (N_ITEMS + 1))

        def wait_acc(eng, j, n):
            if n == NG - 1:
                eng.wait_ge(s_wfree, 4 * j + 8)
            else:
                eng.wait_ge(s_acc, 2 * j + (n + 1))

        def split(pool, j, n=P):
            for k in range(0, KT, 4):
                pool.wait_ge(s_w[k // 4], 16 * j + 16)
                pool.wait_ge(s_wfree, 4 * j + (k // 4 + 1))
                pool.tensor_tensor(w_hi[:, k:k + 4, 0:n], w_raw(k, n), zeros[:, 0:n].unsqueeze(1)
                                   .to_broadcast([P, 4, n]), ALU.add).then_inc(s_whi, 1)
                pool.wait_ge(s_whi, 4 * j + (k // 4 + 1))
                pool.tensor_tensor(w_lo[:, k:k + 4, 0:n], w_raw(k, n), w_hi[:, k:k + 4, 0:n].bitcast(F32),
                                   ALU.subtract).then_inc(s_wready, 1)

        a_q = work[:, 0:1024].rearrange("p (c n) -> p c n", c=8)
        a_k = work[:, 1024:2048].rearrange("p (g n) -> p g n", g=N_KV)
        a_v = work[:, 2048:2560].rearrange("p (c n) -> p c n", c=2)
        a_vtok = work[:, 2560:3072].rearrange("p (k n) -> p k n", k=2)
        a_p = work[:, 3072:4096].rearrange("p (r n) -> p r n", r=GQA)
        a_pt = work[:, 4096:5120].rearrange("p (k n) -> p k n", k=2)
        a_o = work[0:HEAD_DIM, 5120:5632]
        a_mask = work[:, 5632:6144].rearrange("p (m n) -> p m n", m=2)
        a_mx, a_neg, a_sk, a_es, a_sum, a_den = (small[:, 8 + 4 * i:12 + 4 * i] for i in range(6))
        bank_s, bank_t, bank_o = ub[0:2], ub[2:4], ub[4]

        def attend_pe(pe, t):
            def values():
                pe.wait_ge(sa_v, 16 * t + 16)
                for kt in range(2):
                    for c in range(2):
                        mm = pe.transpose(bank_t[0][:, kt * 256 + c * P:kt * 256 + c * P + P],
                                          a_v[:, c, kt * P:kt * P + P], ident)
                mm.then_inc(sa_vtr, 1)

            def scores(g):
                pe.wait_ge(sa_q, 16 * t + 16)
                pe.wait_ge(sa_k, 32 * t + 32)
                pe.wait_ge(sa_max, 16 * t + (4 * g + 1))
                for half in range(2):
                    rows = slice(half * HEAD_DIM, half * HEAD_DIM + HEAD_DIM)
                    for i in range(2):
                        mm = pe.matmul(bank_s[half][:, i * 256:i * 256 + 256],
                                       a_q[rows, 2 * g + i, :], a_k[rows, g, :], start=True, stop=True)
                    mm.then_inc(sa_s, 1)

            def turn(g):
                pe.wait_ge(sa_p, 16 * t + (4 * g + 4))
                pe.wait_ge(sa_pt, 8 * t + (2 * g + 1))
                pe.wait_ge(sa_vtok, t + 1)
                for kt in range(2):
                    for r in range(GQA):
                        mm = pe.transpose(bank_t[kt][:, r * P:r * P + P], a_p[:, r, kt * P:kt * P + P], ident)
                    mm.then_inc(sa_t, 1)

            def outputs(g):
                pe.wait_ge(sa_pt, 8 * t + (2 * g + 3))
                pe.wait_ge(sa_out, 4 * t + (g + 1))
                for kt in range(2):
                    mm = pe.matmul(bank_o[0:HEAD_DIM, :], a_vtok[:, kt, g * HEAD_DIM:g * HEAD_DIM + HEAD_DIM],
                                   a_pt[:, kt, :], start=(kt == 0), stop=(kt == 1))
                mm.then_inc(sa_o, 1)

            def at(*stages):
                return lambda: [f(*a) for f, *a in stages]

            return {4: at((values,), (scores, 0)), 12: at((turn, 0), (scores, 1)), 14: at((outputs, 0)),
                    21: at((turn, 1), (scores, 2)), 23: at((outputs, 1)),
                    30: at((turn, 2), (scores, 3)), 32: at((outputs, 2)),
                    39: at((turn, 3)), 41: at((outputs, 3))}

        class attend_act:

            def __init__(self, act):
                self.act = act

            def load(self, t):
                act = self.act
                act.dma_start(a_q, h_t[Q0:K0, ds(t * P + PAD, P)].rearrange("(c p) n -> p c n", p=P))\
                   .then_inc(sa_q, 16)
                for half in range(2):
                    act.dma_start(a_k[half * HEAD_DIM:half * HEAD_DIM + HEAD_DIM, :, :],
                                  h_t[K0:V0, ds(t * P, 2 * P)].rearrange("(g p) n -> p g n", p=HEAD_DIM))\
                       .then_inc(sa_k, 16)
                act.dma_start(a_v, h_t[V0:GA0, ds(t * P, 2 * P)].rearrange("(c p) n -> p c n", p=P))\
                   .then_inc(sa_v, 16)

            def first(self):
                self.act.sem_inc(sa_pt, 1)
                self.act.sem_inc(sa_out, 1)
                self.act.dma_start(a_mask, consts[:, C_MASK0:C_ALL].rearrange("p (m n) -> p m n", m=2))\
                    .then_inc(sa_mask, 16)
                self.act.dma_start(a_o[:, 0:2], consts[0:HEAD_DIM, 0:2]).then_inc(sa_st, 16)
                for n in range(NG):
                    self.act.wait_ge(s_store[n], 16 * J_ATT)
                self.act.wait_ge(s_zst, 16 * (GA0 - K0) // P)
                self.load(0)

            def exps(self, t, g):
                act = self.act
                act.wait_ge(sa_neg, 4 * t + (g + 1))
                act.activation(a_es, a_sk, ACT.Exp).then_inc(sa_e, 1)
                for r in range(GQA):
                    act.activation(a_p[:, r, :], a_p[:, r, :], ACT.Exp, bias=a_neg[:, r:r + 1],
                                   accum_out=a_sum[:, r:r + 1]).then_inc(sa_e, 1)

            def copy_probs(self, t, g):
                for kt in range(2):
                    self.act.wait_ge(sa_t, 8 * t + (2 * g + kt + 1))
                    self.act.activation(a_pt[:, kt, :], bank_t[kt][:, :], ACT.Copy).then_inc(sa_pt, 1)

            def copy_out(self, t, g):
                act = self.act
                act.wait_ge(sa_o, 4 * t + (g + 1))
                act.wait_ge(sa_st, 64 * t + 16 * (g + 1))
                act.activation(a_o, bank_o[0:HEAD_DIM, :], ACT.Copy).then_inc(sa_out, 1)
                act.wait_ge(sa_out, 4 * t + (g + 2))
                act.dma_start(o_t[g * 256:g * 256 + 256, ds(t * P, P)].rearrange("(r d) n -> d r n", d=HEAD_DIM),
                              a_o.rearrange("p (r n) -> p r n", r=GQA)).then_inc(sa_st, 16)

            def tile(self, t):
                def part_0():
                    self.act.wait_ge(sa_vtr, t + 1)
                    self.act.activation(a_vtok, bank_t[0][:, :].rearrange("p (k n) -> p k n", k=2), ACT.Copy)\
                        .then_inc(sa_vtok, 1)
                    self.exps(t, 0)
                    self.copy_probs(t, 0)
                    self.exps(t, 1)

                def part_1():
                    self.copy_out(t, 0)
                    self.copy_probs(t, 1)
                    self.exps(t, 2)
                    self.copy_out(t, 1)
                    self.copy_probs(t, 2)
                    self.exps(t, 3)

                def part_2():
                    self.copy_out(t, 2)
                    self.copy_probs(t, 3)
                    if not (type(t) is int and t == NTP - 1):
                        self.load(t + 1)
                    self.copy_out(t, 3)
                return part_0, part_1, part_2

        class attend_dve:

            def __init__(self, dve):
                self.dve = dve

            def first(self):
                self.dve.sem_inc(sa_max, 1)
                self.dve.sem_inc(sa_mk, 1)
                self.dve.wait_ge(sa_mask, 16)

            def softmax(self, t, g):
                dve = self.dve
                dve.wait_ge(sa_mk, t + 1)
                dve.wait_ge(sa_pt, 8 * t + (2 * g + 1))
                for r in (0, 2, 1, 3):
                    h = GQA * g + r
                    if r < 2:
                        dve.wait_ge(sa_s, 8 * t + (2 * g + r + 1))
                        dve.nop(nofuse=True)
                    dve.tensor_tensor_reduce(
                        out=a_p[:, r, :], in0=bank_s[r % 2][:, (r // 2) * 256:(r // 2) * 256 + 256],
                        in1=a_mask[:, 0, :], scale=1.0, scalar=sink_row[:, h:h + 1], op0=ALU.add, op1=ALU.max,
                        accum_out=a_mx[:, r:r + 1]).then_inc(sa_max, 1)
                dve.wait_ge(sa_max, 16 * t + (4 * g + 5))
                dve.tensor_scalar(a_neg, a_mx, -1.0, None, ALU.mult).then_inc(sa_dv, 1)
                dve.wait_ge(sa_dv, 12 * t + (3 * g + 1))
                dve.tensor_tensor(a_sk, sink_row[:, GQA * g:GQA * g + GQA], a_neg, ALU.add).then_inc(sa_neg, 1)
                dve.wait_ge(sa_e, 20 * t + (5 * g + 5))
                dve.tensor_tensor(a_den, a_sum, a_es, ALU.add).then_inc(sa_dv, 1)
                dve.wait_ge(sa_dv, 12 * t + (3 * g + 2))
                dve.reciprocal(a_den, a_den).then_inc(sa_dv, 1)
                dve.wait_ge(sa_dv, 12 * t + (3 * g + 3))
                for r in range(GQA):
                    dve.tensor_scalar(a_p[:, r, :], a_p[:, r, :], a_den[:, r:r + 1], None, ALU.mult)\
                       .then_inc(sa_p, 1)

            def tile(self, t):
                def part_0():
                    self.softmax(t, 0)
                    self.softmax(t, 1)

                def part_1():
                    self.softmax(t, 2)
                    self.softmax(t, 3)

                def part_2():
                    self.dve.tensor_copy(a_mask[:, 0, :], a_mask[:, 1, :]).then_inc(sa_mk, 1)
                return part_0, part_1, part_2

        def four(x):
            return x.rearrange("p (h n) -> p h n", h=N_GLA)

        l_q, l_k = work[:, 0:512], work[:, 512:1024]
        l_v = work[:, 1024:2048]
        l_vtok = work[:, 2048:3072]
        l_b = work[:, 3072:3584]
        l_e = [work[:, 3584:4096], work[:, 4096:4608]]
        l_z = [work[:, 4608:5120], work[:, 5120:5632]]
        l_att = work[:, 5632:6144]
        l_qe = work[:, 6144:6656]
        l_ktok = work[:, 6656:7168]
        l_s = work[:, 7168:8192]
        l_og = work[:, 8192:9216]
        l_o = l_v
        l_eb = small[:, 40:72]
        l_ss, l_var, l_rstd = small[:, 76:80], small[:, 80:84], small[:, 84:88]
        NZ = 2 + len(LEVELS)

        def halves(x, s):
            return x.rearrange("p (n two s) -> p n two s", two=2, s=s)

        def linear_stages(pe, t, dec=False):
            levels = DEC_LEVELS if dec else LEVELS

            def logits():
                pe.wait_ge(sl_lr, 16 * t + 16)
                pe.wait_ge(sl_up, 4 * t + 1)
                for h in range(N_GLA):
                    mm = pe.matmul(ub[0][:, h * P:h * P + P], w_up_sb[:, h * P:h * P + P], lr[:, :],
                                   start=True, stop=True)
                mm.then_inc(sl_log, 1)

            def values():
                pe.wait_ge(sl_v, 16 * t + 16)
                pe.wait_ge(sl_on, 4 * t + 1)
                for c in range(8):
                    mm = pe.transpose(ub[1 + c // 4][:, (c % 4) * P:(c % 4) * P + P], l_v[:, c * P:c * P + P], ident)
                    if c % 4 == 3:
                        mm.then_inc(sl_vtr, 1)

            def diagonal():
                pe.wait_ge(sl_q, 16 * t + 16)
                pe.wait_ge(sl_k, 16 * t + 16)
                pe.wait_ge(sl_la, t + 1)
                for h in range(N_GLA):
                    hs = slice(h * P, h * P + P)
                    mm = pe.matmul(ub[0][:, hs], l_k[:, hs], l_q[:, hs], start=True, stop=True)
                mm.then_inc(sl_dg, 1)

            def keys():
                pe.wait_ge(sl_zz, NZ * t + 2)
                pe.wait_ge(sl_og, 4 * t + 1)
                for h in range(N_GLA):
                    mm = pe.transpose(ub[3][:, h * P:h * P + P], l_z[0][:, h * P:h * P + P], ident)
                mm.then_inc(sl_kt, 1)

            def level(i):
                s = levels[i]
                pe.wait_ge(sl_zz, NZ * t + (i + 3))
                if i == 1:
                    pe.wait_ge(sl_ktok, t + 1)
                if i >= 2:
                    pe.wait_ge(sl_cp, len(LEVELS) * t + (i - 1))
                for h in range(N_GLA):
                    z = l_z[(i + 1) % 2][:, h * P:h * P + P]
                    mm = pe.matmul(ub[4 - i % 2][:, h * 64:h * 64 + 64], z, halves(z, s)[:, :, 1, :],
                                   start=True, stop=True)
                mm.then_inc(sl_p, 1)

            def outputs():
                pe.wait_ge(sl_cp, len(LEVELS) * t + len(levels))
                pe.wait_ge(sl_dcp, t + 1)
                pe.wait_ge(sl_vtok, 2 * t + 2)
                for h in range(N_GLA):
                    hs = slice(h * P, h * P + P)
                    out = ub[1 + h // 2][:, (h % 2) * DV:(h % 2) * DV + DV]
                    pe.matmul(out, l_att[:, hs], l_vtok[:, h * DV:h * DV + DV], start=True, stop=False)
                    mm = pe.matmul(out, l_qe[:, hs], l_s[:, h * DV:h * DV + DV], start=False, stop=True)
                    if h % 2:
                        mm.then_inc(sl_o, 1)
                pe.wait_ge(sl_ktok, t + 1)
                for h in range(N_GLA):
                    hs = slice(h * P, h * P + P)
                    mm = pe.matmul(ub[4 * (h // 2)][:, (h % 2) * DV:(h % 2) * DV + DV], l_ktok[:, hs],
                                   l_vtok[:, h * DV:h * DV + DV], start=True, stop=True)
                    if h % 2:
                        mm.then_inc(sl_ds, 1)

            def turn(decoded=False):
                if not decoded:
                    pe.wait_ge(sl_up, 4 * t + 5)
                for c in range(8):
                    if c % 2 == 0:
                        pe.wait_ge(sl_on, 4 * t + (c // 2 + 2))
                    mm = pe.transpose(ub[3 + c // 4][:, (c % 4) * P:(c % 4) * P + P], l_o[:, c * P:c * P + P], ident)
                    if c % 4 == 3:
                        mm.then_inc(sl_gt, 1)
            return logits, values, diagonal, keys, level, outputs, turn

        def linear_pe(pe, t, first=False):
            logits, values, diagonal, keys, level, outputs, _ = linear_stages(pe, t)
            stages = {3: logits, 11: diagonal, 18: keys, 28: values, 45: outputs}
            if not first:
                stages[6] = linear_stages(pe, t - 1)[-1]
            for i, step in enumerate((19, 21, 24, 27, 30, 33, 36)):
                stages[step] = lambda i=i: level(i)
            return stages

        class linear_act:
            def __init__(self, act):
                self.act = act

            def load(self, t):
                act = self.act
                cols = ds(t * P + PAD, P)
                act.dma_start(lr[0:RANK, :], h_t[LR0:IN_TOTAL, cols]).then_inc(sl_lr, 16)
                act.dma_start(four(l_q), h_t[GQ0:GK0, cols].rearrange("(c p) n -> p c n", p=P)).then_inc(sl_q, 16)
                act.dma_start(four(l_k), h_t[GK0:GV0, cols].rearrange("(c p) n -> p c n", p=P)).then_inc(sl_k, 16)

            def load_v(self, t):
                act = self.act
                if type(t) is int and t == 0:
                    for n in range(NG):
                        act.wait_ge(s_store[n], 16 * J_GLA)
                cols = ds(t * P + PAD, P)
                act.dma_start(l_v.rearrange("p (c n) -> p c n", c=8),
                              h_t[GV0:GG0, cols].rearrange("(c p) n -> p c n", p=P)).then_inc(sl_v, 16)

            def first(self):
                act = self.act
                act.wait_ge(sl_ini, 3)
                for n in range(NG):
                    act.wait_ge(s_store[n], 16 * (J_ATT + (GV0 - GQ0) // P))
                act.dma_start(l_og[:, 0:2], consts[:, 0:2]).then_inc(sl_st, 16)
                self.load(0)
                act.sem_inc(sl_og, 1)

            def exp(self, t, i, out, in_, scale):
                self.act.activation(out, in_, ACT.Exp, scale=scale / TAU).then_inc(sl_ex, 1)

            def gates(self, t):
                act = self.act
                act.wait_ge(sl_log, t + 1)
                act.activation(l_e[0], ub[0][:, :], ACT.Abs).then_inc(sl_a, 1)
                act.wait_ge(sl_a, 3 * t + 1)
                act.activation(l_e[0], l_e[0], ACT.Exp, scale=-1.0).then_inc(sl_a, 1)
                act.wait_ge(sl_a, 3 * t + 2)
                act.activation(l_e[0], l_e[0], ACT.Ln, bias=1.0).then_inc(sl_a, 1)

            def values(self, t):
                act = self.act
                for i in range(2):
                    act.wait_ge(sl_vtr, 2 * t + (i + 1))
                    act.activation(l_vtok[:, i * 512:i * 512 + 512], ub[1 + i][:, :], ACT.Copy).then_inc(sl_vtok, 1)

            def decays(self, t, dec=False):
                act = self.act
                act.wait_ge(sl_b, t + 1)
                self.exp(t, 0, l_e[0], l_b, 1.0)
                n = DEC_SEQ if dec else P
                act.activation(l_eb[:, 0:4 * P // n], l_b.rearrange("p (m n) -> p m n", n=n)[:, :, n - 1],
                               ACT.Exp, scale=1.0 / TAU).then_inc(sl_eb, 1)
                act.wait_ge(sl_d, (NZ - 1) * t + 1)
                self.exp(t, 1, l_e[1], l_e[1], -1.0)

            def keys(self, t):
                self.act.wait_ge(sl_kt, t + 1)
                self.act.activation(l_ktok, ub[3][:, :], ACT.Copy).then_inc(sl_ktok, 1)

            def level(self, t, i, s):
                self.act.wait_ge(sl_d, (NZ - 1) * t + (i + 2))
                e = halves(l_e[i % 2], s)
                self.act.activation(e[:, :, 0, :], e[:, :, 0, :], ACT.Exp, scale=-1.0 / TAU)
                self.exp(t, i + 2, e[:, :, 1, :], e[:, :, 1, :], 1.0)

            def squares(self, t):
                act = self.act
                for h in range(N_GLA):
                    act.wait_ge(sl_o, 2 * t + (h // 2 + 1))
                    act.activation(l_o[:, h * DV:h * DV + DV], ub[1 + h // 2][:, (h % 2) * DV:(h % 2) * DV + DV],
                                   ACT.Square, accum_out=l_ss[:, h:h + 1]).then_inc(sl_sq, 1)

            def rstd(self, t):
                act = self.act
                act.wait_ge(sl_var, t + 1)
                act.activation(l_rstd, l_var, ACT.Ln).then_inc(sl_lnv, 1)
                act.wait_ge(sl_lnv, t + 1)
                act.activation(l_rstd, l_rstd, ACT.Exp, scale=-0.5).then_inc(sl_rs, 1)

            def leave(self, t):
                act = self.act
                act.wait_ge(sl_st, 16 * t + 16)
                og = l_og.rearrange("p (h e n) -> p h e n", e=2, n=P)
                for i in range(2):
                    act.wait_ge(sl_gt, 2 * t + (i + 1))
                    bank = ub[3 + i][:, :].rearrange("p (h e n) -> p h e n", e=2, n=P)
                    for e in range(2):
                        act.activation(og[:, 2 * i:2 * i + 2, e, :], bank[:, :, e, :], ACT.Copy,
                                       scale=gn_col[:, e:e + 1]).then_inc(sl_og, 1)
                act.wait_ge(sl_og, 4 * t + 5)
                act.dma_start(o_t[D_MODEL // 2:D_MODEL, ds(t * P, P)].rearrange("(c p) n -> p c n", p=P),
                              l_og.rearrange("p (c n) -> p c n", c=8)).then_inc(sl_st, 16)

            def tile(self, t):
                def part_0():
                    self.gates(t)
                    if not (type(t) is int and t == 0):
                        self.leave(t - 1)
                    self.load_v(t)
                    self.decays(t)
                    self.level(t, 0, LEVELS[0])
                    self.keys(t)
                    for i in range(1, 4):
                        self.level(t, i, LEVELS[i])

                def part_1():
                    self.values(t)
                    for i in range(4, 7):
                        self.level(t, i, LEVELS[i])

                def part_2():
                    self.squares(t)
                    self.rstd(t)
                    self.load(t + 1)
                return part_0, part_1, part_2

        class linear_dve:
            def __init__(self, dve):
                self.dve = dve

            def first(self):
                dve = self.dve
                dve.wait_ge(sb_w, 16 * 5)
                dve.memset(l_s, 0.0).then_inc(sl_ini, 1)
                dve.memset(l_att, 0.0).then_inc(sl_ini, 1)
                dve.memset(lr[:, :], 1.0).then_inc(sl_ini, 1)
                dve.wait_ge(sl_ini, 3)
                dve.sem_inc(sl_up, 1)
                dve.sem_inc(sl_on, 1)

            def distance(self, t, i, n, at):
                dve = self.dve
                if i >= 0:
                    dve.wait_ge(sl_zz, NZ * t + (i + 1))
                b = l_b.rearrange("p (m n) -> p m n", n=n)
                dve.tensor_tensor(l_e[i % 2].rearrange("p (m n) -> p m n", n=n), b,
                                  b[:, :, at:at + 1].to_broadcast([P, 4 * P // n, n]), ALU.subtract).then_inc(sl_d, 1)

            def copy_diagonal(self, t):
                dve = self.dve
                dve.wait_ge(sl_dg, t + 1)
                dve.nop(nofuse=True)
                dve.copy_predicated(l_att, tables_sb[:, M_DIAG:M_DIAG + 512], ub[0][:, :]).then_inc(sl_dcp, 1)

            def gates(self, t, dec=False):
                dve = self.dve
                dve.wait_ge(sl_a, 3 * t + 3)
                dve.scalar_tensor_tensor(out=l_e[1], in0=ub[0][:, :], scalar=0.0, in1=l_e[0], op0=ALU.min,
                                         op1=ALU.subtract).then_inc(sl_la, 1)
                dve.wait_ge(sl_la, t + 1)
                m = M_SCAN_DEC if dec else M_SCAN
                dve.tensor_tensor_scan(l_b, tables_sb[:, m:m + 512], l_e[1], 0.0, ALU.mult, ALU.add)\
                   .then_inc(sl_b, 1)
                dve.wait_ge(sl_b, t + 1)
                n = DEC_SEQ if dec else P
                self.distance(t, -1, n, n - 1)
                self.copy_diagonal(t)
                dve.wait_ge(sl_ex, NZ * t + 1)
                dve.wait_ge(sl_q, 16 * t + 16)
                dve.tensor_tensor(l_qe, l_q, l_e[0], ALU.mult).then_inc(sl_zz, 1)
                s = (DEC_LEVELS if dec else LEVELS)[0]
                self.distance(t, 0, 2 * s, s - 1)
                dve.wait_ge(sl_ex, NZ * t + 2)
                dve.wait_ge(sl_k, 16 * t + 16)
                dve.tensor_tensor(l_z[0], l_k, l_e[1], ALU.mult).then_inc(sl_zz, 1)
                self.distance(t, 1, s, s // 2 - 1)

            def level(self, t, i, s):
                dve = self.dve
                dve.wait_ge(sl_ex, NZ * t + (i + 3))
                if i == 1:
                    dve.wait_ge(sl_kt, t + 1)
                if i >= 2:
                    dve.wait_ge(sl_p, len(LEVELS) * t + (i - 1))
                z, e, q, k = (halves(x, s) for x in (l_z[(i + 1) % 2], l_e[i % 2], l_q, l_k))
                dve.tensor_tensor(z[:, :, 0, :], k[:, :, 0, :], e[:, :, 0, :], ALU.mult)
                dve.tensor_tensor(z[:, :, 1, :], q[:, :, 1, :], e[:, :, 1, :], ALU.mult).then_inc(sl_zz, 1)
                if s >= 4:
                    self.distance(t, i + 2, s // 2, s // 4 - 1)

            def take(self, t, i, s):
                dve = self.dve
                if i:
                    dve.wait_ge(sl_cp, len(LEVELS) * t + i)
                else:
                    dve.wait_ge(sl_dcp, t + 1)
                dve.wait_ge(sl_p, len(LEVELS) * t + (i + 1))
                dve.nop(nofuse=True)
                m = LEVELS.index(s) * 256
                dve.copy_predicated(halves(l_att, s)[:, :, 1, :],
                                    tables_sb[:, m:m + 256].rearrange("p (n s) -> p n s", s=s),
                                    ub[4 - i % 2][:, 0:256].rearrange("p (n s) -> p n s", s=s)).then_inc(sl_cp, 1)

            def variance(self, t):
                dve = self.dve
                dve.wait_ge(sl_sq, 4 * t + 4)
                dve.tensor_scalar(l_var, l_ss, 1.0 / DV, EPS, ALU.mult, ALU.add).then_inc(sl_var, 1)

            def scale_out(self, t):
                dve = self.dve
                dve.wait_ge(sl_rs, t + 1)
                dve.tensor_tensor(l_var, l_var, l_rstd, ALU.mult).then_inc(sl_nt, 1)
                dve.wait_ge(sl_nt, 4 * t + 1)
                dve.tensor_tensor(l_var, l_var, l_rstd, ALU.mult).then_inc(sl_nt, 1)
                dve.wait_ge(sl_nt, 4 * t + 2)
                dve.tensor_scalar(l_var, l_var, -0.5, 1.5, ALU.mult, ALU.add).then_inc(sl_nt, 1)
                dve.wait_ge(sl_nt, 4 * t + 3)
                dve.tensor_tensor(l_rstd, l_rstd, l_var, ALU.mult).then_inc(sl_nt, 1)
                dve.wait_ge(sl_nt, 4 * t + 4)
                for h in range(N_GLA):
                    dve.tensor_scalar(l_o[:, h * DV:h * DV + DV],
                                      ub[1 + h // 2][:, (h % 2) * DV:(h % 2) * DV + DV],
                                      l_rstd[:, h:h + 1], None, ALU.mult).then_inc(sl_on, 1)

            def state(self, t):
                dve = self.dve
                dve.wait_ge(sl_eb, t + 1)
                for h in range(N_GLA):
                    dve.wait_ge(sl_ds, 2 * t + (h // 2 + 1))
                    sh = l_s[:, h * DV:h * DV + DV]
                    dve.scalar_tensor_tensor(out=sh, in0=sh, scalar=l_eb[:, h:h + 1],
                                             in1=ub[4 * (h // 2)][:, (h % 2) * DV:(h % 2) * DV + DV],
                                             op0=ALU.mult, op1=ALU.add).then_inc(sl_up, 1)

            def tile(self, t):
                def part_0():
                    self.gates(t)
                    self.level(t, 0, LEVELS[0])
                    for i in range(1, 4):
                        self.level(t, i, LEVELS[i])
                        self.take(t, i - 1, LEVELS[i - 1])

                def part_1():
                    for i in range(4, 7):
                        self.level(t, i, LEVELS[i])
                        self.take(t, i - 1, LEVELS[i - 1])

                def part_2():
                    self.take(t, 6, LEVELS[6])
                    self.state(t)
                    self.variance(t)
                    self.scale_out(t)
                return part_0, part_1, part_2

        T = NTP
        HALF = DEC_BATCH // 2
        d_s = [work[:, 0:1024], work[:, 4608:5632]]
        d_q = work[:, 3584:4608]
        d_q_own = work[:, 3584:4736].rearrange("p (s m) -> p s m", m=P + DEC_SEQ)[:, :, 0:DEC_SEQ]
        d_k = l_v
        d_bank = ub[3:5]

        class decode_pe:

            def __init__(self, pe):
                self.pe = pe

            def levels(self):
                logits, values, diagonal, keys, level, _, _ = linear_stages(self.pe, T, dec=True)
                stages = {3: logits, 6: linear_stages(self.pe, T - 1)[-1], 12: diagonal, 18: keys, 32: values}
                for i, step in enumerate((20, 22, 25, 28)):
                    stages[step] = lambda i=i: level(i)
                return stages

            def half(self, h, half):
                pe = self.pe
                out = ub[1 + h // 2][:, (h % 2) * DV:(h % 2) * DV + DV]
                vh = l_vtok[:, h * DV:h * DV + DV]
                if half == 0:
                    pe.wait_ge(sl_cp, len(LEVELS) * T + len(DEC_LEVELS))
                    pe.wait_ge(sl_dcp, T + 1)
                    pe.wait_ge(sl_vtok, 2 * T + 2)
                    pe.wait_ge(sd_q, h + 2)
                    pe.matmul(out, l_att[:, h * P:h * P + P], vh, start=True, stop=False)
                pe.wait_ge(sd_in[half], 16 * (h + 1))
                for i in range(HALF):
                    s = half * HALF + i
                    mm = pe.matmul(out, d_q[:, s * P:s * P + P], d_s[half][:, i * DV:i * DV + DV],
                                   start=False, stop=(s == DEC_BATCH - 1))
                pe.wait_ge(sd_k, h + 1)
                if h or half:
                    pe.wait_ge(sd_up, DEC_BATCH * h + HALF * half)
                for i in range(HALF):
                    s = half * HALF + i
                    mm = pe.matmul(d_bank[i // 2][:, (i % 2) * DV:(i % 2) * DV + DV], d_k[:, s * P:s * P + P], vh,
                                   start=True, stop=True)
                    if i % 2:
                        mm.then_inc(sd_ds, 1)

            def head(self, h):
                return {9: lambda: self.half(h, 0), 30: lambda: self.half(h, 1)}

            def out(self):
                def turn():
                    self.pe.wait_ge(sd_up, DEC_BATCH * N_GLA)
                    linear_stages(self.pe, T)[-1](decoded=True)
                return {24: turn}

        class decode_act:

            def __init__(self, act, lin):
                self.act, self.lin = act, lin

            def load(self, h, half):
                self.act.dma_start(d_s[half].rearrange("p (s e) -> p s e", s=HALF),
                                   state[half * HALF:half * HALF + HALF, h].rearrange("s d e -> d s e"))\
                    .then_inc(sd_in[half], 16)

            def store(self, h, half):
                self.act.wait_ge(sd_up, DEC_BATCH * h + HALF * half + HALF)
                self.act.dma_start(gla_s[half * HALF:half * HALF + HALF, h].rearrange("s d e -> d s e"),
                                   d_s[half].rearrange("p (s e) -> p s e", s=HALF)).then_inc(sd_out[half], 16)

            def levels(self):
                act, lin = self.act, self.lin

                def part_0():
                    lin.gates(T)
                    lin.leave(T - 1)
                    lin.load_v(T)
                    act.wait_ge(sl_up, 4 * NTP + 1)
                    act.dma_start(gla_p.rearrange("h d e -> d h e"), l_s.rearrange("p (h e) -> p h e", h=N_GLA))\
                       .then_inc(sd_gp, 16)
                    lin.decays(T, dec=True)
                    lin.level(T, 0, DEC_LEVELS[0])
                    lin.keys(T)
                    for i in range(1, len(DEC_LEVELS)):
                        lin.level(T, i, DEC_LEVELS[i])

                def part_1():
                    lin.values(T)
                    act.wait_ge(sl_zz, NZ * T + 2 + len(DEC_LEVELS))
                    act.wait_ge(sl_p, len(LEVELS) * T + len(DEC_LEVELS))
                    self.load(0, 0)
                    self.load(0, 1)
                return part_0, part_1, lambda: None

            def head(self, h):
                def part_0():
                    if h:
                        self.act.wait_ge(sd_out[1], 16 * h)
                        self.load(h, 1)

                def part_2():
                    self.store(h, 1)
                    if h + 1 < N_GLA:
                        self.act.wait_ge(sd_out[0], 16 * (h + 1))
                        self.load(h + 1, 0)
                return part_0, lambda: self.store(h, 0), part_2

            def out(self):
                def part_0():
                    act = self.act
                    act.wait_ge(sd_ds, 4 * N_GLA)
                    for h in range(N_GLA):
                        act.activation(l_o[:, h * DV:h * DV + DV],
                                       ub[1 + h // 2][:, (h % 2) * DV:(h % 2) * DV + DV],
                                       ACT.Square, accum_out=l_ss[:, h:h + 1]).then_inc(sl_sq, 1)
                    self.lin.rstd(T)
                return part_0, lambda: self.lin.leave(T), lambda: None

            def end(self):
                for half in range(2):
                    self.act.wait_ge(sd_out[half], 16 * N_GLA)
                self.act.wait_ge(sd_gp, 16)
                self.act.wait_ge(sl_st, 16 * (NT + 1))

        class decode_dve:

            def __init__(self, dve, lin):
                self.dve, self.lin = dve, lin

            def levels(self):
                dve, lin = self.dve, self.lin

                def part_0():
                    dve.wait_ge(sl_o, 2 * NTP)
                    dve.memset(l_att, 0.0).then_inc(sl_ini, 1)
                    dve.wait_ge(sl_ini, 4)
                    lin.gates(T, dec=True)
                    lin.level(T, 0, DEC_LEVELS[0])
                    for i in range(1, len(DEC_LEVELS)):
                        lin.level(T, i, DEC_LEVELS[i])
                        lin.take(T, i - 1, DEC_LEVELS[i - 1])

                def part_1():
                    lin.take(T, len(DEC_LEVELS) - 1, DEC_LEVELS[-1])
                    dve.memset(d_q, 0.0).then_inc(sd_q, 1)
                return part_0, part_1, lambda: None

            def head(self, h):
                dve = self.dve

                def part_0():
                    if h:
                        dve.wait_ge(sd_ds, 4 * h)
                    else:
                        dve.wait_ge(sd_q, 1)
                        dve.wait_ge(sl_ktok, T + 1)
                        dve.wait_ge(sl_vtok, 2 * T + 2)
                        dve.wait_ge(sl_eb, T + 1)
                    dve.tensor_copy(d_q_own, l_qe[:, h * P:h * P + P].rearrange("p (s n) -> p s n", n=DEC_SEQ))\
                       .then_inc(sd_q, 1)
                    for s in range(DEC_BATCH):
                        ins = dve.tensor_scalar(d_k[:, s * P:s * P + P], l_ktok[:, h * P:h * P + P],
                                                seq_col[:, s:s + 1], None, ALU.mult)
                    ins.then_inc(sd_k, 1)
                return part_0, lambda: self.update(h, 0), lambda: self.update(h, 1)

            def update(self, h, half):
                dve = self.dve
                for i in range(HALF):
                    dve.wait_ge(sd_ds, 4 * h + 2 * half + i // 2 + 1)
                    m = h * DEC_BATCH + half * HALF + i
                    sh = d_s[half][:, i * DV:i * DV + DV]
                    dve.scalar_tensor_tensor(out=sh, in0=sh, scalar=l_eb[:, m:m + 1],
                                             in1=d_bank[i // 2][:, (i % 2) * DV:(i % 2) * DV + DV],
                                             op0=ALU.mult, op1=ALU.add).then_inc(sd_up, 1)

            def out(self):
                def part_0():
                    self.lin.variance(T)
                    self.lin.scale_out(T)
                return part_0, lambda: None, lambda: None

        KEYS = CACHE + DEC_SEQ
        b_q = work[:, 0:1024].rearrange("p (g r n) -> p g r n", g=2, r=GQA)
        b_kn = work[:, 1024:1280].rearrange("p (c n) -> p c n", c=2)
        b_vn = work[:, 1280:1536].rearrange("p (c n) -> p c n", c=2)
        b_ck = work[:, 1536:1792]
        b_cv = work[:, 2048:2304]
        b_ks = work[:, 2560:2848].rearrange("p (g n) -> p g n", g=2)
        b_p = work[:, 2848:3136].rearrange("p (g n) -> p g n", g=2)
        b_ptc = work[:, 3136:3392]
        b_ptn = work[0:DEC_SEQ, 3392:3648]
        b_vnew = work[0:DEC_SEQ, 3648:3904]
        b_qb = work[:, 3904:4032].rearrange("p (g n) -> p g n", g=2)
        b_vb = work[:, 4032:4064].rearrange("p (c n) -> p c n", c=2)
        b_o = work[0:HEAD_DIM, 4064:6112].rearrange("p (h n) -> p h n", h=N_HEADS)
        b_ex = [work[:, 6112 + 256 * i:6368 + 256 * i] for i in range(4)]
        b_kp = work[:, 7136:7392].rearrange("p (c n) -> p c n", c=2)
        b_vp = work[:, 7392:7648].rearrange("p (c n) -> p c n", c=2)
        b_mx, b_mn, b_neg, b_sk, b_es, b_sum, b_den = (small[:, 8 + 2 * i:10 + 2 * i] for i in range(7))
        kb, vb, sb_, pb, nb = ub
        ob = sb_

        def cached_pe(pe, b, first=False):
            def exports():
                pe.wait_ge(sb_in, 16 * 8)
                pe.wait_ge(sa_out, 4 * NTP + 1)
                for i, x in enumerate((b_kp, b_vp, b_kn, b_vn)):
                    for c in range(2):
                        mm = pe.transpose(ub[i][:, c * P:c * P + P], x[:, c, :], ident)
                    mm.then_inc(sb_xt, 1)

            def keys():
                pe.wait_ge(sb_ck, 16 * b + 16)
                pe.wait_ge(sb_new, b + 1)
                for gp in range(2):
                    pe.transpose(kb[:, gp * P:gp * P + P], b_ck[:, gp * P:gp * P + P], ident)
                for c in range(2):
                    mm = pe.transpose(vb[0:DEC_SEQ, c * P:c * P + P], b_vb[:, c, :], ident)
                mm.then_inc(sb_kt, 1)

            def scores():
                pe.wait_ge(sb_ks, b + 1)
                pe.nop(nofuse=True)
                for gp in range(2):
                    for half in range(2):
                        rows = slice(half * HEAD_DIM, half * HEAD_DIM + HEAD_DIM)
                        mm = pe.matmul(sb_[rows, gp * KEYS:gp * KEYS + KEYS], b_qb[rows, gp, :], b_ks[rows, gp, :],
                                       start=True, stop=True)
                mm.then_inc(sb_s, 1)

            def turn():
                pe.wait_ge(sb_pr, 2 * b + 2)
                for gp in range(2):
                    mm = pe.transpose(pb[:, gp * P:gp * P + P], b_p[:, gp, 0:CACHE], ident)
                mm.then_inc(sb_pt, 1)
                for gp in range(2):
                    mm = pe.transpose(nb[0:DEC_SEQ, gp * P:gp * P + P], b_p[:, gp, CACHE:KEYS], ident)
                mm.then_inc(sb_pt, 1)

            def outputs():
                pe.wait_ge(sb_cv, 16 * b + 16)
                pe.wait_ge(sb_pc, 2 * b + 2)
                for g in range(N_KV):
                    cols = slice((g // 2) * P + (g % 2) * HEAD_DIM, (g // 2) * P + (g % 2) * HEAD_DIM + HEAD_DIM)
                    dims = slice(g * HEAD_DIM, g * HEAD_DIM + HEAD_DIM)
                    pe.matmul(ob[0:HEAD_DIM, dims], b_cv[:, dims], b_ptc[:, cols], start=True, stop=False)
                    mm = pe.matmul(ob[0:HEAD_DIM, dims], b_vnew[:, dims], b_ptn[:, cols], start=False, stop=True)
                mm.then_inc(sb_av, 1)

            def first_keys():
                exports()
                pe.wait_ge(sb_xc, 4)
                keys()

            return {12: first_keys if first else keys, 20: scores, 32: turn, 42: outputs}

        class cached_act:
            def __init__(self, act):
                self.act = act

            def load(self, b, which):
                dst, src, s = ((b_ck, cache_k, sb_ck), (b_cv, cache_v, sb_cv))[which]
                self.act.dma_start(dst, src[ds(b, 1)].rearrange("a t n -> (a t) n")).then_inc(s, 16)

            def first(self):
                act = self.act
                act.wait_ge(sa_st, 16 * (4 * NTP + 1))
                q_v = h_t[Q0:K0, PAD + SEQ:PAD + TOK].rearrange("(g f r d) n -> f d g r n", g=2, f=2, r=GQA)
                for half in range(2):
                    for gp in range(2):
                        act.dma_start(b_q[half * HEAD_DIM:half * HEAD_DIM + HEAD_DIM, gp], q_v[half][:, gp])\
                           .then_inc(sb_in, 16)
                for x, row, col in ((b_kn, K0, PAD + SEQ), (b_vn, V0, PAD + SEQ),
                                    (b_kp, K0, PAD + SEQ - P), (b_vp, V0, PAD + SEQ - P)):
                    act.dma_start(x, h_t[row:row + 256, col:col + P].rearrange("(c p) n -> p c n", p=P))\
                       .then_inc(sb_in, 16)
                self.load(0, 0)
                self.load(0, 1)
                act.wait_ge(sa_mk, NTP + 1)
                for i in range(4):
                    act.wait_ge(sb_xt, i + 1)
                    act.activation(b_ex[i], ub[i][:, 0:256], ACT.Copy).then_inc(sb_xc, 1)
                act.wait_ge(sb_xc, 4)
                act.dma_start(win_kp, b_ex[0]).then_inc(sb_w, 16)
                act.dma_start(win_vp, b_ex[1]).then_inc(sb_w, 16)
                act.dma_start(win_ks[:, CACHE - DEC_SEQ:CACHE, :], b_ex[2]).then_inc(sb_w, 16)
                act.dma_start(win_vs[:, CACHE - DEC_SEQ:CACHE, :], b_ex[3]).then_inc(sb_w, 16)

            def sequence(self, b):
                act = self.act
                more = not (type(b) is int and b == DEC_BATCH - 1)

                def part_0():
                    act.wait_ge(sb_kt, b + 1)
                    act.activation(b_ks[:, :, 0:CACHE], kb[:, 0:256].rearrange("p (g n) -> p g n", g=2), ACT.Copy)
                    act.activation(b_vnew, vb[0:DEC_SEQ, 0:256], ACT.Copy).then_inc(sb_ks, 1)
                    if more:
                        self.load(b + 1, 0)
                    act.wait_ge(sb_neg, b + 1)
                    act.activation(b_es, b_sk, ACT.Exp)
                    for gp in range(2):
                        act.activation(b_p[:, gp, :], sb_[:, gp * KEYS:gp * KEYS + KEYS], ACT.Exp,
                                       bias=b_neg[:, gp:gp + 1], accum_out=b_sum[:, gp:gp + 1]).then_inc(sb_e, 1)
                    act.wait_ge(sb_pt, 2 * b + 1)
                    act.activation(b_ptc, pb[:, 0:256], ACT.Copy).then_inc(sb_pc, 1)
                    act.wait_ge(sb_pt, 2 * b + 2)
                    act.activation(b_ptn, nb[0:DEC_SEQ, 0:256], ACT.Copy).then_inc(sb_pc, 1)
                    act.wait_ge(sb_av, b + 2)
                    act.activation(b_o[:, :, ds(b * DEC_SEQ, DEC_SEQ)],
                                   ob[0:HEAD_DIM, 0:256].rearrange("p (h n) -> p h n", h=N_HEADS), ACT.Copy)\
                       .then_inc(sb_oc, 1)
                    if more:
                        self.load(b + 1, 1)
                return part_0, lambda: None, lambda: None

            def last(self):
                self.act.wait_ge(sb_oc, DEC_BATCH)
                self.act.dma_start(o_t[0:D_MODEL // 2, SEQ:TOK].rearrange("(h d) n -> d h n", d=HEAD_DIM), b_o)\
                    .then_inc(sb_w, 16)
                self.act.wait_ge(sb_w, 16 * 5)

        class cached_dve:
            def __init__(self, dve):
                self.dve = dve

            def first(self):
                self.dve.wait_ge(sb_in, 16 * 8)
                self.dve.sem_inc(sb_av, 1)

            def sequence(self, b):
                dve = self.dve

                def part_0():
                    tok = ds(b * DEC_SEQ, DEC_SEQ)
                    dve.wait_ge(sb_av, b + 1)
                    dve.tensor_copy(b_qb.rearrange("p g (r n) -> p g r n", r=GQA), b_q[:, :, :, tok])
                    dve.tensor_copy(b_vb, b_vn[:, :, tok])
                    dve.tensor_copy(b_ks[:, :, CACHE:KEYS], b_kn[:, :, tok]).then_inc(sb_new, 1)
                    dve.wait_ge(sb_s, b + 1)
                    dve.tensor_reduce(b_mx, sb_[:, 0:2 * KEYS].rearrange("p (g n) -> p g n", g=2), AX.X, ALU.max)\
                       .then_inc(sb_dv, 1)
                    dve.wait_ge(sb_dv, 5 * b + 1)
                    dve.tensor_tensor(b_mn, b_mx, sink_dec[:, :], ALU.max).then_inc(sb_dv, 1)
                    dve.wait_ge(sb_dv, 5 * b + 2)
                    dve.tensor_scalar(b_neg, b_mn, -1.0, None, ALU.mult).then_inc(sb_dv, 1)
                    dve.wait_ge(sb_dv, 5 * b + 3)
                    dve.tensor_tensor(b_sk, sink_dec[:, :], b_neg, ALU.add).then_inc(sb_neg, 1)

                def part_1():
                    dve.wait_ge(sb_e, 2 * b + 2)
                    dve.tensor_tensor(b_den, b_sum, b_es, ALU.add).then_inc(sb_dv, 1)
                    dve.wait_ge(sb_dv, 5 * b + 4)
                    dve.reciprocal(b_den, b_den).then_inc(sb_dv, 1)
                    dve.wait_ge(sb_dv, 5 * b + 5)
                    for gp in range(2):
                        dve.tensor_scalar(b_p[:, gp, :], b_p[:, gp, :], b_den[:, gp:gp + 1], None, ALU.mult)\
                           .then_inc(sb_pr, 1)
                return part_0, part_1, lambda: None

        @block.gpsimd
        def _(pool):
            pool.memset(mhalf[:, :], -0.5).then_inc(s_mh, 1)
            pool.memset(zeros[:, :], 0.0).then_inc(s_mh, 1)
            pool.wait_ge(s_mh, 2)
            for t in range(NT):
                pool.wait_ge(s_var, t + 1)
                pool.tensor_tensor(rstd, var, mhalf[:, 0:1], ALU.pow).then_inc(s_rstd, 1)
                if t == 1:
                    split(pool, 0, RANK)
            split(pool, 1)
            pool.wait_ge(s_tload, 16)
            pool.tensor_copy(tables_sb[:, :], work[:, 2 * D_MODEL:2 * D_MODEL + M_ALL]).then_inc(s_tables, 1)
            with pool.Fori(2, 1 + N_ITEMS) as j:
                split(pool, j)

        @block.scalar
        def _(act):
            act.sem_inc(s_wfree, 4)
            act.sem_inc(s_staged, 3)
            act.sem_inc(s_xt, 4)

            def high_halves(t):
                for b in range(4):
                    act.wait_ge(s_xt, 4 * t + (b + 5))
                    act.activation(x_hi[:, 4 * b:4 * b + 4, t * P:t * P + P],
                                   xt_bank[b][:, :].rearrange("p (k n) -> p k n", k=4), ACT.Copy)\
                       .then_inc(s_xhi, 1)

            for t in range(NT):
                act.wait_ge(s_x[t % 3], 16 * (t // 3) + 16)
                if t >= 1:
                    act.wait_ge(s_ss, t)
                if t >= 2:
                    act.wait_ge(s_var, t - 1)
                act.activation(squares, x_buf[t % 3], ACT.Square, accum_out=ss[:, t % 2:t % 2 + 1])\
                   .then_inc(s_ss, 1)
                if t >= 1:
                    high_halves(t - 1)
            high_halves(NT - 1)

            def item_norm_b(j, n):
                wait_acc(act, j, n)
                act.wait_ge(s_ssq, (j - 1) * NG + (n + 1))
                act.activation(tmp_a, acc[n][:, 0:TN], ACT.Square).then_inc(s_sq, 1)
                act.wait_ge(s_v, (j - 1) * NG + (n + 2))
                act.activation(tmp_b, tmp_b, ACT.Sqrt).then_inc(s_sd, 1)

            def item_silu(j, n):
                wait_acc(act, j, n)
                act.wait_ge(s_staged, j * NG + (n + 3))
                act.activation(tmp_a, acc[n][:, 0:TN], ACT.Exp, scale=-1.0).then_inc(s_sig, 1)

            def nothing(j, n):
                pass

            def item(j, before, now, unit=(lambda: None, lambda: None, lambda: None)):
                before(j - 1, 2)
                unit[0]()
                now(j, 0)
                unit[1]()
                now(j, 1)
                unit[2]()

            act.sem_inc(s_ssq, 1)
            item(1, nothing, item_norm_b)
            with act.Fori(2, 1 + N_QK) as j:
                item(j, item_norm_b, item_norm_b)
            item(1 + N_QK, item_norm_b, nothing)
            item(2 + N_QK, nothing, nothing)
            attend = attend_act(act)
            act.wait_ge(s_tab, 16 * 21)
            act.wait_ge(s_tables, 1)
            attend.first()
            with act.Fori(J_ATT, J_DEC - 1) as j:
                item(j, nothing, nothing, attend.tile(j - J_ATT))
            item(J_DEC - 1, nothing, nothing, attend.tile(NTP - 1))
            cached = cached_act(act)
            cached.first()
            with act.Fori(J_DEC, J_GLA - 1) as j:
                item(j, nothing, nothing, cached.sequence(j - J_DEC))
            item(J_GLA - 1, nothing, nothing, cached.sequence(DEC_BATCH - 1))
            cached.last()
            linear = linear_act(act)
            linear.first()
            item(J_GLA, nothing, item_silu, linear.tile(0))
            with act.Fori(J_GLA + 1, J_GLA + NTP) as j:
                item(j, item_silu, item_silu, linear.tile(j - J_GLA))
            decode = decode_act(act, linear)
            item(J_LEV, item_silu, item_silu, decode.levels())
            for h in range(N_GLA):
                item(J_LEV + 1 + h, item_silu, item_silu, decode.head(h))
            item(J_LEV + 1 + N_GLA, item_silu, item_silu, decode.out())
            with act.Fori(J_LEV + 2 + N_GLA, 1 + N_ITEMS) as j:
                item(j, item_silu, item_silu)
            item_silu(N_ITEMS, 2)
            decode.end()

        @block.tensor
        def _(pe):
            pe.wait_ge(s_const, 16 * 6)

            def turn_x(t):
                pe.wait_ge(s_xn, t + 1)
                for b in range(4):
                    pe.wait_ge(s_xlo, 4 * t + (b + 1))
                    for k in range(4):
                        c = (4 * b + k) * P
                        mm = pe.transpose(xt_bank[b][:, k * P:k * P + P], x_buf[t % 3][:, c:c + P], ident)
                    mm.then_inc(s_xt, 1)

            def item(j, cols, norm=False, norm_before=False, stages={}):
                for n in range(NG):
                    group(j, n, cols, norm, norm_before, stages)

            def group(j, n, cols, norm=False, norm_before=False, stages={}):
                pe.wait_ge(s_staged, NG * j + (n + 1))
                for k in range(KT):
                    if n * KT + k in stages:
                        stages[n * KT + k]()
                    if n == 0 and k % 4 == 0:
                        pe.wait_ge(s_wready, 4 * j + (k // 4 + 1))
                    if n > 0 and k == 4 and norm:
                        sum_squares(j, n - 1)
                    if n == 0 and k == 4 and norm_before:
                        sum_squares(j - 1, NG - 1)
                    tok = slice(n * TN, n * TN + TN)
                    out = acc[n][0:cols, 0:TN]
                    pe.matmul(out, w_lo[:, k, 0:cols], x_hi[:, k, tok], start=(k == 0), stop=False)
                    pe.matmul(out, w_hi[:, k, 0:cols], x_lo[:, k, tok], start=False, stop=False)
                    mm = pe.matmul(out, w_hi[:, k, 0:cols], x_hi[:, k, tok], start=False,
                                   stop=(k == KT - 1))
                    if n == NG - 1 and k % 4 == 3:
                        mm.then_inc(s_wfree, 1)
                if n < NG - 1:
                    mm.then_inc(s_acc, 1)

            def sum_squares(j, n):
                pe.wait_ge(s_sq, (j - 1) * NG + (n + 1))
                pe.wait_ge(s_v, (j - 1) * NG + (n + 1))
                pe.matmul(ss_bank[:, 0:TN], ones_pair, tmp_a, start=True, stop=True).then_inc(s_ssq, 1)

            for t in range(NT):
                turn_x(t)
                if t % NG == 0 and t > 0:
                    pe.wait_ge(s_xlo, 4 * t + 4)
                    group(0, t // NG - 1, RANK)
            pe.wait_ge(s_xlo, 4 * NT + 4)
            group(0, NG - 1, RANK)
            item(1, P, norm=True)
            with pe.Fori(2, 1 + N_QK) as j:
                item(j, P, norm=True, norm_before=True)
            item(1 + N_QK, P, norm_before=True)
            item(2 + N_QK, P)
            pe.wait_ge(s_tab, 16 * 21)
            with pe.Fori(J_ATT, J_DEC) as j:
                item(j, P, stages=attend_pe(pe, j - J_ATT))
            item(J_DEC, P, stages=cached_pe(pe, 0, True))
            with pe.Fori(J_DEC + 1, J_GLA) as j:
                item(j, P, stages=cached_pe(pe, j - J_DEC))
            item(J_GLA, P, stages=linear_pe(pe, 0, True))
            with pe.Fori(J_GLA + 1, J_GLA + NTP) as j:
                item(j, P, stages=linear_pe(pe, j - J_GLA))
            decode = decode_pe(pe)
            item(J_LEV, P, stages=decode.levels())
            for h in range(N_GLA):
                item(J_LEV + 1 + h, P, stages=decode.head(h))
            item(J_LEV + 1 + N_GLA, P, stages=decode.out())
            with pe.Fori(J_LEV + 2 + N_GLA, 1 + N_ITEMS) as j:
                item(j, P)

        @block.vector
        def _(dve):
            dve.sem_inc(s_v, 1)
            dve.sem_inc(s_xlo, 4)
            dve.wait_ge(s_const, 16 * 6)
            dve.tensor_scalar(gq_col[:, 0:1], gq_col[:, 0:1], HEAD_DIM ** -0.5, None, ALU.mult)\
               .then_inc(s_nchain, 1)

            def low_halves(t):
                for b in range(4):
                    dve.wait_ge(s_xhi, 4 * t + (b + 1))
                    dst = x_lo[:, 4 * b:4 * b + 4, t * P:t * P + P]
                    dve.tensor_tensor(dst, xt_bank[b][:, :].rearrange("p (k n) -> p k n", k=4),
                                      x_hi[:, 4 * b:4 * b + 4, t * P:t * P + P].bitcast(F32),
                                      ALU.subtract).then_inc(s_xlo, 1)

            for t in range(NT):
                dve.wait_ge(s_ss, t + 1)
                dve.tensor_scalar(var[:, :], ss[:, t % 2:t % 2 + 1], 1.0 / D_MODEL, EPS, ALU.mult, ALU.add)\
                   .then_inc(s_var, 1)
                if t >= 1:
                    low_halves(t - 1)
                dve.wait_ge(s_rstd, t + 1)
                dve.scalar_tensor_tensor(out=x_buf[t % 3], in0=x_buf[t % 3], scalar=rstd[:, 0:1],
                                         in1=g_row, op0=ALU.mult, op1=ALU.mult).then_inc(s_xn, 1)
            low_halves(NT - 1)
            dve.wait_ge(s_xt, 4 * NT + 4)
            dve.memset(xn[:, 5 * TN:5 * TN + PAD], 0.0).then_inc(s_zero, 1)

            def staging_free(j, n):
                dve.wait_ge(s_store[n], 16 * j)

            def done(ins):
                ins.then_inc(s_staged, 1)

            def plain(j, n, rows=P, first=False):
                wait_acc(dve, j, n)
                if not first:
                    staging_free(j, n)
                done(dve.tensor_copy(stage[n][0:rows, :], acc[n][0:rows, 0:TN]))

            def scaled(j, n):
                wait_acc(dve, j, n)
                staging_free(j, n)
                done(dve.tensor_scalar(stage[n], acc[n][:, 0:TN], DK ** -0.5, None, ALU.mult))

            def normed(which):
                def run(j, n):
                    dve.wait_ge(s_ssq, (j - 1) * NG + (n + 2))
                    dve.tensor_scalar(tmp_b, ss_bank[:, 0:TN], 1.0 / HEAD_DIM, EPS, ALU.mult, ALU.add)\
                       .then_inc(s_v, 1)
                    dve.wait_ge(s_sd, (j - 1) * NG + (n + 1))
                    staging_free(j, n)
                    dve.reciprocal(stage[n], tmp_b).then_inc(s_nchain, 1)
                    dve.wait_ge(s_nchain, (j - 1) * NG + (n + 2))
                    done(dve.scalar_tensor_tensor(out=stage[n], in0=acc[n][:, 0:TN],
                                                  scalar=gq_col[:, which:which + 1], in1=stage[n],
                                                  op0=ALU.mult, op1=ALU.mult))
                return run

            def silu(j, n):
                base = (j - J_GLA) * (2 * NG) + 2 * n
                dve.wait_ge(s_sig, (j - J_GLA) * NG + (n + 1))
                dve.tensor_scalar(tmp_a, tmp_a, 1.0, None, ALU.add).then_inc(s_schain, 1)
                dve.wait_ge(s_schain, base + 1)
                dve.reciprocal(tmp_a, tmp_a).then_inc(s_schain, 1)
                dve.wait_ge(s_schain, base + 2)
                staging_free(j, n)
                done(dve.tensor_tensor(stage[n], acc[n][:, 0:TN], tmp_a, ALU.mult))

            def item(j, before, now, unit=(lambda: None, lambda: None, lambda: None)):
                before(j - 1, 2)
                unit[0]()
                now(j, 0)
                unit[1]()
                now(j, 1)
                unit[2]()

            q, k = normed(0), normed(1)
            plain(0, 0, RANK, True)
            plain(0, 1, RANK, True)
            plain(0, 2, RANK, True)
            q(1, 0)
            q(1, 1)
            n_q = (K0 - Q0) // P
            with dve.Fori(2, 1 + n_q) as j:
                item(j, q, q)
            item(n_q + 1, q, k)
            item(n_q + 2, k, k)
            item(n_q + 3, k, plain)
            item(n_q + 4, plain, plain)
            attend = attend_dve(dve)
            dve.wait_ge(s_tab, 16 * 21)
            dve.wait_ge(s_tables, 1)
            attend.first()
            n_gq = (GK0 - GQ0) // P
            item(J_ATT, plain, scaled, attend.tile(0))
            with dve.Fori(J_ATT + 1, J_ATT + n_gq) as j:
                item(j, scaled, scaled, attend.tile(j - J_ATT))
            item(J_ATT + n_gq, scaled, plain, attend.tile(n_gq))
            with dve.Fori(J_ATT + n_gq + 1, J_DEC) as j:
                item(j, plain, plain, attend.tile(j - J_ATT))
            cached = cached_dve(dve)
            cached.first()
            with dve.Fori(J_DEC, J_GLA) as j:
                item(j, plain, plain, cached.sequence(j - J_DEC))
            linear = linear_dve(dve)
            linear.first()
            item(J_GLA, plain, silu, linear.tile(0))
            with dve.Fori(J_GLA + 1, J_GLA + NTP) as j:
                item(j, silu, silu, linear.tile(j - J_GLA))
            decode = decode_dve(dve, linear)
            item(J_LEV, silu, silu, decode.levels())
            for h in range(N_GLA):
                item(J_LEV + 1 + h, silu, silu, decode.head(h))
            item(J_LEV + 1 + N_GLA, silu, silu, decode.out())
            with dve.Fori(J_LEV + 2 + N_GLA, 1 + N_ITEMS) as j:
                item(j, silu, silu)
            silu(N_ITEMS, 2)


def project_out(nc, sem, dram):
    x_p, x_s, w_out, h_t, o_t, y_p, y_s = dram
    SLOTS = 4
    with ExitStack() as ctx:
        def sb(name, shape, dt=F32):
            return ctx.enter_context(nc.sbuf_tensor(name, shape, dt))

        m_hi = sb("m_hi", [P, KT, TOK], F32R)
        m_lo = sb("m_lo", [P, KT, TOK], F32R)
        w_raw = sb("wo_raw", [P, KT, WCH])
        w_hi = sb("wo_hi", [P, KT, WCH], F32R)
        w_lo = sb("wo_lo", [P, KT, WCH], F32R)
        parts = sb("parts", [P, SLOTS, 2, TN])
        x_res = sb("x_res", [P, 3, WCH])
        y_sb = sb("y_sb", [P, 3, WCH])
        acc = [ctx.enter_context(nc.psum_tensor(f"p2_{i}", [P, 512], F32)) for i in range(3)]

        t_part = [sem(f"t_part{i}") for i in range(SLOTS)]
        t_mul = sem("t_mul")
        t_mhi = sem("t_mhi")
        t_mlo = sem("t_mlo")
        t_w = [sem(f"t_w{i}") for i in range(4)]
        t_whi = sem("t_whi")
        t_wready = sem("t_wready")
        t_wfree = sem("t_wfree")
        t_x = [sem(f"t_x{i}") for i in range(3)]
        t_acc = sem("t_acc")
        t_y = sem("t_y")
        t_st = [sem(f"t_st{i}") for i in range(3)]
        block = ctx.enter_context(nc.Block())
        w_v = w_out.rearrange("(k p) n -> p k n", p=P)

        def load_w(eng, c):
            for q in range(4):
                eng.wait_ge(t_wready, 4 * c + (q + 1))
                eng.dma_start(w_raw[:, 4 * q:4 * q + 4, :], w_v[:, 4 * q:4 * q + 4, ds(c * WCH, WCH)])\
                   .then_inc(t_w[q], 16)

        def rows_of(p, s, t, c):
            if t < NTP:
                return p[t * P:t * P + P, ds(c * WCH, WCH)]
            return s[:, ds(c * WCH, WCH)]

        @block.sync
        def _(sp):
            for q in range(4):
                sp.dma_start(w_raw[:, 4 * q:4 * q + 4, :], w_v[:, 4 * q:4 * q + 4, 0:WCH]).then_inc(t_w[q], 16)

            def load_x(c, t):
                sp.wait_ge(t_y, NT * c + (t + 1))
                sp.dma_start(x_res[:, t % 3, :], rows_of(x_p, x_s, t, c)).then_inc(t_x[t % 3], 16)

            def load_parts(n, k, slot, gate_row):
                sp.wait_ge(t_mlo, k + (KT * n + 1))
                sp.dma_start(parts[:, slot, 0, :], o_t[ds(k * P, P), n * TN:n * TN + TN])\
                  .then_inc(t_part[slot], 16)
                sp.dma_start(parts[:, slot, 1, :], h_t[ds(gate_row, P), PAD + n * TN:PAD + n * TN + TN])\
                  .then_inc(t_part[slot], 16)

            for t in range(3):
                load_x(0, t)
            for n in range(NG):
                for half, base in ((0, GA0), (1, GG0 - KT // 2 * P)):
                    with sp.Fori(2 * half, 2 * half + 2) as k4:
                        for slot in range(SLOTS):
                            k = k4 * SLOTS + slot
                            load_parts(n, k, slot, k * P + base)
            for t in range(3, NT):
                load_x(0, t)
            with sp.Fori(1, NCH) as c:
                for t in range(NT):
                    load_x(c, t)

        @block.scalar
        def _(act):
            act.sem_inc(t_wfree, 4)
            act.sem_inc(t_mlo, SLOTS)

            def split(c):
                for q in range(4):
                    act.wait_ge(t_w[q], 16 * c + 16)
                    act.wait_ge(t_wfree, 4 * c + (q + 1))
                    act.activation(w_hi[:, 4 * q:4 * q + 4, :], w_raw[:, 4 * q:4 * q + 4, :], ACT.Copy)\
                       .then_inc(t_whi, 1)

            def store(c, t):
                act.wait_ge(t_y, NT * c + (t + 4))
                act.dma_start(rows_of(y_p, y_s, t, c), y_sb[:, t % 3, :]).then_inc(t_st[t % 3], 16)

            split(0)
            for n in range(NG):
                with act.Fori(0, KT // SLOTS) as k4:
                    for slot in range(SLOTS):
                        k = k4 * SLOTS + slot
                        act.wait_ge(t_mul, k + (KT * n + 1))
                        act.activation(m_hi[:, ds(k, 1), n * TN:n * TN + TN].rearrange("p a n -> p (a n)"),
                                       parts[:, slot, 0, :], ACT.Copy).then_inc(t_mhi, 1)
            with act.Fori(0, NCH - 1) as c:
                load_w(act, c + 1)
                for t in range(NT - 1):
                    store(c, t)
                split(c + 1)
                store(c, NT - 1)
            for t in range(NT):
                store(NCH - 1, t)
            for i in range(3):
                act.wait_ge(t_st[i], 16 * NCH * NT // 3)

        @block.tensor
        def _(pe):
            with pe.Fori(0, NCH) as c:
                for t in range(NT):
                    if t % 3 == 0:
                        pe.wait_ge(t_mlo, KT * (t // 3 + 1) + SLOTS)
                    pe.wait_ge(t_y, NT * c + (t + 1))
                    out = acc[t % 3][:, 0:WCH]
                    tok = slice(t * P, t * P + P)
                    for k in range(KT):
                        if t == 0 and k % 4 == 0:
                            pe.wait_ge(t_wready, 4 * c + (k // 4 + 5))
                        pe.matmul(out, m_lo[:, k, tok], w_hi[:, k, :], start=(k == 0), stop=False)
                        pe.matmul(out, m_hi[:, k, tok], w_lo[:, k, :], start=False, stop=False)
                        mm = pe.matmul(out, m_hi[:, k, tok], w_hi[:, k, :], start=False, stop=(k == KT - 1))
                        if t == NT - 1 and k % 4 == 3:
                            mm.then_inc(t_wfree, 1)
                    if t < NT - 1:
                        mm.then_inc(t_acc, 1)

        @block.vector
        def _(dve):
            dve.sem_inc(t_y, 3)
            dve.sem_inc(t_wready, 4)

            def split(c):
                for q in range(4):
                    dve.wait_ge(t_whi, 4 * c + (q + 1))
                    dve.tensor_tensor(w_lo[:, 4 * q:4 * q + 4, :], w_raw[:, 4 * q:4 * q + 4, :],
                                      w_hi[:, 4 * q:4 * q + 4, :].bitcast(F32), ALU.subtract).then_inc(t_wready, 1)

            split(0)

            def multiply(n, k4, slot):
                dve.wait_ge(t_part[slot], 32 * k4 + (KT // SLOTS * 32 * n + 32))
                dve.tensor_tensor(parts[:, slot, 0, :], parts[:, slot, 0, :], parts[:, slot, 1, :], ALU.mult)\
                   .then_inc(t_mul, 1)

            def low(n, k4, slot):
                k = k4 * SLOTS + slot
                dve.wait_ge(t_mhi, k + (KT * n + 1))
                m = (slice(None), ds(k, 1), slice(n * TN, n * TN + TN))
                dve.tensor_tensor(m_lo[m].rearrange("p a n -> p (a n)"), parts[:, slot, 0, :],
                                  m_hi[m].rearrange("p a n -> p (a n)").bitcast(F32), ALU.subtract)\
                   .then_inc(t_mlo, 1)

            def prepare(n):
                with dve.Fori(0, KT // SLOTS) as k4:
                    multiply(n, k4, 0)
                    for slot in range(1, SLOTS):
                        multiply(n, k4, slot)
                        low(n, k4, slot - 1)
                    low(n, k4, SLOTS - 1)

            def add(c, t, first=False):
                if t == NT - 1:
                    dve.wait_ge(t_wfree, 4 * c + 8)
                else:
                    dve.wait_ge(t_acc, (NT - 1) * c + (t + 1))
                dve.wait_ge(t_x[t % 3], 48 * c + (16 * (t // 3) + 16))
                if not (first and t < 3):
                    dve.wait_ge(t_st[t % 3], 48 * c + 16 * (t // 3))
                dve.tensor_tensor(y_sb[:, t % 3, :], acc[t % 3][:, 0:WCH], x_res[:, t % 3, :], ALU.add)\
                   .then_inc(t_y, 1)

            prepare(0)
            prepare(1)
            for t in range(NT):
                if t == 3:
                    prepare(2)
                if t == NT - 1:
                    split(1)
                add(0, t, True)
            with dve.Fori(1, NCH - 1) as c:
                for t in range(NT):
                    if t == NT - 1:
                        split(c + 1)
                    add(c, t)
            for t in range(NT):
                add(NCH - 1, t)


def hybrid_step(nc, x_p, x_s, cache_k, cache_v, state, norm_g, w_in, w_up, b_gate, qg, kg, sinks, gla_g, w_out,
                consts, tables, y_p, y_s, win_kp, win_vp, gla_p, win_ks, win_vs, gla_s):
    flat = "a b t g d -> (a b) t (g d)"
    h_t = nc.dram_tensor("h_t", [IN_TOTAL, PAD + TOK], F32, kind="Internal").ap()
    o_t = nc.dram_tensor("o_t", [D_MODEL, TOK], F32, kind="Internal").ap()
    x_p = x_p.rearrange("a t d -> (a t) d")
    x_s = x_s.rearrange("b t d -> (b t) d")
    with ExitStack() as ctx:
        def sem(name):
            return ctx.enter_context(nc.semaphore(name))

        project_in(nc, sem, (x_p, x_s, cache_k.rearrange(flat), cache_v.rearrange(flat), state[0], norm_g,
                             w_in[0], w_up, b_gate, qg, kg, sinks, gla_g, consts, tables,
                             win_kp.rearrange(flat)[0], win_vp.rearrange(flat)[0], gla_p[0, 0],
                             win_ks.rearrange(flat), win_vs.rearrange(flat), gla_s[0], h_t, o_t))
        project_out(nc, sem, (x_p, x_s, w_out[0], h_t, o_t, y_p.rearrange("a t d -> (a t) d"),
                              y_s.rearrange("b t d -> (b t) d")))


def shape_constants():
    import numpy as np

    c = np.zeros((P, C_ALL), np.float32)
    c[:, C_IDENT:C_IDENT + P] = np.eye(P)
    c[:, C_PAIR:C_PAIR + P] = np.kron(np.eye(2), np.ones((HEAD_DIM, HEAD_DIM)))
    c[:, C_SEQ:C_SEQ + DEC_BATCH] = np.kron(np.eye(DEC_BATCH), np.ones((DEC_SEQ, 1)))
    mask = np.zeros((P, 2 * P), np.float32)
    mask[:CHUNK, 3 * CHUNK:] = MASKED
    mask[CHUNK:, :CHUNK] = MASKED
    c[:, C_MASK:] = mask
    mask = mask.copy()
    mask[:, :P] = MASKED
    c[:, C_MASK0:C_MASK] = mask
    m = np.zeros((P, M_ALL), np.float32)
    for i, s in enumerate(LEVELS):
        n = P // (2 * s)
        pairs = np.kron(np.eye(n), np.concatenate([np.ones((s, s)), np.zeros((s, s))]))
        m[:, i * 256:i * 256 + 256] = np.tile(pairs, (1, N_GLA))
    m[:, M_DIAG:M_SCAN] = np.tile(np.eye(P), (1, N_GLA))
    m[:, M_SCAN:M_SCAN_DEC] = np.arange(4 * P) % P > 0
    m[:, M_SCAN_DEC:] = np.arange(4 * P) % DEC_SEQ > 0
    return c, m


_INS = ["x_prompt", "x_sample", "cache_k", "cache_v", "state_gla", "norm_g", "w_in", "w_gate_up", "b_gate",
        "q_norm_g", "k_norm_g", "sinks", "gla_norm_g", "w_out"]
_OUTS = [(1, SEQ, D_MODEL), (DEC_BATCH, DEC_SEQ, D_MODEL),
         (1, 1, CACHE, N_KV, HEAD_DIM), (1, 1, CACHE, N_KV, HEAD_DIM), (1, 1, N_GLA, DK, DV),
         (1, DEC_BATCH, CACHE, N_KV, HEAD_DIM), (1, DEC_BATCH, CACHE, N_KV, HEAD_DIM),
         (1, DEC_BATCH, N_GLA, DK, DV)]


def kernel(**inputs):
    import numpy as _np
    import concourse.bacc as _bacc
    from concourse import mybir as _mybir
    from concourse.bass_utils import run_bass_kernel_spmd as _run

    nc = _bacc.Bacc("TRN2", target_bir_lowering=False, num_devices=1, dynamic_dma_scratch_size=1024)
    consts, tables = shape_constants()
    arrays, args = {}, []
    for name in _INS + ["consts", "tables"]:
        a = consts if name == "consts" else tables if name == "tables" else _np.ascontiguousarray(inputs[name])
        arrays[f"in_{name}"] = a
        args.append(nc.dram_tensor(f"in_{name}", a.shape, _mybir.dt.from_np(a.dtype), kind="ExternalInput").ap())
    for i, shape in enumerate(_OUTS):
        args.append(nc.dram_tensor(f"out_{i}", shape, F32, kind="ExternalOutput").ap())
    hybrid_step(nc, *args)
    r = _run(nc, [arrays], core_ids=[0])
    return tuple(r.results[0][f"out_{i}"] for i in range(len(_OUTS)))
```

```python
from contextlib import ExitStack

import concourse.bass as bass
from concourse import mybir

P = 128
D_MODEL = 2048
SEQ = 1024
DEC_BATCH = 8
DEC_SEQ = 16
CACHE = 128
HEAD_DIM = 64
N_HEADS = 16
N_KV = 4
GQA = N_HEADS // N_KV
N_GLA = 4
DK = 128
DV = 256
RANK = 16
TAU = 16.0
EPS = 1e-6
CHUNK = 64

TOK = SEQ + DEC_BATCH * DEC_SEQ
NT = TOK // P
NTP = SEQ // P
KT = D_MODEL // P
TN = 384
NG = TOK // TN
PAD = P

Q0, K0, V0, GA0, GQ0, GK0, GV0, GG0, LR0 = 0, 1024, 1280, 1536, 2560, 3072, 3584, 4608, 5632
IN_TOTAL = LR0 + RANK
LRR = 2 * RANK

N_QK = (V0 - Q0) // P
N_PLAIN = (GA0 - Q0 + GG0 - GQ0) // P
N_ITEMS = (IN_TOTAL - RANK) // P
J_ATT = 1 + (GA0 - Q0) // P
J_DEC = J_ATT + NTP
J_GLA = 1 + N_PLAIN
J_LEV = J_GLA + NTP
SLOTS = 4
WCH = 256
NCH = D_MODEL // WCH
LEVELS = (64, 32, 16, 8, 4, 2, 1)
DEC_LEVELS = (8, 4, 2, 1)

F32 = mybir.dt.float32
F32R = mybir.dt.float32r
U8 = mybir.dt.uint8
ALU = mybir.AluOpType
ACT = mybir.ActivationFunctionType
AX = mybir.AxisListType
ds = bass.ds


C_IDENT, C_PAIR, C_SEQ, C_MASK0 = 0, P, 2 * P, 2 * P + DEC_BATCH
C_MASK = C_MASK0 + 2 * P
C_ALL = C_MASK + 2 * P
M_DIAG = len(LEVELS) * 256
M_SCAN = M_DIAG + 4 * P
M_SCAN_DEC = M_SCAN + 4 * P
M_ALL = M_SCAN_DEC + 4 * P
MASKED = -1.0e30


def project(nc, sem, dram):
    (x_p, x_s, cache_k, cache_v, state, norm_g, w_in, w_up, b_gate, qg, kg, sinks, gla_g, consts, tables,
     win_kp, win_vp, gla_p, win_ks, win_vs, gla_s, h_t, o_t, w_out, y_p, y_s) = dram
    with ExitStack() as ctx:
        def sb(name, shape, dt=F32):
            return ctx.enter_context(nc.sbuf_tensor(name, shape, dt))

        x_hi = sb("x_hi", [P, KT, TOK], F32R)
        x_lo = sb("x_lo", [P, KT, TOK], F32R)
        raw = sb("raw", [P, D_MODEL])
        w_hi = sb("w_hi", [P, KT, P], F32R)
        w_lo = sb("w_lo", [P, KT, P], F32R)
        xn = sb("xn", [P, D_MODEL])
        work = sb("work", [P, 9216])
        sq_parts = sb("sq_parts", [P, 2 * TN + P], F32R)
        consts_sb = sb("consts_sb", [P, C_MASK0])
        tables_sb = sb("tables_sb", [P, M_ALL], U8)
        w_up_sb = sb("w_up_sb", [LRR + 1, N_GLA * DK])
        lr = sb("lr", [LRR + 1, P])
        sink_row = sb("sink_row", [P, N_HEADS])
        sink_dec = sb("sink_dec", [P, 2])
        gq_col = sb("gq_col", [P, 2])
        gn_col = sb("gn_col", [P, 2])
        small = sb("small", [P, 96])
        mhalf, zeros = small[:, 92:93], small[:, 93:94]
        ident = consts_sb[:, C_IDENT:C_IDENT + P]
        ones_pair = consts_sb[:, C_PAIR:C_PAIR + P]
        seq_col = consts_sb[:, C_SEQ:C_SEQ + DEC_BATCH]
        x_buf = [work[:, 0:D_MODEL], raw[:, :], xn[:, :]]
        g_row = work[:, D_MODEL:2 * D_MODEL]
        squares = work[:, 2 * D_MODEL:3 * D_MODEL]
        sq_hi, sq_lo = (sq_parts[:, TN * i:TN * i + TN] for i in range(2))
        ones_r = sq_parts[:, 2 * TN:2 * TN + P]
        lr_raw = work[:, 4 * D_MODEL:4 * D_MODEL + KT * RANK].rearrange("p (k n) -> p k n", n=RANK)
        ss, var, rstd = small[:, 0:2], small[:, 2:3], small[:, 3:4]
        stage = [xn[:, TN * n:TN * n + TN] for n in range(3)]
        tmp_a = xn[:, 3 * TN:4 * TN]
        tmp_b = xn[:, 4 * TN:5 * TN]

        banks = [ctx.enter_context(nc.psum_tensor(f"p1_{i}", [P, 512], F32)) for i in range(8)]
        acc = banks[0:3]
        xt_bank = banks[3:7]
        ss_bank = banks[7]
        ub = banks[3:8]

        s_norm = sem("s_norm")
        s_ident = sem("s_ident")
        s_const = sem("s_const")
        s_x = [sem(f"s_x{i}") for i in range(3)]
        s_w = [sem(f"s_w{i}") for i in range(4)]
        s_ss = sem("s_ss")
        s_var = sem("s_var")
        s_rstd = sem("s_rstd")
        s_xn = sem("s_xn")
        s_xt = sem("s_xt")
        s_xhi = sem("s_xhi")
        s_xlo = sem("s_xlo")
        s_mh = sem("s_mh")
        s_whi = sem("s_whi")
        s_wready = sem("s_wready")
        s_wfree = sem("s_wfree")
        s_acc = sem("s_acc")
        s_staged = sem("s_staged")
        s_store = [sem(f"s_store{i}") for i in range(3)]
        s_gate = [sem(f"s_gate{i}") for i in range(3)]
        s_sq = sem("s_sq")
        s_sqhi = sem("s_sqhi")
        s_sqlo = sem("s_sqlo")
        s_ones = sem("s_ones")
        s_ssq = sem("s_ssq")
        s_v = sem("s_v")
        s_sd = sem("s_sd")
        s_nchain = sem("s_nchain")
        s_sig = sem("s_sig")
        s_schain = sem("s_schain")
        s_zero = sem("s_zero")
        s_zst = sem("s_zst")
        s_tab = sem("s_tab")
        s_win = sem("s_win")
        s_tload = sem("s_tload")
        s_tables = sem("s_tables")
        sa_dv = sem("sa_dv")
        sa_e = sem("sa_e")
        sa_k = sem("sa_k")
        sa_mask = sem("sa_mask")
        sa_max = sem("sa_max")
        sa_mk = sem("sa_mk")
        sa_neg = sem("sa_neg")
        sa_o = sem("sa_o")
        sa_out = sem("sa_out")
        sa_p = sem("sa_p")
        sa_pt = sem("sa_pt")
        sa_q = sem("sa_q")
        sa_s = sem("sa_s")
        sa_st = sem("sa_st")
        sa_t = sem("sa_t")
        sa_v = sem("sa_v")
        sa_vtok = sem("sa_vtok")
        sa_vtr = sem("sa_vtr")
        sb_av = sem("sb_av")
        sb_ck = sem("sb_ck")
        sb_cv = sem("sb_cv")
        sb_dv = sem("sb_dv")
        sb_e = sem("sb_e")
        sb_in = sem("sb_in")
        sb_ks = sem("sb_ks")
        sb_kt = sem("sb_kt")
        sb_neg = sem("sb_neg")
        sb_new = sem("sb_new")
        sb_oc = sem("sb_oc")
        sb_pc = sem("sb_pc")
        sb_pr = sem("sb_pr")
        sb_pt = sem("sb_pt")
        sb_s = sem("sb_s")
        sb_w = sem("sb_w")
        sb_xc = sem("sb_xc")
        sb_xt = sem("sb_xt")
        sd_ds = sem("sd_ds")
        sd_gp = sem("sd_gp")
        sd_in = [sem(f"sd_in{i}") for i in range(2)]
        sd_k = sem("sd_k")
        sd_out = [sem(f"sd_out{i}") for i in range(2)]
        sd_q = sem("sd_q")
        sd_up = sem("sd_up")
        sl_a = sem("sl_a")
        sl_b = sem("sl_b")
        sl_cp = sem("sl_cp")
        sl_d = sem("sl_d")
        sl_dcp = sem("sl_dcp")
        sl_dg = sem("sl_dg")
        sl_ds = sem("sl_ds")
        sl_eb = sem("sl_eb")
        sl_ex = sem("sl_ex")
        sl_gt = sem("sl_gt")
        sl_ini = sem("sl_ini")
        sl_k = sem("sl_k")
        sl_kt = sem("sl_kt")
        sl_ktok = sem("sl_ktok")
        sl_la = sem("sl_la")
        sl_lnv = sem("sl_lnv")
        sl_log = sem("sl_log")
        sl_lr = sem("sl_lr")
        sl_nt = sem("sl_nt")
        sl_o = sem("sl_o")
        sl_og = sem("sl_og")
        sl_on = sem("sl_on")
        sl_p = sem("sl_p")
        sl_q = sem("sl_q")
        sl_rs = sem("sl_rs")
        sl_sq = sem("sl_sq")
        sl_st = sem("sl_st")
        sl_up = sem("sl_up")
        sl_v = sem("sl_v")
        sl_var = sem("sl_var")
        sl_vtok = sem("sl_vtok")
        sl_vtr = sem("sl_vtr")
        sl_zz = sem("sl_zz")
        t_piece = [sem(f"t_piece{i}") for i in range(SLOTS)]
        t_dec = sem("t_dec")
        t_mul = sem("t_mul")
        t_mhi = sem("t_mhi")
        t_mlo = sem("t_mlo")
        t_w = [sem(f"t_w{i}") for i in range(2)]
        t_whi = sem("t_whi")
        t_wready = sem("t_wready")
        t_wfree = sem("t_wfree")
        t_x = [sem(f"t_x{i}") for i in range(NT)]
        t_acc = sem("t_acc")
        t_y = sem("t_y")
        t_st = [sem(f"t_st{i}") for i in range(3)]
        block = ctx.enter_context(nc.Block())

        def pieces():
            return [(q, n, i) for q in range(4) for n in range(NG) for i in range(2)]

        o_w = w_out.rearrange("(k p) n -> p k n", p=P)
        o_raw = [raw[:, s * 1024:s * 1024 + 1024] for s in range(2)]
        o_hi = [w_hi[:, 8 * s:8 * s + 8, :] for s in range(2)]
        o_lo = [w_lo[:, 8 * s:8 * s + 8, :] for s in range(2)]
        piece_sb = work[:, 0:3072].rearrange("p (s k n) -> p s k n", s=SLOTS, k=2)
        o_dec = work[:, 3072:4096].rearrange("p (k n) -> p k n", n=P)
        x_res = work[:, 4096:6400].rearrange("p (t n) -> p t n", n=WCH)
        y_sb = work[:, 6400:7168].rearrange("p (t n) -> p t n", n=WCH)

        def rows_of(p, s, t, c):
            if t < NTP:
                return p[t * P:t * P + P, ds(c * WCH, WCH)]
            return s[:, ds(c * WCH, WCH)]

        def is_gated_late(q, n):
            return q >= 2 and n == NG - 1
        w_v = w_in.rearrange("(k p) n -> p k n", p=P)

        def w_raw(k, n):
            if n == RANK:
                return lr_raw[:, k:k + 4, :]
            return raw[:, k * P:k * P + 4 * P].rearrange("p (k n) -> p k n", k=4)

        RUNS = [(1, J_ATT, Q0, None, None), (J_ATT, J_GLA, GQ0, None, 0), (J_GLA, J_LEV, GA0, 0, 1),
                (J_LEV, 1 + N_ITEMS, GG0, 1, None)]

        @block.sync
        def _(sp):
            def load_x(t):
                if t >= 3:
                    sp.wait_ge(s_xt, 4 * (t - 2) + 4)
                sp.dma_start(x_buf[t % 3], x_p[t * P:t * P + P, :] if t < NTP else x_s).then_inc(s_x[t % 3], 16)

            load_x(0)
            sp.dma_start(g_row, norm_g[0:1, :].to_broadcast([P, D_MODEL])).then_inc(s_norm, 16)
            load_x(1)
            sp.dma_start(consts_sb[:, :], consts[:, 0:C_MASK0]).then_inc(s_ident, 16)
            load_x(2)
            for half in range(2):
                rows = slice(half * HEAD_DIM, half * HEAD_DIM + HEAD_DIM)
                sp.dma_start(gq_col[rows, 0:1], qg.rearrange("a d -> d a")).then_inc(s_const, 16)
                sp.dma_start(gq_col[rows, 1:2], kg.rearrange("a d -> d a")).then_inc(s_const, 16)
            for q in range(4):
                sp.dma_start(w_raw(4 * q, RANK), w_v[:, 4 * q:4 * q + 4, LR0:LR0 + RANK]).then_inc(s_w[q], 16)
            for t in range(3, NT):
                load_x(t)
            for half in range(2):
                sp.dma_start(w_up_sb[half * RANK:half * RANK + RANK, :], w_up[0]).then_inc(s_tab, 16)
            sp.dma_start(w_up_sb[LRR:LRR + 1, :], b_gate).then_inc(s_tab, 16)
            for e in range(2):
                sp.dma_start(gn_col[:, e:e + 1], gla_g[:, e * P:e * P + P].rearrange("a p -> p a")).then_inc(s_tab, 16)
            sp.dma_start(sink_row[:, :], sinks.to_broadcast([P, N_HEADS])).then_inc(s_tab, 16)
            for half in range(2):
                for gp in range(2):
                    for r in range(GQA):
                        rows = slice(half * HEAD_DIM + r * DEC_SEQ, half * HEAD_DIM + r * DEC_SEQ + DEC_SEQ)
                        h = (2 * gp + half) * GQA + r
                        sp.dma_start(sink_dec[rows, gp:gp + 1],
                                     sinks[0:1, h:h + 1].to_broadcast([DEC_SEQ, 1])).then_inc(s_tab, 16)

            def load_w(j, col, n):
                for q in range(4):
                    if type(j) is int and j == 1:
                        sp.wait_ge(s_xt, 4 * NTP + 4)
                    else:
                        sp.wait_ge(s_wready, 4 * j + (q - 3))
                    sp.dma_start(w_raw(4 * q, n), w_v[:, 4 * q:4 * q + 4, ds(col, n)]).then_inc(s_w[q], 16)

            def out_loads():
                def load_w_out(c, q):
                    sp.wait_ge(t_wready, 4 * c + (q + 1))
                    sp.dma_start(o_raw[q % 2].rearrange("p (k n) -> p k n", n=WCH),
                                 o_w[:, 4 * (q % 4):4 * (q % 4) + 4, ds(c * WCH + (q // 4) * WCH, WCH)])\
                      .then_inc(t_w[q % 2], 16)

                def load_x_res(c, t):
                    sp.wait_ge(t_y, NT * c + (t + 1))
                    sp.dma_start(x_res[:, t, :], rows_of(x_p, x_s, t, c)).then_inc(t_x[t], 16)

                def load_pieces(first, last):
                    for p, (q, n, i) in list(enumerate(pieces()))[first:last]:
                        k = 4 * q + 2 * i
                        row = k * P + (GA0 if q < 2 else GG0 - D_MODEL // 2)
                        if p >= SLOTS:
                            sp.wait_ge(t_mlo, p + 1)
                        sp.wait_ge(s_store[n], 16 * (J_GLA + k + 2))
                        sp.dma_start(piece_sb[:, p % SLOTS, :, :], h_t[row:row + 2 * P, PAD + n * TN:PAD + n * TN + TN]
                                     .rearrange("(k p) n -> p k n", p=P)).then_inc(t_piece[p % SLOTS], 16)

                def store_last(n):
                    sp.wait_ge(s_staged, N_ITEMS * NG + (n + 4))
                    sp.dma_start(h_t[LR0 - P:LR0, PAD + n * TN:PAD + n * TN + TN], stage[n]).then_inc(s_store[n], 16)

                for half in range(2):
                    sp.wait_ge(sd_out[half], 16 * N_GLA)
                sp.wait_ge(sd_gp, 16)
                sp.wait_ge(sl_st, 16 * (NT + 1))
                load_pieces(0, 4)
                sp.wait_ge(s_wready, 4 * (N_ITEMS + 1))
                load_w_out(0, 0)
                load_w_out(0, 1)
                store_last(0)
                store_last(1)
                load_pieces(4, 6)
                sp.dma_start(o_dec, o_t[D_MODEL // 2:D_MODEL, SEQ:TOK].rearrange("(k p) n -> p k n", p=P))\
                  .then_inc(t_dec, 16)
                store_last(2)
                load_pieces(6, 12)
                load_w_out(0, 2)
                load_pieces(12, 18)
                load_w_out(0, 3)
                load_pieces(18, 24)
                for t in range(NT):
                    load_x_res(0, t)
                with sp.Fori(0, NCH - 1) as c:
                    for q in range(4, 7):
                        load_w_out(c, q)
                    for t in range(NT):
                        load_x_res(c + 1, t)
                    load_w_out(c, 7)

            def store_item(j, row, n_rows, gates=None):
                for n in range(NG):
                    sp.wait_ge(s_staged, j * NG + (n + 4))
                    sp.dma_start(h_t[ds(row, n_rows), PAD + n * TN:PAD + n * TN + TN],
                                 stage[n][0:n_rows, :]).then_inc(s_store[n], 16)
                    if gates is None:
                        continue
                    n_tok = TN
                    if gates == 0:
                        sp.wait_ge(sa_st, 16 * (4 * NTP + 1))
                        sp.wait_ge(sb_w, 16 * 5)
                    else:
                        sp.wait_ge(sl_st, 16 * (min(3 * n + 3, NTP) + 1))
                        n_tok = min(TN, SEQ - n * TN)
                    sp.wait_ge(s_store[n], 16 * j + 16)
                    sp.dma_start(stage[n][:, 0:n_tok], o_t[ds(j * P + (P - J_GLA * P), P), n * TN:n * TN + n_tok])\
                      .then_inc(s_gate[n], 16)

            load_w(1, Q0, P)
            sp.wait_ge(s_ss, NT)
            sp.dma_start(work[:, 2 * D_MODEL:2 * D_MODEL + M_ALL], tables).then_inc(s_tload, 16)
            sp.wait_ge(s_zero, 1)
            for r in range(K0 // P, GA0 // P):
                sp.dma_start(h_t[r * P:r * P + P, 0:PAD], xn[:, 5 * TN:5 * TN + PAD]).then_inc(s_zst, 16)
            store_item(0, LR0, LRR)
            old = CACHE - DEC_SEQ
            sp.dma_start(win_ks[:, 0:old, :], cache_k[:, DEC_SEQ:CACHE, :]).then_inc(s_win, 16)
            sp.dma_start(win_vs[:, 0:old, :], cache_v[:, DEC_SEQ:CACHE, :]).then_inc(s_win, 16)
            for i, (j0, j1, col, gates, next_gates) in enumerate(RUNS):
                with sp.Fori(j0, j1 - 1) as j:
                    load_w(j + 1, (j - j0) * P + (col + P), P)
                    store_item(j, (j - j0) * P + col, P, gates)
                if i + 1 < len(RUNS):
                    load_w(j1, RUNS[i + 1][2], P)
                    store_item(j1 - 1, (j1 - 1 - j0) * P + col, P, next_gates)
            out_loads()
            sp.wait_ge(s_zst, 16 * (GA0 - K0) // P)
            sp.wait_ge(s_win, 32)
            for n in range(NG):
                sp.wait_ge(s_store[n], 16 * (N_ITEMS + 1))

        def wait_acc(eng, j, n):
            if n == NG - 1:
                eng.wait_ge(s_wfree, 4 * j + 8)
            else:
                eng.wait_ge(s_acc, 2 * j + (n + 1))

        def split(pool, j, n=P):
            for k in range(0, KT, 4):
                pool.wait_ge(s_w[k // 4], 16 * j + 16)
                pool.wait_ge(s_wfree, 4 * j + (k // 4 + 1))
                pool.tensor_tensor(w_hi[:, k:k + 4, 0:n], w_raw(k, n), zeros[:, :].unsqueeze(1)
                                   .to_broadcast([P, 4, n]), ALU.add).then_inc(s_whi, 1)
                pool.wait_ge(s_whi, 4 * j + (k // 4 + 1))
                lo = w_hi[:, k:k + 4, RANK:LRR] if n == RANK else w_lo[:, k:k + 4, 0:n]
                pool.tensor_tensor(lo, w_raw(k, n), w_hi[:, k:k + 4, 0:n].bitcast(F32),
                                   ALU.subtract).then_inc(s_wready, 1)

        a_q = work[:, 0:1024].rearrange("p (c n) -> p c n", c=8)
        a_k = work[:, 1024:2048].rearrange("p (g n) -> p g n", g=N_KV)
        a_v = work[:, 2048:2560].rearrange("p (c n) -> p c n", c=2)
        a_vtok = work[:, 2560:3072].rearrange("p (k n) -> p k n", k=2)
        a_p = work[:, 3072:4096].rearrange("p (r n) -> p r n", r=GQA)
        a_pt = work[:, 4096:5120].rearrange("p (k n) -> p k n", k=2)
        a_o = work[0:HEAD_DIM, 5120:5632]
        a_mask = work[:, 5632:6144].rearrange("p (m n) -> p m n", m=2)
        a_mx, a_neg, a_sk, a_es, a_sum, a_den = (small[:, 8 + 4 * i:12 + 4 * i] for i in range(6))
        bank_s, bank_t, bank_o = ub[0:2], ub[2:4], ub[4]

        def attend_pe(pe, t, later=0):
            def values():
                pe.wait_ge(sa_v, 16 * t + 16)
                for kt in range(2):
                    for c in range(2):
                        mm = pe.transpose(bank_t[0][:, kt * 256 + c * P:kt * 256 + c * P + P],
                                          a_v[:, c, kt * P:kt * P + P], ident)
                mm.then_inc(sa_vtr, 1)

            def scores(g):
                pe.wait_ge(sa_q, 16 * t + 16)
                pe.wait_ge(sa_k, 32 * t + 32)
                pe.wait_ge(sa_max, 16 * t + (4 * g + 1))
                for half in range(2):
                    rows = slice(half * HEAD_DIM, half * HEAD_DIM + HEAD_DIM)
                    for i in range(2):
                        mm = pe.matmul(bank_s[half][:, i * 256:i * 256 + 256],
                                       a_q[rows, 2 * g + i, :], a_k[rows, g, :], start=True, stop=True)
                    mm.then_inc(sa_s, 1)

            def turn(g):
                pe.wait_ge(sa_p, 16 * t + (4 * g + 4))
                pe.wait_ge(sa_pt, 8 * t + (2 * g + 1))
                pe.wait_ge(sa_vtok, t + 1)
                for kt in range(2):
                    for r in range(GQA):
                        mm = pe.transpose(bank_t[kt][:, r * P:r * P + P], a_p[:, r, kt * P:kt * P + P], ident)
                    mm.then_inc(sa_t, 1)

            def outputs(g):
                pe.wait_ge(sa_pt, 8 * t + (2 * g + 3))
                pe.wait_ge(sa_out, 4 * t + (g + 1))
                for kt in range(2):
                    mm = pe.matmul(bank_o[0:HEAD_DIM, :], a_vtok[:, kt, g * HEAD_DIM:g * HEAD_DIM + HEAD_DIM],
                                   a_pt[:, kt, :], start=(kt == 0), stop=(kt == 1))
                mm.then_inc(sa_o, 1)

            def at(*stages):
                return lambda: [f(*a) for f, *a in stages]

            stages = {4: at((values,), (scores, 0)), 14: at((turn, 0), (scores, 1)), 16: at((outputs, 0)),
                      22: at((turn, 1), (scores, 2)), 24: at((outputs, 1)),
                      31: at((turn, 2), (scores, 3)), 33: at((outputs, 2)),
                      39: at((turn, 3)), 41: at((outputs, 3))}
            return {step + later * (41 - step) // 37: stage for step, stage in stages.items()}

        class attend_act:

            def __init__(self, act):
                self.act = act

            def load(self, t):
                act = self.act
                act.dma_start(a_q, h_t[Q0:K0, ds(t * P + PAD, P)].rearrange("(c p) n -> p c n", p=P))\
                   .then_inc(sa_q, 16)
                for half in range(2):
                    act.dma_start(a_k[half * HEAD_DIM:half * HEAD_DIM + HEAD_DIM, :, :],
                                  h_t[K0:V0, ds(t * P, 2 * P)].rearrange("(g p) n -> p g n", p=HEAD_DIM))\
                       .then_inc(sa_k, 16)
                act.dma_start(a_v, h_t[V0:GA0, ds(t * P, 2 * P)].rearrange("(c p) n -> p c n", p=P))\
                   .then_inc(sa_v, 16)

            def first(self):
                self.act.sem_inc(sa_pt, 1)
                self.act.sem_inc(sa_out, 1)
                self.act.dma_start(a_mask, consts[:, C_MASK0:C_ALL].rearrange("p (m n) -> p m n", m=2))\
                    .then_inc(sa_mask, 16)
                self.act.dma_start(a_o[:, 0:2], consts[0:HEAD_DIM, 0:2]).then_inc(sa_st, 16)
                for n in range(NG):
                    self.act.wait_ge(s_store[n], 16 * J_ATT)
                self.act.wait_ge(s_zst, 16 * (GA0 - K0) // P)
                self.load(0)

            def exps(self, t, g):
                act = self.act
                act.wait_ge(sa_neg, 4 * t + (g + 1))
                act.activation(a_es, a_sk, ACT.Exp).then_inc(sa_e, 1)
                for r in range(GQA):
                    act.activation(a_p[:, r, :], a_p[:, r, :], ACT.Exp, bias=a_neg[:, r:r + 1],
                                   accum_out=a_sum[:, r:r + 1]).then_inc(sa_e, 1)

            def copy_probs(self, t, g):
                for kt in range(2):
                    self.act.wait_ge(sa_t, 8 * t + (2 * g + kt + 1))
                    self.act.activation(a_pt[:, kt, :], bank_t[kt][:, :], ACT.Copy).then_inc(sa_pt, 1)

            def copy_out(self, t, g):
                act = self.act
                act.wait_ge(sa_o, 4 * t + (g + 1))
                act.wait_ge(sa_st, 64 * t + 16 * (g + 1))
                act.activation(a_o, bank_o[0:HEAD_DIM, :], ACT.Copy).then_inc(sa_out, 1)
                act.wait_ge(sa_out, 4 * t + (g + 2))
                act.dma_start(o_t[g * 256:g * 256 + 256, ds(t * P, P)].rearrange("(r d) n -> d r n", d=HEAD_DIM),
                              a_o.rearrange("p (r n) -> p r n", r=GQA)).then_inc(sa_st, 16)

            def tile(self, t):
                def part_0():
                    self.act.wait_ge(sa_vtr, t + 1)
                    self.act.activation(a_vtok, bank_t[0][:, :].rearrange("p (k n) -> p k n", k=2), ACT.Copy)\
                        .then_inc(sa_vtok, 1)
                    self.exps(t, 0)
                    self.copy_probs(t, 0)
                    self.exps(t, 1)

                def part_1():
                    self.copy_out(t, 0)
                    self.copy_probs(t, 1)
                    self.exps(t, 2)
                    self.copy_out(t, 1)
                    self.copy_probs(t, 2)
                    self.exps(t, 3)

                def part_2():
                    self.copy_out(t, 2)
                    self.copy_probs(t, 3)
                    if not (type(t) is int and t == NTP - 1):
                        self.load(t + 1)
                    self.copy_out(t, 3)
                return part_0, part_1, part_2

        class attend_dve:

            def __init__(self, dve):
                self.dve = dve

            def first(self):
                self.dve.sem_inc(sa_max, 1)
                self.dve.sem_inc(sa_mk, 1)
                self.dve.wait_ge(sa_mask, 16)

            def softmax(self, t, g):
                dve = self.dve
                dve.wait_ge(sa_mk, t + 1)
                dve.wait_ge(sa_pt, 8 * t + (2 * g + 1))
                for r in (0, 2, 1, 3):
                    h = GQA * g + r
                    if r < 2:
                        dve.wait_ge(sa_s, 8 * t + (2 * g + r + 1))
                        dve.nop(nofuse=True)
                    dve.tensor_tensor_reduce(
                        out=a_p[:, r, :], in0=bank_s[r % 2][:, (r // 2) * 256:(r // 2) * 256 + 256],
                        in1=a_mask[:, 0, :], scale=1.0, scalar=sink_row[:, h:h + 1], op0=ALU.add, op1=ALU.max,
                        accum_out=a_mx[:, r:r + 1]).then_inc(sa_max, 1)
                dve.wait_ge(sa_max, 16 * t + (4 * g + 5))
                dve.tensor_scalar(a_neg, a_mx, -1.0, None, ALU.mult).then_inc(sa_dv, 1)
                dve.wait_ge(sa_dv, 12 * t + (3 * g + 1))
                dve.tensor_tensor(a_sk, sink_row[:, GQA * g:GQA * g + GQA], a_neg, ALU.add).then_inc(sa_neg, 1)
                dve.wait_ge(sa_e, 20 * t + (5 * g + 5))
                dve.tensor_tensor(a_den, a_sum, a_es, ALU.add).then_inc(sa_dv, 1)
                dve.wait_ge(sa_dv, 12 * t + (3 * g + 2))
                dve.reciprocal(a_den, a_den).then_inc(sa_dv, 1)
                dve.wait_ge(sa_dv, 12 * t + (3 * g + 3))
                for r in range(GQA):
                    dve.tensor_scalar(a_p[:, r, :], a_p[:, r, :], a_den[:, r:r + 1], None, ALU.mult)\
                       .then_inc(sa_p, 1)

            def tile(self, t):
                def part_0():
                    self.softmax(t, 0)
                    self.softmax(t, 1)

                def part_1():
                    self.softmax(t, 2)
                    self.softmax(t, 3)

                def part_2():
                    self.dve.tensor_copy(a_mask[:, 0, :], a_mask[:, 1, :]).then_inc(sa_mk, 1)
                return part_0, part_1, part_2

        def four(x):
            return x.rearrange("p (h n) -> p h n", h=N_GLA)

        l_q, l_k = work[:, 0:512], work[:, 512:1024]
        l_v = work[:, 1024:2048]
        l_vtok = work[:, 2048:3072]
        l_b = work[:, 3072:3584]
        l_e = [work[:, 3584:4096], work[:, 4096:4608]]
        l_z = [work[:, 4608:5120], work[:, 5120:5632]]
        l_att = work[:, 5632:6144]
        l_qe = work[:, 6144:6656]
        l_ktok = work[:, 6656:7168]
        l_s = work[:, 7168:8192]
        l_og = work[:, 8192:9216]
        l_o = l_v
        l_eb = small[:, 40:72]
        l_ss, l_var, l_rstd = small[:, 76:80], small[:, 80:84], small[:, 84:88]
        NZ = 2 + len(LEVELS)

        def halves(x, s):
            return x.rearrange("p (n two s) -> p n two s", two=2, s=s)

        def linear_stages(pe, t, dec=False):
            levels = DEC_LEVELS if dec else LEVELS

            def logits():
                pe.wait_ge(sl_lr, 16 * t + 16)
                pe.wait_ge(sl_up, 4 * t + 1)
                for h in range(N_GLA):
                    mm = pe.matmul(ub[0][:, h * P:h * P + P], w_up_sb[:, h * P:h * P + P], lr[:, :],
                                   start=True, stop=True)
                mm.then_inc(sl_log, 1)

            def values():
                pe.wait_ge(sl_v, 16 * t + 16)
                pe.wait_ge(sl_on, 4 * t + 1)
                for c in range(8):
                    mm = pe.transpose(ub[1 + c // 4][:, (c % 4) * P:(c % 4) * P + P], l_v[:, c * P:c * P + P], ident)
                    if c % 4 == 3:
                        mm.then_inc(sl_vtr, 1)

            def diagonal():
                pe.wait_ge(sl_q, 16 * t + 16)
                pe.wait_ge(sl_k, 16 * t + 16)
                pe.wait_ge(sl_la, t + 1)
                for h in range(N_GLA):
                    hs = slice(h * P, h * P + P)
                    mm = pe.matmul(ub[0][:, hs], l_k[:, hs], l_q[:, hs], start=True, stop=True)
                mm.then_inc(sl_dg, 1)

            def keys():
                pe.wait_ge(sl_zz, NZ * t + 2)
                pe.wait_ge(sl_og, 4 * t + 1)
                for h in range(N_GLA):
                    mm = pe.transpose(ub[3][:, h * P:h * P + P], l_z[0][:, h * P:h * P + P], ident)
                mm.then_inc(sl_kt, 1)

            def level(i):
                s = levels[i]
                pe.wait_ge(sl_zz, NZ * t + (i + 3))
                if i == 1:
                    pe.wait_ge(sl_ktok, t + 1)
                if i >= 2:
                    pe.wait_ge(sl_cp, len(LEVELS) * t + (i - 1))
                for h in range(N_GLA):
                    z = l_z[(i + 1) % 2][:, h * P:h * P + P]
                    mm = pe.matmul(ub[4 - i % 2][:, h * 64:h * 64 + 64], z, halves(z, s)[:, :, 1, :],
                                   start=True, stop=True)
                mm.then_inc(sl_p, 1)

            def outputs():
                pe.wait_ge(sl_cp, len(LEVELS) * t + len(levels))
                pe.wait_ge(sl_dcp, t + 1)
                pe.wait_ge(sl_vtok, 2 * t + 2)
                for h in range(N_GLA):
                    hs = slice(h * P, h * P + P)
                    out = ub[1 + h // 2][:, (h % 2) * DV:(h % 2) * DV + DV]
                    pe.matmul(out, l_att[:, hs], l_vtok[:, h * DV:h * DV + DV], start=True, stop=False)
                    mm = pe.matmul(out, l_qe[:, hs], l_s[:, h * DV:h * DV + DV], start=False, stop=True)
                    if h % 2:
                        mm.then_inc(sl_o, 1)
                pe.wait_ge(sl_ktok, t + 1)
                for h in range(N_GLA):
                    hs = slice(h * P, h * P + P)
                    mm = pe.matmul(ub[4 * (h // 2)][:, (h % 2) * DV:(h % 2) * DV + DV], l_ktok[:, hs],
                                   l_vtok[:, h * DV:h * DV + DV], start=True, stop=True)
                    if h % 2:
                        mm.then_inc(sl_ds, 1)

            def turn(decoded=False):
                if not decoded:
                    pe.wait_ge(sl_up, 4 * t + 5)
                for c in range(8):
                    if c % 2 == 0:
                        pe.wait_ge(sl_on, 4 * t + (c // 2 + 2))
                    mm = pe.transpose(ub[3 + c // 4][:, (c % 4) * P:(c % 4) * P + P], l_o[:, c * P:c * P + P], ident)
                    if c % 4 == 3:
                        mm.then_inc(sl_gt, 1)
            return logits, values, diagonal, keys, level, outputs, turn

        def linear_pe(pe, t, first=False):
            logits, values, diagonal, keys, level, outputs, _ = linear_stages(pe, t)
            stages = {6: logits, 14: diagonal, 22: keys, 30: values, 47: outputs}
            if not first:
                stages[9] = linear_stages(pe, t - 1)[-1]
            for i, step in enumerate((23, 25, 28, 32, 35, 38, 42)):
                stages[step] = lambda i=i: level(i)
            return stages

        class linear_act:
            def __init__(self, act):
                self.act = act

            def load(self, t):
                act = self.act
                cols = ds(t * P + PAD, P)
                act.dma_start(lr[0:LRR, :], h_t[LR0:LR0 + LRR, cols]).then_inc(sl_lr, 16)
                act.dma_start(four(l_q), h_t[GQ0:GK0, cols].rearrange("(c p) n -> p c n", p=P)).then_inc(sl_q, 16)
                act.dma_start(four(l_k), h_t[GK0:GV0, cols].rearrange("(c p) n -> p c n", p=P)).then_inc(sl_k, 16)

            def load_v(self, t):
                act = self.act
                if type(t) is int and t == 0:
                    for n in range(NG):
                        act.wait_ge(s_store[n], 16 * J_GLA)
                cols = ds(t * P + PAD, P)
                act.dma_start(l_v.rearrange("p (c n) -> p c n", c=8),
                              h_t[GV0:GG0, cols].rearrange("(c p) n -> p c n", p=P)).then_inc(sl_v, 16)

            def first(self):
                act = self.act
                act.wait_ge(sl_ini, 3)
                for n in range(NG):
                    act.wait_ge(s_store[n], 16 * (J_ATT + (GV0 - GQ0) // P))
                act.dma_start(l_og[:, 0:2], consts[:, 0:2]).then_inc(sl_st, 16)
                self.load(0)
                act.sem_inc(sl_og, 1)

            def exp(self, t, i, out, in_, scale):
                self.act.activation(out, in_, ACT.Exp, scale=scale / TAU).then_inc(sl_ex, 1)

            def gates(self, t):
                act = self.act
                act.wait_ge(sl_log, t + 1)
                act.activation(l_e[0], ub[0][:, :], ACT.Abs).then_inc(sl_a, 1)
                act.wait_ge(sl_a, 3 * t + 1)
                act.activation(l_e[0], l_e[0], ACT.Exp, scale=-1.0).then_inc(sl_a, 1)
                act.wait_ge(sl_a, 3 * t + 2)
                act.activation(l_e[0], l_e[0], ACT.Ln, bias=1.0).then_inc(sl_a, 1)

            def values(self, t):
                act = self.act
                for i in range(2):
                    act.wait_ge(sl_vtr, 2 * t + (i + 1))
                    act.activation(l_vtok[:, i * 512:i * 512 + 512], ub[1 + i][:, :], ACT.Copy).then_inc(sl_vtok, 1)

            def decays(self, t, dec=False):
                act = self.act
                act.wait_ge(sl_b, t + 1)
                self.exp(t, 0, l_e[0], l_b, 1.0)
                n = DEC_SEQ if dec else P
                act.activation(l_eb[:, 0:4 * P // n], l_b.rearrange("p (m n) -> p m n", n=n)[:, :, n - 1],
                               ACT.Exp, scale=1.0 / TAU).then_inc(sl_eb, 1)
                act.wait_ge(sl_d, (NZ - 1) * t + 1)
                self.exp(t, 1, l_e[1], l_e[1], -1.0)

            def keys(self, t):
                self.act.wait_ge(sl_kt, t + 1)
                self.act.activation(l_ktok, ub[3][:, :], ACT.Copy).then_inc(sl_ktok, 1)

            def level(self, t, i, s):
                self.act.wait_ge(sl_d, (NZ - 1) * t + (i + 2))
                e = halves(l_e[i % 2], s)
                self.act.activation(e[:, :, 0, :], e[:, :, 0, :], ACT.Exp, scale=-1.0 / TAU)
                self.exp(t, i + 2, e[:, :, 1, :], e[:, :, 1, :], 1.0)

            def squares(self, t):
                act = self.act
                for h in range(N_GLA):
                    act.wait_ge(sl_o, 2 * t + (h // 2 + 1))
                    act.activation(l_o[:, h * DV:h * DV + DV], ub[1 + h // 2][:, (h % 2) * DV:(h % 2) * DV + DV],
                                   ACT.Square, accum_out=l_ss[:, h:h + 1]).then_inc(sl_sq, 1)

            def rstd(self, t):
                act = self.act
                act.wait_ge(sl_var, t + 1)
                act.activation(l_rstd, l_var, ACT.Ln).then_inc(sl_lnv, 1)
                act.wait_ge(sl_lnv, t + 1)
                act.activation(l_rstd, l_rstd, ACT.Exp, scale=-0.5).then_inc(sl_rs, 1)

            def leave(self, t):
                act = self.act
                act.wait_ge(sl_st, 16 * t + 16)
                og = l_og.rearrange("p (h e n) -> p h e n", e=2, n=P)
                for i in range(2):
                    act.wait_ge(sl_gt, 2 * t + (i + 1))
                    bank = ub[3 + i][:, :].rearrange("p (h e n) -> p h e n", e=2, n=P)
                    for e in range(2):
                        act.activation(og[:, 2 * i:2 * i + 2, e, :], bank[:, :, e, :], ACT.Copy,
                                       scale=gn_col[:, e:e + 1]).then_inc(sl_og, 1)
                act.wait_ge(sl_og, 4 * t + 5)
                act.dma_start(o_t[D_MODEL // 2:D_MODEL, ds(t * P, P)].rearrange("(c p) n -> p c n", p=P),
                              l_og.rearrange("p (c n) -> p c n", c=8)).then_inc(sl_st, 16)

            def tile(self, t):
                def part_0():
                    self.gates(t)
                    if not (type(t) is int and t == 0):
                        self.leave(t - 1)
                    self.load_v(t)
                    self.decays(t)
                    self.level(t, 0, LEVELS[0])
                    self.keys(t)
                    for i in range(1, 4):
                        self.level(t, i, LEVELS[i])

                def part_1():
                    self.values(t)
                    for i in range(4, 7):
                        self.level(t, i, LEVELS[i])

                def part_2():
                    self.squares(t)
                    self.rstd(t)
                    self.load(t + 1)
                return part_0, part_1, part_2

        class linear_dve:
            def __init__(self, dve):
                self.dve = dve

            def first(self):
                dve = self.dve
                dve.wait_ge(sb_w, 16 * 5)
                dve.memset(l_s, 0.0).then_inc(sl_ini, 1)
                dve.memset(l_att, 0.0).then_inc(sl_ini, 1)
                dve.memset(lr[:, :], 1.0).then_inc(sl_ini, 1)
                dve.wait_ge(sl_ini, 3)
                dve.sem_inc(sl_up, 1)
                dve.sem_inc(sl_on, 1)

            def copy_diagonal(self, t):
                dve = self.dve
                dve.wait_ge(sl_dg, t + 1)
                dve.nop(nofuse=True)
                dve.copy_predicated(l_att, tables_sb[:, M_DIAG:M_DIAG + 512], ub[0][:, :]).then_inc(sl_dcp, 1)

            def gates(self, t, dec=False):
                dve = self.dve
                dve.wait_ge(sl_a, 3 * t + 3)
                dve.scalar_tensor_tensor(out=l_e[1], in0=ub[0][:, :], scalar=0.0, in1=l_e[0], op0=ALU.min,
                                         op1=ALU.subtract).then_inc(sl_la, 1)
                dve.wait_ge(sl_la, t + 1)
                m = M_SCAN_DEC if dec else M_SCAN
                dve.tensor_tensor_scan(l_b, tables_sb[:, m:m + 512], l_e[1], 0.0, ALU.mult, ALU.add)\
                   .then_inc(sl_b, 1)
                self.copy_diagonal(t)
                dve.wait_ge(sl_ex, NZ * t + 1)
                dve.wait_ge(sl_q, 16 * t + 16)
                dve.tensor_tensor(l_qe, l_q, l_e[0], ALU.mult).then_inc(sl_zz, 1)
                dve.wait_ge(sl_ex, NZ * t + 2)
                dve.wait_ge(sl_k, 16 * t + 16)
                dve.tensor_tensor(l_z[0], l_k, l_e[1], ALU.mult).then_inc(sl_zz, 1)

            def level(self, t, i, s):
                dve = self.dve
                dve.wait_ge(sl_ex, NZ * t + (i + 3))
                if i == 1:
                    dve.wait_ge(sl_kt, t + 1)
                if i >= 2:
                    dve.wait_ge(sl_p, len(LEVELS) * t + (i - 1))
                z, e, q, k = (halves(x, s) for x in (l_z[(i + 1) % 2], l_e[i % 2], l_q, l_k))
                dve.tensor_tensor(z[:, :, 0, :], k[:, :, 0, :], e[:, :, 0, :], ALU.mult)
                dve.tensor_tensor(z[:, :, 1, :], q[:, :, 1, :], e[:, :, 1, :], ALU.mult).then_inc(sl_zz, 1)

            def take(self, t, i, s):
                dve = self.dve
                if i:
                    dve.wait_ge(sl_cp, len(LEVELS) * t + i)
                else:
                    dve.wait_ge(sl_dcp, t + 1)
                dve.wait_ge(sl_p, len(LEVELS) * t + (i + 1))
                dve.nop(nofuse=True)
                m = LEVELS.index(s) * 256
                dve.copy_predicated(halves(l_att, s)[:, :, 1, :],
                                    tables_sb[:, m:m + 256].rearrange("p (n s) -> p n s", s=s),
                                    ub[4 - i % 2][:, 0:256].rearrange("p (n s) -> p n s", s=s)).then_inc(sl_cp, 1)

            def variance(self, t):
                dve = self.dve
                dve.wait_ge(sl_sq, 4 * t + 4)
                dve.tensor_scalar(l_var, l_ss, 1.0 / DV, EPS, ALU.mult, ALU.add).then_inc(sl_var, 1)

            def scale_out(self, t):
                dve = self.dve
                dve.wait_ge(sl_rs, t + 1)
                dve.tensor_tensor(l_var, l_var, l_rstd, ALU.mult).then_inc(sl_nt, 1)
                dve.wait_ge(sl_nt, 4 * t + 1)
                dve.tensor_tensor(l_var, l_var, l_rstd, ALU.mult).then_inc(sl_nt, 1)
                dve.wait_ge(sl_nt, 4 * t + 2)
                dve.tensor_scalar(l_var, l_var, -0.5, 1.5, ALU.mult, ALU.add).then_inc(sl_nt, 1)
                dve.wait_ge(sl_nt, 4 * t + 3)
                dve.tensor_tensor(l_rstd, l_rstd, l_var, ALU.mult).then_inc(sl_nt, 1)
                dve.wait_ge(sl_nt, 4 * t + 4)
                for h in range(N_GLA):
                    dve.tensor_scalar(l_o[:, h * DV:h * DV + DV],
                                      ub[1 + h // 2][:, (h % 2) * DV:(h % 2) * DV + DV],
                                      l_rstd[:, h:h + 1], None, ALU.mult).then_inc(sl_on, 1)

            def state(self, t):
                dve = self.dve
                dve.wait_ge(sl_eb, t + 1)
                for h in range(N_GLA):
                    dve.wait_ge(sl_ds, 2 * t + (h // 2 + 1))
                    sh = l_s[:, h * DV:h * DV + DV]
                    dve.scalar_tensor_tensor(out=sh, in0=sh, scalar=l_eb[:, h:h + 1],
                                             in1=ub[4 * (h // 2)][:, (h % 2) * DV:(h % 2) * DV + DV],
                                             op0=ALU.mult, op1=ALU.add).then_inc(sl_up, 1)

            def tile(self, t):
                def part_0():
                    self.gates(t)
                    self.level(t, 0, LEVELS[0])
                    for i in range(1, 4):
                        self.level(t, i, LEVELS[i])
                        self.take(t, i - 1, LEVELS[i - 1])

                def part_1():
                    for i in range(4, 7):
                        self.level(t, i, LEVELS[i])
                        self.take(t, i - 1, LEVELS[i - 1])

                def part_2():
                    self.take(t, 6, LEVELS[6])
                    self.state(t)
                    self.variance(t)
                    self.scale_out(t)
                return part_0, part_1, part_2

        def linear_pool(pool, t, levels, n):
            pool.wait_ge(sl_b, t + 1)
            for i, (n, at) in enumerate([(n, n - 1)] + [(2 * s, s - 1) for s in levels]):
                if i:
                    pool.wait_ge(sl_zz, NZ * t + i)
                b = l_b.rearrange("p (m n) -> p m n", n=n)
                pool.tensor_tensor(l_e[(i + 1) % 2].rearrange("p (m n) -> p m n", n=n), b,
                                   b[:, :, at:at + 1].to_broadcast([P, 4 * P // n, n]), ALU.subtract)\
                    .then_inc(sl_d, 1)

        T = NTP
        HALF = DEC_BATCH // 2
        d_s = [work[:, 0:1024], work[:, 4608:5632]]
        d_q = work[:, 3584:4608]
        d_q_own = work[:, 3584:4736].rearrange("p (s m) -> p s m", m=P + DEC_SEQ)[:, :, 0:DEC_SEQ]
        d_k = l_v
        d_bank = ub[3:5]

        class decode_pe:

            def __init__(self, pe):
                self.pe = pe

            def levels(self):
                logits, values, diagonal, keys, level, _, _ = linear_stages(self.pe, T, dec=True)
                stages = {3: logits, 6: linear_stages(self.pe, T - 1)[-1], 12: diagonal, 18: keys, 32: values}
                for i, step in enumerate((20, 22, 25, 28)):
                    stages[step] = lambda i=i: level(i)
                return stages

            def half(self, h, half):
                pe = self.pe
                out = ub[1 + h // 2][:, (h % 2) * DV:(h % 2) * DV + DV]
                vh = l_vtok[:, h * DV:h * DV + DV]
                if half == 0:
                    pe.wait_ge(sl_cp, len(LEVELS) * T + len(DEC_LEVELS))
                    pe.wait_ge(sl_dcp, T + 1)
                    pe.wait_ge(sl_vtok, 2 * T + 2)
                    pe.wait_ge(sd_q, h + 2)
                    pe.matmul(out, l_att[:, h * P:h * P + P], vh, start=True, stop=False)
                pe.wait_ge(sd_in[half], 16 * (h + 1))
                for i in range(HALF):
                    s = half * HALF + i
                    mm = pe.matmul(out, d_q[:, s * P:s * P + P], d_s[half][:, i * DV:i * DV + DV],
                                   start=False, stop=(s == DEC_BATCH - 1))
                pe.wait_ge(sd_k, h + 1)
                if h or half:
                    pe.wait_ge(sd_up, DEC_BATCH * h + HALF * half)
                for i in range(HALF):
                    s = half * HALF + i
                    mm = pe.matmul(d_bank[i // 2][:, (i % 2) * DV:(i % 2) * DV + DV], d_k[:, s * P:s * P + P], vh,
                                   start=True, stop=True)
                    if i % 2:
                        mm.then_inc(sd_ds, 1)

            def head(self, h):
                return {9: lambda: self.half(h, 0), 30: lambda: self.half(h, 1)}

            def out(self):
                def turn():
                    self.pe.wait_ge(sd_up, DEC_BATCH * N_GLA)
                    linear_stages(self.pe, T)[-1](decoded=True)
                return {24: turn}

        class decode_act:

            def __init__(self, act, lin):
                self.act, self.lin = act, lin

            def load(self, h, half):
                self.act.dma_start(d_s[half].rearrange("p (s e) -> p s e", s=HALF),
                                   state[half * HALF:half * HALF + HALF, h].rearrange("s d e -> d s e"))\
                    .then_inc(sd_in[half], 16)

            def store(self, h, half):
                self.act.wait_ge(sd_up, DEC_BATCH * h + HALF * half + HALF)
                self.act.dma_start(gla_s[half * HALF:half * HALF + HALF, h].rearrange("s d e -> d s e"),
                                   d_s[half].rearrange("p (s e) -> p s e", s=HALF)).then_inc(sd_out[half], 16)

            def levels(self):
                act, lin = self.act, self.lin

                def part_0():
                    lin.gates(T)
                    lin.leave(T - 1)
                    lin.load_v(T)
                    act.wait_ge(sl_up, 4 * NTP + 1)
                    act.dma_start(gla_p.rearrange("h d e -> d h e"), l_s.rearrange("p (h e) -> p h e", h=N_GLA))\
                       .then_inc(sd_gp, 16)
                    lin.decays(T, dec=True)
                    lin.level(T, 0, DEC_LEVELS[0])
                    lin.keys(T)
                    for i in range(1, len(DEC_LEVELS)):
                        lin.level(T, i, DEC_LEVELS[i])

                def part_1():
                    lin.values(T)
                    act.wait_ge(sl_zz, NZ * T + 2 + len(DEC_LEVELS))
                    act.wait_ge(sl_p, len(LEVELS) * T + len(DEC_LEVELS))
                    self.load(0, 0)
                    self.load(0, 1)
                return part_0, part_1, lambda: None

            def head(self, h):
                def part_0():
                    if h:
                        self.act.wait_ge(sd_out[1], 16 * h)
                        self.load(h, 1)

                def part_2():
                    self.store(h, 1)
                    if h + 1 < N_GLA:
                        self.act.wait_ge(sd_out[0], 16 * (h + 1))
                        self.load(h + 1, 0)
                return part_0, lambda: self.store(h, 0), part_2

            def out(self):
                def part_0():
                    act = self.act
                    act.wait_ge(sd_ds, 4 * N_GLA)
                    for h in range(N_GLA):
                        act.activation(l_o[:, h * DV:h * DV + DV],
                                       ub[1 + h // 2][:, (h % 2) * DV:(h % 2) * DV + DV],
                                       ACT.Square, accum_out=l_ss[:, h:h + 1]).then_inc(sl_sq, 1)
                    self.lin.rstd(T)
                return part_0, lambda: self.lin.leave(T), lambda: None

            def end(self):
                for half in range(2):
                    self.act.wait_ge(sd_out[half], 16 * N_GLA)
                self.act.wait_ge(sd_gp, 16)
                self.act.wait_ge(sl_st, 16 * (NT + 1))

        class decode_dve:

            def __init__(self, dve, lin):
                self.dve, self.lin = dve, lin

            def levels(self):
                dve, lin = self.dve, self.lin

                def part_0():
                    dve.wait_ge(sl_o, 2 * NTP)
                    dve.memset(l_att, 0.0).then_inc(sl_ini, 1)
                    dve.wait_ge(sl_ini, 4)
                    lin.gates(T, dec=True)
                    lin.level(T, 0, DEC_LEVELS[0])
                    for i in range(1, len(DEC_LEVELS)):
                        lin.level(T, i, DEC_LEVELS[i])
                        lin.take(T, i - 1, DEC_LEVELS[i - 1])

                def part_1():
                    lin.take(T, len(DEC_LEVELS) - 1, DEC_LEVELS[-1])
                    dve.memset(d_q, 0.0).then_inc(sd_q, 1)
                return part_0, part_1, lambda: None

            def head(self, h):
                dve = self.dve

                def part_0():
                    if h:
                        dve.wait_ge(sd_ds, 4 * h)
                    else:
                        dve.wait_ge(sd_q, 1)
                        dve.wait_ge(sl_ktok, T + 1)
                        dve.wait_ge(sl_vtok, 2 * T + 2)
                        dve.wait_ge(sl_eb, T + 1)
                    dve.tensor_copy(d_q_own, l_qe[:, h * P:h * P + P].rearrange("p (s n) -> p s n", n=DEC_SEQ))\
                       .then_inc(sd_q, 1)
                    for s in range(DEC_BATCH):
                        ins = dve.tensor_scalar(d_k[:, s * P:s * P + P], l_ktok[:, h * P:h * P + P],
                                                seq_col[:, s:s + 1], None, ALU.mult)
                    ins.then_inc(sd_k, 1)
                return part_0, lambda: self.update(h, 0), lambda: self.update(h, 1)

            def update(self, h, half):
                dve = self.dve
                for i in range(HALF):
                    dve.wait_ge(sd_ds, 4 * h + 2 * half + i // 2 + 1)
                    m = h * DEC_BATCH + half * HALF + i
                    sh = d_s[half][:, i * DV:i * DV + DV]
                    dve.scalar_tensor_tensor(out=sh, in0=sh, scalar=l_eb[:, m:m + 1],
                                             in1=d_bank[i // 2][:, (i % 2) * DV:(i % 2) * DV + DV],
                                             op0=ALU.mult, op1=ALU.add).then_inc(sd_up, 1)

            def out(self):
                def part_0():
                    self.lin.variance(T)
                    self.lin.scale_out(T)
                return part_0, lambda: None, lambda: None

        KEYS = CACHE + DEC_SEQ
        b_q = work[:, 0:1024].rearrange("p (g r n) -> p g r n", g=2, r=GQA)
        b_kn = work[:, 1024:1280].rearrange("p (c n) -> p c n", c=2)
        b_vn = work[:, 1280:1536].rearrange("p (c n) -> p c n", c=2)
        b_ck = work[:, 1536:1792]
        b_cv = work[:, 2048:2304]
        b_ks = work[:, 2560:2848].rearrange("p (g n) -> p g n", g=2)
        b_p = work[:, 2848:3136].rearrange("p (g n) -> p g n", g=2)
        b_ptc = work[:, 3136:3392]
        b_ptn = work[0:DEC_SEQ, 3392:3648]
        b_vnew = work[0:DEC_SEQ, 3648:3904]
        b_qb = work[:, 3904:4032].rearrange("p (g n) -> p g n", g=2)
        b_vb = work[:, 4032:4064].rearrange("p (c n) -> p c n", c=2)
        b_o = work[0:HEAD_DIM, 4064:6112].rearrange("p (h n) -> p h n", h=N_HEADS)
        b_ex = [work[:, 6112 + 256 * i:6368 + 256 * i] for i in range(4)]
        b_kp = work[:, 7136:7392].rearrange("p (c n) -> p c n", c=2)
        b_vp = work[:, 7392:7648].rearrange("p (c n) -> p c n", c=2)
        b_mx, b_mn, b_neg, b_sk, b_es, b_sum, b_den = (small[:, 8 + 2 * i:10 + 2 * i] for i in range(7))
        kb, vb, sb_, pb, nb = ub
        ob = sb_

        def cached_pe(pe, b, first=False):
            def exports():
                pe.wait_ge(sb_in, 16 * 8)
                pe.wait_ge(sa_out, 4 * NTP + 1)
                for i, x in enumerate((b_kp, b_vp, b_kn, b_vn)):
                    for c in range(2):
                        mm = pe.transpose(ub[i][:, c * P:c * P + P], x[:, c, :], ident)
                    mm.then_inc(sb_xt, 1)

            def keys():
                pe.wait_ge(sb_ck, 16 * b + 16)
                pe.wait_ge(sb_new, b + 1)
                for gp in range(2):
                    pe.transpose(kb[:, gp * P:gp * P + P], b_ck[:, gp * P:gp * P + P], ident)
                for c in range(2):
                    mm = pe.transpose(vb[0:DEC_SEQ, c * P:c * P + P], b_vb[:, c, :], ident)
                mm.then_inc(sb_kt, 1)

            def scores():
                pe.wait_ge(sb_ks, b + 1)
                pe.nop(nofuse=True)
                for gp in range(2):
                    for half in range(2):
                        rows = slice(half * HEAD_DIM, half * HEAD_DIM + HEAD_DIM)
                        mm = pe.matmul(sb_[rows, gp * KEYS:gp * KEYS + KEYS], b_qb[rows, gp, :], b_ks[rows, gp, :],
                                       start=True, stop=True)
                mm.then_inc(sb_s, 1)

            def turn():
                pe.wait_ge(sb_pr, 2 * b + 2)
                for gp in range(2):
                    mm = pe.transpose(pb[:, gp * P:gp * P + P], b_p[:, gp, 0:CACHE], ident)
                mm.then_inc(sb_pt, 1)
                for gp in range(2):
                    mm = pe.transpose(nb[0:DEC_SEQ, gp * P:gp * P + P], b_p[:, gp, CACHE:KEYS], ident)
                mm.then_inc(sb_pt, 1)

            def outputs():
                pe.wait_ge(sb_cv, 16 * b + 16)
                pe.wait_ge(sb_pc, 2 * b + 2)
                for g in range(N_KV):
                    cols = slice((g // 2) * P + (g % 2) * HEAD_DIM, (g // 2) * P + (g % 2) * HEAD_DIM + HEAD_DIM)
                    dims = slice(g * HEAD_DIM, g * HEAD_DIM + HEAD_DIM)
                    pe.matmul(ob[0:HEAD_DIM, dims], b_cv[:, dims], b_ptc[:, cols], start=True, stop=False)
                    mm = pe.matmul(ob[0:HEAD_DIM, dims], b_vnew[:, dims], b_ptn[:, cols], start=False, stop=True)
                mm.then_inc(sb_av, 1)

            def first_keys():
                exports()
                pe.wait_ge(sb_xc, 4)
                keys()

            return {12: first_keys if first else keys, 20: scores, 32: turn, 42: outputs}

        class cached_act:
            def __init__(self, act):
                self.act = act

            def load(self, b, which):
                dst, src, s = ((b_ck, cache_k, sb_ck), (b_cv, cache_v, sb_cv))[which]
                self.act.dma_start(dst, src[ds(b, 1)].rearrange("a t n -> (a t) n")).then_inc(s, 16)

            def first(self):
                act = self.act
                act.wait_ge(sa_st, 16 * (4 * NTP + 1))
                q_v = h_t[Q0:K0, PAD + SEQ:PAD + TOK].rearrange("(g f r d) n -> f d g r n", g=2, f=2, r=GQA)
                for half in range(2):
                    for gp in range(2):
                        act.dma_start(b_q[half * HEAD_DIM:half * HEAD_DIM + HEAD_DIM, gp], q_v[half][:, gp])\
                           .then_inc(sb_in, 16)
                for x, row, col in ((b_kn, K0, PAD + SEQ), (b_vn, V0, PAD + SEQ),
                                    (b_kp, K0, PAD + SEQ - P), (b_vp, V0, PAD + SEQ - P)):
                    act.dma_start(x, h_t[row:row + 256, col:col + P].rearrange("(c p) n -> p c n", p=P))\
                       .then_inc(sb_in, 16)
                self.load(0, 0)
                self.load(0, 1)
                act.wait_ge(sa_mk, NTP + 1)
                for i in range(4):
                    act.wait_ge(sb_xt, i + 1)
                    act.activation(b_ex[i], ub[i][:, 0:256], ACT.Copy).then_inc(sb_xc, 1)
                act.wait_ge(sb_xc, 4)
                act.dma_start(win_kp, b_ex[0]).then_inc(sb_w, 16)
                act.dma_start(win_vp, b_ex[1]).then_inc(sb_w, 16)
                act.dma_start(win_ks[:, CACHE - DEC_SEQ:CACHE, :], b_ex[2]).then_inc(sb_w, 16)
                act.dma_start(win_vs[:, CACHE - DEC_SEQ:CACHE, :], b_ex[3]).then_inc(sb_w, 16)

            def sequence(self, b):
                act = self.act
                more = not (type(b) is int and b == DEC_BATCH - 1)

                def part_0():
                    act.wait_ge(sb_kt, b + 1)
                    act.activation(b_ks[:, :, 0:CACHE], kb[:, 0:256].rearrange("p (g n) -> p g n", g=2), ACT.Copy)
                    act.activation(b_vnew, vb[0:DEC_SEQ, 0:256], ACT.Copy).then_inc(sb_ks, 1)
                    if more:
                        self.load(b + 1, 0)
                    act.wait_ge(sb_neg, b + 1)
                    act.activation(b_es, b_sk, ACT.Exp)
                    for gp in range(2):
                        act.activation(b_p[:, gp, :], sb_[:, gp * KEYS:gp * KEYS + KEYS], ACT.Exp,
                                       bias=b_neg[:, gp:gp + 1], accum_out=b_sum[:, gp:gp + 1]).then_inc(sb_e, 1)
                    act.wait_ge(sb_pt, 2 * b + 1)
                    act.activation(b_ptc, pb[:, 0:256], ACT.Copy).then_inc(sb_pc, 1)
                    act.wait_ge(sb_pt, 2 * b + 2)
                    act.activation(b_ptn, nb[0:DEC_SEQ, 0:256], ACT.Copy).then_inc(sb_pc, 1)
                    act.wait_ge(sb_av, b + 2)
                    act.activation(b_o[:, :, ds(b * DEC_SEQ, DEC_SEQ)],
                                   ob[0:HEAD_DIM, 0:256].rearrange("p (h n) -> p h n", h=N_HEADS), ACT.Copy)\
                       .then_inc(sb_oc, 1)
                    if more:
                        self.load(b + 1, 1)
                return part_0, lambda: None, lambda: None

            def last(self):
                self.act.wait_ge(sb_oc, DEC_BATCH)
                self.act.dma_start(o_t[0:D_MODEL // 2, SEQ:TOK].rearrange("(h d) n -> d h n", d=HEAD_DIM), b_o)\
                    .then_inc(sb_w, 16)
                self.act.wait_ge(sb_w, 16 * 5)

        class cached_dve:
            def __init__(self, dve):
                self.dve = dve

            def first(self):
                self.dve.wait_ge(sb_in, 16 * 8)
                self.dve.sem_inc(sb_av, 1)

            def sequence(self, b):
                dve = self.dve

                def part_0():
                    tok = ds(b * DEC_SEQ, DEC_SEQ)
                    dve.wait_ge(sb_av, b + 1)
                    dve.tensor_copy(b_qb.rearrange("p g (r n) -> p g r n", r=GQA), b_q[:, :, :, tok])
                    dve.tensor_copy(b_vb, b_vn[:, :, tok])
                    dve.tensor_copy(b_ks[:, :, CACHE:KEYS], b_kn[:, :, tok]).then_inc(sb_new, 1)
                    dve.wait_ge(sb_s, b + 1)
                    dve.tensor_reduce(b_mx, sb_[:, 0:2 * KEYS].rearrange("p (g n) -> p g n", g=2), AX.X, ALU.max)\
                       .then_inc(sb_dv, 1)
                    dve.wait_ge(sb_dv, 5 * b + 1)
                    dve.tensor_tensor(b_mn, b_mx, sink_dec[:, :], ALU.max).then_inc(sb_dv, 1)
                    dve.wait_ge(sb_dv, 5 * b + 2)
                    dve.tensor_scalar(b_neg, b_mn, -1.0, None, ALU.mult).then_inc(sb_dv, 1)
                    dve.wait_ge(sb_dv, 5 * b + 3)
                    dve.tensor_tensor(b_sk, sink_dec[:, :], b_neg, ALU.add).then_inc(sb_neg, 1)

                def part_1():
                    dve.wait_ge(sb_e, 2 * b + 2)
                    dve.tensor_tensor(b_den, b_sum, b_es, ALU.add).then_inc(sb_dv, 1)
                    dve.wait_ge(sb_dv, 5 * b + 4)
                    dve.reciprocal(b_den, b_den).then_inc(sb_dv, 1)
                    dve.wait_ge(sb_dv, 5 * b + 5)
                    for gp in range(2):
                        dve.tensor_scalar(b_p[:, gp, :], b_p[:, gp, :], b_den[:, gp:gp + 1], None, ALU.mult)\
                           .then_inc(sb_pr, 1)
                return part_0, part_1, lambda: None

        @block.gpsimd
        def _(pool):
            pool.memset(mhalf[:, :], -0.5).then_inc(s_mh, 1)
            pool.memset(zeros[:, :], 0.0).then_inc(s_mh, 1)
            pool.wait_ge(s_mh, 2)
            for t in range(NT):
                pool.wait_ge(s_var, t + 1)
                pool.tensor_tensor(rstd, var, mhalf[:, 0:1], ALU.pow).then_inc(s_rstd, 1)
                if t == 1:
                    split(pool, 0, RANK)
            split(pool, 1)
            pool.wait_ge(s_tload, 16)
            pool.tensor_copy(tables_sb[:, :], work[:, 2 * D_MODEL:2 * D_MODEL + M_ALL]).then_inc(s_tables, 1)
            with pool.Fori(2, J_GLA + 1) as j:
                split(pool, j)
            with pool.Fori(J_GLA, J_LEV) as j:
                linear_pool(pool, j - J_GLA, LEVELS, P)
                split(pool, j + 1)
            linear_pool(pool, T, DEC_LEVELS, DEC_SEQ)
            with pool.Fori(J_LEV + 1, 1 + N_ITEMS) as j:
                split(pool, j)
            pool.sem_inc(t_wready, 2)
            pool.wait_ge(s_wfree, 4 * N_ITEMS + 6)
            with pool.Fori(0, NCH) as c:
                for q in range(4):
                    s = q % 2
                    if q == 1:
                        pool.wait_ge(s_wfree, 4 * N_ITEMS + 8)
                    pool.wait_ge(t_w[s], 32 * c + (16 * (q // 2) + 16))
                    pool.wait_ge(t_wfree, 4 * c + (q + 1))
                    src = o_raw[s].rearrange("p (k n) -> p k n", n=P)
                    pool.tensor_tensor(o_hi[s], src, zeros[:, :].unsqueeze(1).to_broadcast([P, 8, P]), ALU.add)\
                        .then_inc(t_whi, 1)
                    pool.wait_ge(t_whi, 4 * c + (q + 1))
                    pool.tensor_tensor(o_lo[s], src, o_hi[s].bitcast(F32), ALU.subtract).then_inc(t_wready, 1)

        @block.scalar
        def _(act):
            act.sem_inc(s_wfree, 4)
            act.sem_inc(s_staged, 3)
            act.sem_inc(s_xt, 4)

            def high_halves(t):
                for b in range(4):
                    act.wait_ge(s_xt, 4 * t + (b + 5))
                    act.activation(x_hi[:, 4 * b:4 * b + 4, t * P:t * P + P],
                                   xt_bank[b][:, :].rearrange("p (k n) -> p k n", k=4), ACT.Copy)\
                       .then_inc(s_xhi, 1)

            def sum_of_squares(t):
                act.wait_ge(s_x[t % 3], 16 * (t // 3) + 16)
                if t >= 1:
                    act.wait_ge(s_ss, t)
                if t >= 2:
                    act.wait_ge(s_var, t - 1)
                act.activation(squares, x_buf[t % 3], ACT.Square, accum_out=ss[:, t % 2:t % 2 + 1])\
                   .then_inc(s_ss, 1)

            sum_of_squares(0)
            sum_of_squares(1)
            for t in range(NT):
                high_halves(t)
                if t + 2 < NT:
                    sum_of_squares(t + 2)

            def item_norm_b(j, n):
                wait_acc(act, j, n)
                act.wait_ge(s_ssq, (j - 1) * NG + (n + 1))
                act.activation(tmp_a, acc[n][:, 0:TN], ACT.Square).then_inc(s_sq, 1)
                act.wait_ge(s_sq, (j - 1) * NG + (n + 1))
                act.activation(sq_hi, tmp_a, ACT.Copy).then_inc(s_sqhi, 1)
                act.wait_ge(s_v, (j - 1) * NG + (n + 2))
                act.activation(tmp_b, tmp_b, ACT.Sqrt).then_inc(s_sd, 1)

            def item_silu(j, n):
                wait_acc(act, j, n)
                act.wait_ge(s_staged, j * NG + (n + 3))
                act.activation(tmp_a, acc[n][:, 0:TN], ACT.Exp, scale=-1.0).then_inc(s_sig, 1)

            def nothing(j, n):
                pass

            def item(j, before, now, unit=(lambda: None, lambda: None, lambda: None)):
                before(j - 1, 2)
                unit[0]()
                now(j, 0)
                unit[1]()
                now(j, 1)
                unit[2]()

            act.sem_inc(s_ssq, 1)
            item(1, nothing, item_norm_b)
            with act.Fori(2, 1 + N_QK) as j:
                item(j, item_norm_b, item_norm_b)
            item(1 + N_QK, item_norm_b, nothing)
            item(2 + N_QK, nothing, nothing)
            attend = attend_act(act)
            act.wait_ge(s_tab, 16 * 22)
            act.wait_ge(s_tables, 1)
            attend.first()
            with act.Fori(J_ATT, J_DEC - 1) as j:
                item(j, nothing, nothing, attend.tile(j - J_ATT))
            item(J_DEC - 1, nothing, nothing, attend.tile(NTP - 1))
            cached = cached_act(act)
            cached.first()
            with act.Fori(J_DEC, J_GLA - 1) as j:
                item(j, nothing, nothing, cached.sequence(j - J_DEC))
            item(J_GLA - 1, nothing, nothing, cached.sequence(DEC_BATCH - 1))
            cached.last()
            linear = linear_act(act)
            linear.first()
            item(J_GLA, nothing, item_silu, linear.tile(0))
            with act.Fori(J_GLA + 1, J_GLA + NTP) as j:
                item(j, item_silu, item_silu, linear.tile(j - J_GLA))
            decode = decode_act(act, linear)
            item(J_LEV, item_silu, item_silu, decode.levels())
            for h in range(N_GLA):
                item(J_LEV + 1 + h, item_silu, item_silu, decode.head(h))
            item(J_LEV + 1 + N_GLA, item_silu, item_silu, decode.out())
            with act.Fori(J_LEV + 2 + N_GLA, 1 + N_ITEMS) as j:
                item(j, item_silu, item_silu)

            def high(first, last):
                for p, (q, n, i) in list(enumerate(pieces()))[first:last]:
                    wait_acc(act, N_ITEMS, n)
                    if is_gated_late(q, n):
                        act.wait_ge(t_mul, 2 * (q - 2) + i + 1)
                    else:
                        act.wait_ge(t_piece[p % SLOTS], 16 * (p // SLOTS) + 16)
                    act.activation(x_hi[:, 4 * q + 2 * i:4 * q + 2 * i + 2, n * TN:n * TN + TN],
                                   piece_sb[:, p % SLOTS, :, :], ACT.Copy).then_inc(t_mhi, 1)

            act.sem_inc(t_mlo, SLOTS)
            act.sem_inc(t_wfree, 2)
            high(0, 6)
            item_silu(N_ITEMS, 2)
            high(6, 24)
            decode.end()
            with act.Fori(0, NCH) as c:
                for t in range(NT):
                    act.wait_ge(t_y, NT * c + (t + 1 + NT))
                    act.dma_start(rows_of(y_p, y_s, t, c), y_sb[:, t % 3, :]).then_inc(t_st[t % 3], 16)
            for i in range(3):
                act.wait_ge(t_st[i], 16 * NCH * NT // 3)

        @block.tensor
        def _(pe):
            pe.wait_ge(s_ident, 16)

            def turn_x(t):
                pe.wait_ge(s_xn, t + 1)
                for b in range(4):
                    pe.wait_ge(s_xlo, 4 * t + (b + 1))
                    for k in range(4):
                        c = (4 * b + k) * P
                        mm = pe.transpose(xt_bank[b][:, k * P:k * P + P], x_buf[t % 3][:, c:c + P], ident)
                    mm.then_inc(s_xt, 1)

            def item(j, cols, norm=False, norm_before=False, stages={}):
                for n in range(NG):
                    group(j, n, cols, norm, norm_before, stages)

            def group(j, n, cols, norm=False, norm_before=False, stages={}):
                pe.wait_ge(s_staged, NG * j + (n + 1))
                for k in range(KT):
                    if n * KT + k in stages:
                        stages[n * KT + k]()
                    if n == 0 and k % 4 == 0:
                        pe.wait_ge(s_wready, 4 * j + (k // 4 + 1))
                    if n > 0 and k == 6 and norm:
                        sum_squares(j, n - 1)
                    if n == 0 and k == 6 and norm_before:
                        sum_squares(j - 1, NG - 1)
                    tok = slice(n * TN, n * TN + TN)
                    out = acc[n][0:cols, 0:TN]
                    if cols == P:
                        pe.matmul(out, w_lo[:, k, :], x_hi[:, k, tok], start=(k == 0), stop=False)
                        pe.matmul(out, w_hi[:, k, :], x_lo[:, k, tok], start=False, stop=False)
                        mm = pe.matmul(out, w_hi[:, k, :], x_hi[:, k, tok], start=False, stop=(k == KT - 1))
                    else:
                        if k == 0:
                            pe.matmul(out, w_hi[:, k, 0:cols], x_hi[:, k, tok], start=True, stop=False)
                        mm = pe.matmul(acc[n][0:RANK, 0:TN], w_hi[:, k, 0:RANK], x_lo[:, k, tok],
                                       start=False, stop=False)
                        if k > 0:
                            mm = pe.matmul(out, w_hi[:, k, 0:cols], x_hi[:, k, tok], start=False,
                                           stop=(k == KT - 1))
                    if n == NG - 1 and k % 4 == 3:
                        mm.then_inc(s_wfree, 1)
                if n < NG - 1:
                    mm.then_inc(s_acc, 1)

            def sum_squares(j, n):
                pe.wait_ge(s_sqlo, (j - 1) * NG + (n + 1))
                pe.wait_ge(s_v, (j - 1) * NG + (n + 1))
                pe.matmul(ss_bank[:, 0:TN], ones_r, sq_lo, start=True, stop=False)
                pe.matmul(ss_bank[:, 0:TN], ones_r, sq_hi, start=False, stop=True).then_inc(s_ssq, 1)

            for t in range(NT):
                turn_x(t)
                if t % NG == 0 and t > 0:
                    pe.wait_ge(s_xlo, 4 * t + 4)
                    group(0, t // NG - 1, LRR)
            pe.wait_ge(s_xlo, 4 * NT + 4)
            group(0, NG - 1, LRR)
            pe.wait_ge(s_ones, 1)
            item(1, P, norm=True)
            with pe.Fori(2, 1 + N_QK) as j:
                item(j, P, norm=True, norm_before=True)
            item(1 + N_QK, P, norm_before=True)
            item(2 + N_QK, P)
            pe.wait_ge(s_tab, 16 * 22)
            item(J_ATT, P, stages=attend_pe(pe, 0, 18))
            with pe.Fori(J_ATT + 1, J_DEC) as j:
                item(j, P, stages=attend_pe(pe, j - J_ATT))
            item(J_DEC, P, stages=cached_pe(pe, 0, True))
            with pe.Fori(J_DEC + 1, J_GLA) as j:
                item(j, P, stages=cached_pe(pe, j - J_DEC))
            item(J_GLA, P, stages=linear_pe(pe, 0, True))
            with pe.Fori(J_GLA + 1, J_GLA + NTP) as j:
                item(j, P, stages=linear_pe(pe, j - J_GLA))
            decode = decode_pe(pe)
            item(J_LEV, P, stages=decode.levels())
            for h in range(N_GLA):
                item(J_LEV + 1 + h, P, stages=decode.head(h))
            item(J_LEV + 1 + N_GLA, P, stages=decode.out())
            with pe.Fori(J_LEV + 2 + N_GLA, 1 + N_ITEMS) as j:
                item(j, P)

            pe.wait_ge(sl_og, 4 * NT + 1)
            with pe.Fori(0, NCH) as c:
                for q in range(4):
                    pe.wait_ge(t_wready, 4 * c + (q + 3))
                    for t in range(NT):
                        if t % 3 == 0:
                            pe.wait_ge(t_mlo, SLOTS + 2 * (NG * q + t // 3 + 1))
                        if q == 0 and t % 2 == 0:
                            pe.wait_ge(t_y, NT * c + min(t + 2, NT))
                        out = ub[t // 2][:, (t % 2) * WCH:(t % 2) * WCH + WCH]
                        tok = slice(t * P, t * P + P)
                        for i in range(4):
                            k = 4 * q + i
                            hi = o_hi[q % 2][:, 2 * i:2 * i + 2, :].rearrange("p a n -> p (a n)")
                            lo = o_lo[q % 2][:, 2 * i:2 * i + 2, :].rearrange("p a n -> p (a n)")
                            pe.matmul(out, x_lo[:, k, tok], hi, start=(k == 0 and t % 2 == 0), stop=False)
                            pe.matmul(out, x_hi[:, k, tok], lo, start=False, stop=False)
                            mm = pe.matmul(out, x_hi[:, k, tok], hi, start=False,
                                           stop=(k == KT - 1 and (t % 2 == 1 or t == NT - 1)))
                        if t == NT - 1:
                            mm.then_inc(t_wfree, 1)
                        elif q == 3 and t % 2:
                            mm.then_inc(t_acc, 1)

        @block.vector
        def _(dve):
            dve.sem_inc(s_v, 1)
            dve.sem_inc(s_xlo, 4)
            def low_halves(t, banks=range(4)):
                for b in banks:
                    dve.wait_ge(s_xhi, 4 * t + (b + 1))
                    dst = x_lo[:, 4 * b:4 * b + 4, t * P:t * P + P]
                    dve.tensor_tensor(dst, xt_bank[b][:, :].rearrange("p (k n) -> p k n", k=4),
                                      x_hi[:, 4 * b:4 * b + 4, t * P:t * P + P].bitcast(F32),
                                      ALU.subtract).then_inc(s_xlo, 1)

            def variance(t):
                dve.wait_ge(s_ss, t + 1)
                dve.tensor_scalar(var[:, :], ss[:, t % 2:t % 2 + 1], 1.0 / D_MODEL, EPS, ALU.mult, ALU.add)\
                   .then_inc(s_var, 1)

            variance(0)
            dve.wait_ge(s_norm, 16)
            for t in range(NT):
                dve.wait_ge(s_rstd, t + 1)
                dve.scalar_tensor_tensor(out=x_buf[t % 3], in0=x_buf[t % 3], scalar=rstd[:, 0:1],
                                         in1=g_row, op0=ALU.mult, op1=ALU.mult).then_inc(s_xn, 1)
                if t >= 1:
                    low_halves(t - 1, range(2))
                if t + 1 < NT:
                    variance(t + 1)
                if t >= 1:
                    low_halves(t - 1, range(2, 4))
            low_halves(NT - 1)
            dve.wait_ge(s_ident, 16)
            dve.wait_ge(s_const, 16 * 4)
            dve.tensor_copy(ones_r, ones_pair).then_inc(s_ones, 1)
            dve.tensor_scalar(gq_col[:, 0:1], gq_col[:, 0:1], HEAD_DIM ** -0.5, None, ALU.mult)\
               .then_inc(s_nchain, 1)
            dve.wait_ge(s_xt, 4 * NT + 4)
            dve.memset(xn[:, 5 * TN:5 * TN + PAD], 0.0).then_inc(s_zero, 1)

            def staging_free(j, n):
                dve.wait_ge(s_store[n], 16 * j)

            def done(ins):
                ins.then_inc(s_staged, 1)

            def plain(j, n, rows=P, first=False):
                wait_acc(dve, j, n)
                if not first:
                    staging_free(j, n)
                done(dve.tensor_copy(stage[n][0:rows, :], acc[n][0:rows, 0:TN]))

            def scaled(j, n):
                wait_acc(dve, j, n)
                staging_free(j, n)
                done(dve.tensor_scalar(stage[n], acc[n][:, 0:TN], DK ** -0.5, None, ALU.mult))

            def normed(which):
                def run(j, n):
                    dve.wait_ge(s_sqhi, (j - 1) * NG + (n + 1))
                    dve.tensor_tensor(sq_lo, tmp_a, sq_hi.bitcast(F32), ALU.subtract).then_inc(s_sqlo, 1)
                    dve.wait_ge(s_ssq, (j - 1) * NG + (n + 2))
                    dve.tensor_scalar(tmp_b, ss_bank[:, 0:TN], 1.0 / HEAD_DIM, EPS, ALU.mult, ALU.add)\
                       .then_inc(s_v, 1)
                    dve.wait_ge(s_sd, (j - 1) * NG + (n + 1))
                    staging_free(j, n)
                    dve.reciprocal(stage[n], tmp_b).then_inc(s_nchain, 1)
                    dve.wait_ge(s_nchain, (j - 1) * NG + (n + 2))
                    done(dve.scalar_tensor_tensor(out=stage[n], in0=acc[n][:, 0:TN],
                                                  scalar=gq_col[:, which:which + 1], in1=stage[n],
                                                  op0=ALU.mult, op1=ALU.mult))
                return run

            def gated(prompt_only):
                def run(j, n):
                    base = (j - J_GLA) * (3 * NG) + 3 * n
                    m = min(TN, SEQ - n * TN) if prompt_only else TN
                    dve.wait_ge(s_sig, (j - J_GLA) * NG + (n + 1))
                    dve.tensor_scalar(tmp_a, tmp_a, 1.0, None, ALU.add).then_inc(s_schain, 1)
                    dve.wait_ge(s_schain, base + 1)
                    dve.reciprocal(tmp_a, tmp_a).then_inc(s_schain, 1)
                    dve.wait_ge(s_schain, base + 2)
                    if m < TN:
                        staging_free(j, n)
                        dve.tensor_tensor(stage[n][:, m:TN], acc[n][:, m:TN], tmp_a[:, m:TN], ALU.mult)
                    dve.tensor_tensor(tmp_a[:, 0:m], acc[n][:, 0:m], tmp_a[:, 0:m], ALU.mult).then_inc(s_schain, 1)
                    dve.wait_ge(s_schain, base + 3)
                    dve.wait_ge(s_gate[n], (j - J_GLA) * 16 + 16)
                    done(dve.tensor_tensor(stage[n][:, 0:m], stage[n][:, 0:m], tmp_a[:, 0:m], ALU.mult))
                return run

            def item(j, before, now, unit=(lambda: None, lambda: None, lambda: None)):
                before(j - 1, 2)
                unit[0]()
                now(j, 0)
                unit[1]()
                now(j, 1)
                unit[2]()

            q, k = normed(0), normed(1)
            silu, silu_g = gated(False), gated(True)
            plain(0, 0, LRR, True)
            plain(0, 1, LRR, True)
            plain(0, 2, LRR, True)
            q(1, 0)
            q(1, 1)
            n_q = (K0 - Q0) // P
            with dve.Fori(2, 1 + n_q) as j:
                item(j, q, q)
            item(n_q + 1, q, k)
            item(n_q + 2, k, k)
            item(n_q + 3, k, plain)
            item(n_q + 4, plain, plain)
            attend = attend_dve(dve)
            dve.wait_ge(s_tab, 16 * 22)
            dve.wait_ge(s_tables, 1)
            attend.first()
            n_gq = (GK0 - GQ0) // P
            item(J_ATT, plain, scaled, attend.tile(0))
            with dve.Fori(J_ATT + 1, J_ATT + n_gq) as j:
                item(j, scaled, scaled, attend.tile(j - J_ATT))
            item(J_ATT + n_gq, scaled, plain, attend.tile(n_gq))
            with dve.Fori(J_ATT + n_gq + 1, J_DEC) as j:
                item(j, plain, plain, attend.tile(j - J_ATT))
            cached = cached_dve(dve)
            cached.first()
            with dve.Fori(J_DEC, J_GLA) as j:
                item(j, plain, plain, cached.sequence(j - J_DEC))
            linear = linear_dve(dve)
            linear.first()
            item(J_GLA, plain, silu, linear.tile(0))
            with dve.Fori(J_GLA + 1, J_GLA + NTP) as j:
                item(j, silu, silu, linear.tile(j - J_GLA))
            decode = decode_dve(dve, linear)
            item(J_LEV, silu, silu_g, decode.levels())
            for h in range(N_GLA):
                item(J_LEV + 1 + h, silu_g, silu_g, decode.head(h))
            item(J_LEV + 1 + N_GLA, silu_g, silu_g, decode.out())
            with dve.Fori(J_LEV + 2 + N_GLA, 1 + N_ITEMS) as j:
                item(j, silu_g, silu_g)

            def low(first, last):
                for p, (q, n, i) in list(enumerate(pieces()))[first:last]:
                    k = 4 * q + 2 * i
                    piece = piece_sb[:, p % SLOTS, :, :]
                    if is_gated_late(q, n):
                        dve.wait_ge(t_dec, 16)
                        dve.wait_ge(t_piece[p % SLOTS], 16 * (p // SLOTS) + 16)
                        dve.tensor_tensor(piece[:, :, TN - P:TN], piece[:, :, TN - P:TN],
                                          o_dec[:, k - KT // 2:k - KT // 2 + 2, :], ALU.mult).then_inc(t_mul, 1)
                    dve.wait_ge(t_mhi, p + 1)
                    m = (slice(None), slice(k, k + 2), slice(n * TN, n * TN + TN))
                    dve.tensor_tensor(x_lo[m], piece, x_hi[m].bitcast(F32), ALU.subtract).then_inc(t_mlo, 1)

            def add(c, t, first=False):
                if t == NT - 1:
                    dve.wait_ge(t_wfree, 4 * c + 6)
                else:
                    dve.wait_ge(t_acc, 4 * c + (t // 2 + 1))
                dve.wait_ge(t_x[t], 16 * c + 16)
                if not (first and t < 3):
                    dve.wait_ge(t_st[t % 3], 48 * c + 16 * (t // 3))
                dve.tensor_tensor(y_sb[:, t % 3, :], ub[t // 2][:, (t % 2) * WCH:(t % 2) * WCH + WCH],
                                  x_res[:, t, :], ALU.add).then_inc(t_y, 1)

            dve.sem_inc(t_y, NT)
            low(0, 6)
            silu_g(N_ITEMS, 2)
            low(6, 24)
            for t in range(NT):
                add(0, t, True)
            with dve.Fori(1, NCH) as c:
                for t in range(NT):
                    add(c, t)


def hybrid_step(nc, x_p, x_s, cache_k, cache_v, state, norm_g, w_in, w_up, b_gate, qg, kg, sinks, gla_g, w_out,
                consts, tables, y_p, y_s, win_kp, win_vp, gla_p, win_ks, win_vs, gla_s):
    flat = "a b t g d -> (a b) t (g d)"
    h_t = nc.dram_tensor("h_t", [LR0 + LRR, PAD + TOK], F32, kind="Internal").ap()
    o_t = nc.dram_tensor("o_t", [D_MODEL, TOK], F32, kind="Internal").ap()
    x_p = x_p.rearrange("a t d -> (a t) d")
    x_s = x_s.rearrange("b t d -> (b t) d")
    with ExitStack() as ctx:
        def sem(name):
            return ctx.enter_context(nc.semaphore(name))

        project(nc, sem, (x_p, x_s, cache_k.rearrange(flat), cache_v.rearrange(flat), state[0], norm_g,
                             w_in[0], w_up, b_gate, qg, kg, sinks, gla_g, consts, tables,
                             win_kp.rearrange(flat)[0], win_vp.rearrange(flat)[0], gla_p[0, 0],
                             win_ks.rearrange(flat), win_vs.rearrange(flat), gla_s[0], h_t, o_t,
                             w_out[0], y_p.rearrange("a t d -> (a t) d"), y_s.rearrange("b t d -> (b t) d")))


def shape_constants():
    import numpy as np

    c = np.zeros((P, C_ALL), np.float32)
    c[:, C_IDENT:C_IDENT + P] = np.eye(P)
    c[:, C_PAIR:C_PAIR + P] = np.kron(np.eye(2), np.ones((HEAD_DIM, HEAD_DIM)))
    c[:, C_SEQ:C_SEQ + DEC_BATCH] = np.kron(np.eye(DEC_BATCH), np.ones((DEC_SEQ, 1)))
    mask = np.zeros((P, 2 * P), np.float32)
    mask[:CHUNK, 3 * CHUNK:] = MASKED
    mask[CHUNK:, :CHUNK] = MASKED
    c[:, C_MASK:] = mask
    mask = mask.copy()
    mask[:, :P] = MASKED
    c[:, C_MASK0:C_MASK] = mask
    m = np.zeros((P, M_ALL), np.float32)
    for i, s in enumerate(LEVELS):
        n = P // (2 * s)
        pairs = np.kron(np.eye(n), np.concatenate([np.ones((s, s)), np.zeros((s, s))]))
        m[:, i * 256:i * 256 + 256] = np.tile(pairs, (1, N_GLA))
    m[:, M_DIAG:M_SCAN] = np.tile(np.eye(P), (1, N_GLA))
    m[:, M_SCAN:M_SCAN_DEC] = np.arange(4 * P) % P > 0
    m[:, M_SCAN_DEC:] = np.arange(4 * P) % DEC_SEQ > 0
    return c, m


_INS = ["x_prompt", "x_sample", "cache_k", "cache_v", "state_gla", "norm_g", "w_in", "w_gate_up", "b_gate",
        "q_norm_g", "k_norm_g", "sinks", "gla_norm_g", "w_out"]
_OUTS = [(1, SEQ, D_MODEL), (DEC_BATCH, DEC_SEQ, D_MODEL),
         (1, 1, CACHE, N_KV, HEAD_DIM), (1, 1, CACHE, N_KV, HEAD_DIM), (1, 1, N_GLA, DK, DV),
         (1, DEC_BATCH, CACHE, N_KV, HEAD_DIM), (1, DEC_BATCH, CACHE, N_KV, HEAD_DIM),
         (1, DEC_BATCH, N_GLA, DK, DV)]


def kernel(**inputs):
    import numpy as _np
    import concourse.bacc as _bacc
    from concourse import mybir as _mybir
    from concourse.bass_utils import run_bass_kernel_spmd as _run

    nc = _bacc.Bacc("TRN2", target_bir_lowering=False, num_devices=1, dynamic_dma_scratch_size=1024)
    consts, tables = shape_constants()
    arrays, args = {}, []
    for name in _INS + ["consts", "tables"]:
        a = consts if name == "consts" else tables if name == "tables" else _np.ascontiguousarray(inputs[name])
        arrays[f"in_{name}"] = a
        args.append(nc.dram_tensor(f"in_{name}", a.shape, _mybir.dt.from_np(a.dtype), kind="ExternalInput").ap())
    for i, shape in enumerate(_OUTS):
        args.append(nc.dram_tensor(f"out_{i}", shape, F32, kind="ExternalOutput").ap())
    hybrid_step(nc, *args)
    r = _run(nc, [arrays], core_ids=[0])
    return tuple(r.results[0][f"out_{i}"] for i in range(len(_OUTS)))
```
